# Optimizing a Trainium2 kernel written in Bass

```python
import math
import jax, jax.numpy as jnp
from jax import lax
import numpy as np

D_MODEL = 1024
BATCH = 1
SEQ = 256
DEPTH = 2
DEC_BATCH = 8
DEC_SEQ = 1
PAST_LEN = 2048
PAGE_SIZE = 128

N_META = 16
EPS = 1e-6
N_EVEN = (DEPTH + 1) // 2
N_ODD = DEPTH // 2
D_POOL = D_MODEL // 2
POOL_WINDOWS = (2, 4, 8, 16)
N_POOL_GROUPS = len(POOL_WINDOWS)
POOL_GROUP = D_POOL // N_POOL_GROUPS
POOL_BUF = max(POOL_WINDOWS) - 1
D_SSM = D_MODEL - D_POOL
SSM_GROUP = 16
N_SSM_GROUPS = D_SSM // SSM_GROUP
SSM_STATE = 64
D_FF = 2816
GLA_HEADS = 4
GLA_DK = D_MODEL // 2 // GLA_HEADS
GLA_DV = D_MODEL // GLA_HEADS
GLA_KEY = GLA_HEADS * GLA_DK
GLA_VAL = GLA_HEADS * GLA_DV
GLA_GATE_RANK = 16
GLA_GATE_NORM = 16.0
GLA_CHUNK = 64
META_PAD = (-N_META) % GLA_CHUNK
N_EXPERTS = 8
TOP_K = 2
D_EXPERT = 896

kernel_name = "hybrid_pool_s5_gla_moe_step"

def rmsnorm(x, w):
    xf = x.astype(jnp.float32)
    y = xf * lax.rsqrt(jnp.mean(xf * xf, axis=-1, keepdims=True) + EPS)
    return (y * w.astype(jnp.float32)).astype(x.dtype)

def swiglu(x, w1, w3, w2):
    return (jax.nn.silu(x @ w1) * (x @ w3)) @ w2

def pool_mix(u, start_pos, n_past, w_pool, pool_scale):
    L = u.shape[1]
    uf = u.astype(jnp.float32)
    cs = jnp.concatenate([jnp.zeros_like(uf[:, :1]), jnp.cumsum(uf, axis=1)], axis=1)
    rows = jnp.arange(n_past, L)
    pos = start_pos + rows
    outs = []
    for gi, w in enumerate(POOL_WINDOWS):
        sl = slice(gi * POOL_GROUP, (gi + 1) * POOL_GROUP)
        lo = jnp.maximum(rows + 1 - w, 0)
        cnt = jnp.minimum(pos + 1, w).astype(jnp.float32)
        mean = (cs[:, rows + 1, sl] - cs[:, lo, sl]) / cnt[None, :, None]
        d = (mean - uf[:, rows, sl]).astype(u.dtype)
        outs.append(jnp.einsum('btc,cd->btd', d, w_pool[gi]))
    return jnp.concatenate(outs, axis=-1) * pool_scale

def s5_discretize(a_re, a_im, log_dt, b_re, b_im):
    dt = jnp.exp(log_dt.astype(jnp.float32))[:, None]
    ar = a_re.astype(jnp.float32)
    ai = a_im.astype(jnp.float32)
    mag = jnp.exp(ar * dt)
    lb_re = mag * jnp.cos(ai * dt)
    lb_im = mag * jnp.sin(ai * dt)
    den = ar * ar + ai * ai
    nr = lb_re - 1.0
    f_re = (nr * ar + lb_im * ai) / den
    f_im = (lb_im * ar - nr * ai) / den
    br = b_re.astype(jnp.float32)
    bi = b_im.astype(jnp.float32)
    bb_re = f_re[..., None] * br - f_im[..., None] * bi
    bb_im = f_re[..., None] * bi + f_im[..., None] * br
    return lb_re, lb_im, bb_re, bb_im

def s5_combine(e1, e2):
    a1r, a1i, b1r, b1i = e1
    a2r, a2i, b2r, b2i = e2
    return (a2r * a1r - a2i * a1i, a2r * a1i + a2i * a1r,
            a2r * b1r - a2i * b1i + b2r, a2r * b1i + a2i * b1r + b2i)

def s5_mix(u, h0_re, h0_im, a_re, a_im, log_dt, b_re, b_im, c_re, c_im, d_skip):
    Bn, T, _ = u.shape
    uf = u.astype(jnp.float32)
    ug = uf.reshape(Bn, T, N_SSM_GROUPS, SSM_GROUP)
    lb_re, lb_im, bb_re, bb_im = s5_discretize(a_re, a_im, log_dt, b_re, b_im)
    bu_re = jnp.einsum('gnp,btgp->btgn', bb_re, ug)
    bu_im = jnp.einsum('gnp,btgp->btgn', bb_im, ug)
    el_re = jnp.broadcast_to(lb_re, bu_re.shape)
    el_im = jnp.broadcast_to(lb_im, bu_re.shape)
    ac_re, ac_im, hr, hi = lax.associative_scan(s5_combine, (el_re, el_im, bu_re, bu_im), axis=1)
    if h0_re is not None:
        r0 = h0_re.astype(jnp.float32)[:, None]
        i0 = h0_im.astype(jnp.float32)[:, None]
        hr, hi = hr + ac_re * r0 - ac_im * i0, hi + ac_re * i0 + ac_im * r0
    y = (jnp.einsum('gpn,btgn->btgp', c_re.astype(jnp.float32), hr)
         - jnp.einsum('gpn,btgn->btgp', c_im.astype(jnp.float32), hi))
    y = y.reshape(Bn, T, D_SSM) + d_skip.astype(jnp.float32) * uf
    return y.astype(u.dtype), hr[:, -1].astype(u.dtype), hi[:, -1].astype(u.dtype)

def even_layer(h, pool_past, h0_re, h0_im, start_pos, pe):
    (norm_mix, w_in, w_pool, pool_scale, a_re, a_im, log_dt, b_re, b_im, c_re, c_im,
     d_skip, w_glu, b_glu, w_out, norm_ffn, w1, w3, w2) = pe
    xn = rmsnorm(h, norm_mix)
    u = xn @ w_in
    u_a, u_b = u[..., :D_POOL], u[..., D_POOL:]
    if pool_past is None:
        u_full, n_past = u_a, 0
    else:
        u_full, n_past = jnp.concatenate([pool_past.astype(u_a.dtype), u_a], axis=1), POOL_BUF
    y_a = pool_mix(u_full, start_pos, n_past, w_pool, pool_scale)
    y_b, hr, hi = s5_mix(u_b, h0_re, h0_im, a_re, a_im, log_dt, b_re, b_im, c_re, c_im, d_skip)
    z = jax.nn.gelu(y_b)
    y_b = z * jax.nn.sigmoid(z @ w_glu + b_glu)
    h = h + jnp.concatenate([y_a, y_b], axis=-1) @ w_out
    h = h + swiglu(rmsnorm(h, norm_ffn), w1, w3, w2)
    return h, u_full[:, -POOL_BUF:], hr, hi

def gla_chunked(q, k, v, gk):
    Bn, H, L, _ = q.shape
    padw = ((0, 0), (0, 0), (META_PAD, 0), (0, 0))
    q, k, v, gk = (jnp.pad(t, padw) for t in (q, k, v, gk))
    nc = (L + META_PAD) // GLA_CHUNK
    def chunks(t):
        return jnp.moveaxis(t.reshape(Bn, H, nc, GLA_CHUNK, t.shape[-1]), 2, 0)
    causal = jnp.tril(jnp.ones((GLA_CHUNK, GLA_CHUNK), dtype=bool))[:, :, None]
    def step(S, inp):
        qc, kc, vc, gc = inp
        bc = jnp.cumsum(gc, axis=2)
        diff = bc[:, :, :, None, :] - bc[:, :, None, :, :]
        decay = jnp.where(causal, jnp.exp(jnp.where(causal, diff, 0.0)), 0.0)
        att = jnp.einsum('bhtk,bhsk,bhtsk->bhts', qc, kc, decay)
        o = (jnp.einsum('bhtk,bhkv->bhtv', qc * jnp.exp(bc), S)
             + jnp.einsum('bhts,bhsv->bhtv', att, vc))
        blast = bc[:, :, -1:, :]
        S = (jnp.exp(blast[:, :, 0, :, None]) * S
             + jnp.einsum('bhsk,bhsv->bhkv', kc * jnp.exp(blast - bc), vc))
        return S, o
    S0 = jnp.zeros((Bn, H, GLA_DK, GLA_DV), jnp.float32)
    S, o = lax.scan(step, S0, (chunks(q), chunks(k), chunks(v), chunks(gk)))
    o = jnp.moveaxis(o, 0, 2).reshape(Bn, H, nc * GLA_CHUNK, GLA_DV)[:, :, META_PAD:]
    return o, S

def gla_recurrent(q, k, v, gk, S0):
    def step(S, inp):
        qt, kt, vt, gt = inp
        S = jnp.exp(gt)[..., None] * S + kt[..., :, None] * vt[..., None, :]
        return S, jnp.einsum('bhk,bhkv->bhv', qt, S)
    S, o = lax.scan(step, S0, tuple(jnp.moveaxis(t, 2, 0) for t in (q, k, v, gk)))
    return jnp.moveaxis(o, 0, 2), S

def moe_ffn(x, w_router, w1, w3, w2):
    probs = jax.nn.softmax((x @ w_router).astype(jnp.float32), axis=-1)
    top_p, top_i = lax.top_k(probs, TOP_K)
    top_p = top_p / jnp.sum(top_p, axis=-1, keepdims=True)
    gates = jnp.sum(jax.nn.one_hot(top_i, N_EXPERTS, dtype=jnp.float32) * top_p[..., None], axis=-2)
    y = jnp.zeros(x.shape, jnp.float32)
    for e in range(N_EXPERTS):
        y = y + gates[..., e:e + 1] * swiglu(x, w1[e], w3[e], w2[e]).astype(jnp.float32)
    return y.astype(x.dtype)

def odd_layer(h, S0, po):
    (norm_mix, w_in, w_gk1, w_gk2, b_gk, gla_norm, w_out, norm_ffn, w_router, w1, w3, w2) = po
    Bn, T, _ = h.shape
    xn = rmsnorm(h, norm_mix)
    proj = xn @ w_in
    q, k, v, g = jnp.split(proj, [GLA_KEY, 2 * GLA_KEY, 2 * GLA_KEY + GLA_VAL], axis=-1)
    gk = jax.nn.log_sigmoid(((xn @ w_gk1) @ w_gk2 + b_gk).astype(jnp.float32)) / GLA_GATE_NORM
    def heads(t, dh):
        return t.astype(jnp.float32).reshape(Bn, T, GLA_HEADS, dh).transpose(0, 2, 1, 3)
    q = heads(q, GLA_DK) * (GLA_DK ** -0.5)
    k, v, gk = heads(k, GLA_DK), heads(v, GLA_DV), heads(gk, GLA_DK)
    if S0 is None:
        o, S = gla_chunked(q, k, v, gk)
    else:
        o, S = gla_recurrent(q, k, v, gk, S0.astype(jnp.float32))
    o = o.transpose(0, 2, 1, 3)
    o = rmsnorm(o, gla_norm) * jax.nn.silu(g.astype(jnp.float32).reshape(Bn, T, GLA_HEADS, GLA_DV))
    h = h + o.reshape(Bn, T, GLA_VAL).astype(h.dtype) @ w_out
    h = h + moe_ffn(rmsnorm(h, norm_ffn), w_router, w1, w3, w2)
    return h, S.astype(h.dtype)

def setup_inputs(seed: int = 0) -> dict:
    key = jax.random.key(seed)
    ks = iter(jax.random.split(key, 64))
    f32 = jnp.float32
    def nrm(shape, scale):
        return jax.random.normal(next(ks), shape, f32) * scale
    def gain(shape):
        return 1.0 + 0.02 * jax.random.normal(next(ks), shape, f32)
    G, N, P = N_SSM_GROUPS, SSM_STATE, SSM_GROUP
    d = {}
    d["x_prompt"] = nrm((BATCH, SEQ, D_MODEL), 1.0)
    d["x_sample"] = nrm((DEC_BATCH, DEC_SEQ, D_MODEL), 1.0)
    d["state_pool"] = nrm((N_EVEN, DEC_BATCH, POOL_BUF, D_POOL), 1.0)
    d["state_s5_re"] = nrm((N_EVEN, DEC_BATCH, G, N), 0.5)
    d["state_s5_im"] = nrm((N_EVEN, DEC_BATCH, G, N), 0.5)
    d["state_gla"] = nrm((N_ODD, DEC_BATCH, GLA_HEADS, GLA_DK, GLA_DV), 1.0)
    d["meta_tokens"] = nrm((N_META, D_MODEL), 1.0)
    d["norm_mix_e"] = gain((N_EVEN, D_MODEL))
    d["w_in_e"] = nrm((N_EVEN, D_MODEL, D_POOL + D_SSM), D_MODEL ** -0.5)
    d["w_pool"] = nrm((N_EVEN, N_POOL_GROUPS, POOL_GROUP, POOL_GROUP), POOL_GROUP ** -0.5)
    d["pool_scale"] = gain((N_EVEN, D_POOL))
    d["s5_a_re"] = -0.5 + 0.01 * jax.random.normal(next(ks), (N_EVEN, G, N), f32)
    d["s5_a_im"] = (math.pi * jnp.broadcast_to(jnp.arange(N, dtype=f32), (N_EVEN, G, N))
                    + 0.01 * jax.random.normal(next(ks), (N_EVEN, G, N), f32))
    d["s5_log_dt"] = jax.random.uniform(next(ks), (N_EVEN, G), f32, math.log(1e-3), math.log(1e-1))
    d["s5_b_re"] = nrm((N_EVEN, G, N, P), (2 * P) ** -0.5)
    d["s5_b_im"] = nrm((N_EVEN, G, N, P), (2 * P) ** -0.5)
    d["s5_c_re"] = nrm((N_EVEN, G, P, N), N ** -0.5)
    d["s5_c_im"] = nrm((N_EVEN, G, P, N), N ** -0.5)
    d["s5_d"] = nrm((N_EVEN, D_SSM), 1.0)
    d["w_glu"] = nrm((N_EVEN, D_SSM, D_SSM), D_SSM ** -0.5)
    d["b_glu"] = nrm((N_EVEN, D_SSM), 0.02)
    d["w_out_e"] = nrm((N_EVEN, D_MODEL, D_MODEL), D_MODEL ** -0.5)
    d["norm_ffn_e"] = gain((N_EVEN, D_MODEL))
    d["ffn_w1"] = nrm((N_EVEN, D_MODEL, D_FF), D_MODEL ** -0.5)
    d["ffn_w3"] = nrm((N_EVEN, D_MODEL, D_FF), D_MODEL ** -0.5)
    d["ffn_w2"] = nrm((N_EVEN, D_FF, D_MODEL), D_FF ** -0.5)
    d["norm_mix_o"] = gain((N_ODD, D_MODEL))
    d["w_in_o"] = nrm((N_ODD, D_MODEL, 2 * GLA_KEY + 2 * GLA_VAL), D_MODEL ** -0.5)
    d["w_gk1"] = nrm((N_ODD, D_MODEL, GLA_GATE_RANK), D_MODEL ** -0.5)
    d["w_gk2"] = nrm((N_ODD, GLA_GATE_RANK, GLA_KEY), GLA_GATE_RANK ** -0.5)
    d["b_gk"] = nrm((N_ODD, GLA_KEY), 0.02)
    d["gla_norm"] = gain((N_ODD, GLA_DV))
    d["w_out_o"] = nrm((N_ODD, GLA_VAL, D_MODEL), GLA_VAL ** -0.5)
    d["norm_ffn_o"] = gain((N_ODD, D_MODEL))
    d["w_router"] = nrm((N_ODD, D_MODEL, N_EXPERTS), D_MODEL ** -0.5)
    d["moe_w1"] = nrm((N_ODD, N_EXPERTS, D_MODEL, D_EXPERT), D_MODEL ** -0.5)
    d["moe_w3"] = nrm((N_ODD, N_EXPERTS, D_MODEL, D_EXPERT), D_MODEL ** -0.5)
    d["moe_w2"] = nrm((N_ODD, N_EXPERTS, D_EXPERT, D_MODEL), D_EXPERT ** -0.5)
    d["norm_final"] = gain((D_MODEL,))
    return d

def reference(x_prompt, x_sample, state_pool, state_s5_re, state_s5_im, state_gla, meta_tokens,
              norm_mix_e, w_in_e, w_pool, pool_scale, s5_a_re, s5_a_im, s5_log_dt, s5_b_re, s5_b_im,
              s5_c_re, s5_c_im, s5_d, w_glu, b_glu, w_out_e, norm_ffn_e, ffn_w1, ffn_w3, ffn_w2,
              norm_mix_o, w_in_o, w_gk1, w_gk2, b_gk, gla_norm, w_out_o, norm_ffn_o, w_router,
              moe_w1, moe_w3, moe_w2, norm_final):
    meta = jnp.broadcast_to(meta_tokens.astype(x_prompt.dtype)[None], (x_prompt.shape[0], N_META, D_MODEL))
    h_p = jnp.concatenate([meta, x_prompt], axis=1)
    h_s = x_sample
    pool_p, pool_s, re_p, re_s, im_p, im_s, gla_p, gla_s = [], [], [], [], [], [], [], []
    for layer in range(DEPTH):
        j = layer // 2
        if layer % 2 == 0:
            pe = (norm_mix_e[j], w_in_e[j], w_pool[j], pool_scale[j], s5_a_re[j], s5_a_im[j],
                  s5_log_dt[j], s5_b_re[j], s5_b_im[j], s5_c_re[j], s5_c_im[j], s5_d[j],
                  w_glu[j], b_glu[j], w_out_e[j], norm_ffn_e[j], ffn_w1[j], ffn_w3[j], ffn_w2[j])
            h_p, bp, rp, ip = even_layer(h_p, None, None, None, 0, pe)
            h_s, bs, rs, is_ = even_layer(h_s, state_pool[j], state_s5_re[j], state_s5_im[j],
                                          PAST_LEN - POOL_BUF, pe)
            pool_p.append(bp); pool_s.append(bs)
            re_p.append(rp); re_s.append(rs)
            im_p.append(ip); im_s.append(is_)
        else:
            po = (norm_mix_o[j], w_in_o[j], w_gk1[j], w_gk2[j], b_gk[j], gla_norm[j], w_out_o[j],
                  norm_ffn_o[j], w_router[j], moe_w1[j], moe_w3[j], moe_w2[j])
            h_p, sp = odd_layer(h_p, None, po)
            h_s, ss = odd_layer(h_s, state_gla[j], po)
            gla_p.append(sp); gla_s.append(ss)
    y_prompt = rmsnorm(h_p, norm_final)[:, N_META:]
    y_sample = rmsnorm(h_s, norm_final)
    return (y_prompt, y_sample, jnp.stack(pool_p), jnp.stack(pool_s), jnp.stack(re_p), jnp.stack(re_s),
            jnp.stack(im_p), jnp.stack(im_s), jnp.stack(gla_p), jnp.stack(gla_s))


_drawn_inputs = setup_inputs


def setup_inputs(seed=0):
    import zlib

    import numpy as np

    out = dict(_drawn_inputs(seed))
    spreads = {}
    factors = {'s5_a_re': 18.867,
     'b_glu': 16.935,
     'norm_ffn_e': 3.036,
     'b_gk': 6.039,
     'gla_norm': 22.08,
     'norm_final': 8.115,
     'pool_scale': 2.697,
     'norm_ffn_o': 4.838}
    for name, (base, spread) in spreads.items():
        noise = np.random.default_rng([zlib.crc32(name.encode()), seed]).standard_normal(out[name].shape)
        drawn = base * np.exp(spread * noise) if base else spread * noise
        out[name] = __import__('jax').numpy.asarray(drawn.astype(out[name].dtype))
    for name, factor in factors.items():
        out[name] = (out[name] * factor).astype(out[name].dtype)
    return out
```

```python
import math

import concourse.bass as bass
from concourse import mybir
from contextlib import ExitStack

F32 = mybir.dt.float32
U32 = mybir.dt.uint32
ALU = mybir.AluOpType
ACT = mybir.ActivationFunctionType
AX = mybir.AxisListType

P = 128
D = 1024
DC = D // P
NPROMPT = 272
NSAMP = 8
T = NPROMPT + NSAMP
EPS = 1e-6
NG = 4
PAST = 15
ST = 16
FF = 2816
FC = FF // P
H = 4
DV = 256
VC = DV // P
CH = 68
NCH = NPROMPT // CH
SUB = 17
NSUB = CH // SUB
MID = SUB // 2
NE = 8
EC = 896 // P
RT = 70
NRT = T // RT

UT = 16
UNIT = UT * P
SLOTS = 11
W_IN_E, W_GLU, W_OUT_E = 0, 4, 5
FFN_UP = W_OUT_E + 4
FFN_DOWN = FFN_UP + FC
W_IN_O = FFN_DOWN + FC * DC // UT
W_OUT_O = W_IN_O + 12
MOE = W_OUT_O + 4
DOWN_UNIT = 2 * EC * P
PER_EXPERT = EC + DC // 2

DENSE_POOL, DENSE_GLU, DENSE_OUT, DENSE_DOWN, DENSE_IN_O, DENSE_OUT_O, DENSE_MOE = 8, 12, 16, 24, 32, 56, 64
GATED0 = 4

V_NORM = [0, 8, 16, 24, 32]
V_PSCALE, V_D, V_BGLU, V_BGK, V_GNORM = 40, 44, 48, 52, 56
NVEC = 58
C_ID, C_ONE, C_MASK, C_IOTA, C_CNT, C_RESET, C_SEL = 0, 128, 256, 324, 332, 396, 668
C_EPS = C_SEL
NCST = C_EPS + 1


TWO_PI = 2 * math.pi
PI_1 = 6.28125
PI_2 = 0.0019350051879882812
PI_3 = TWO_PI - PI_1 - PI_2
ROUND = 12582912.0


def build(nc, xT_d, vecs_d, cst_d, sel_d, s5p_d, h0_d, bblk_d, cblk_d, past_d, wpool_d, main_d,
          up_d, down_d, gk1_d, gk2_d, router_d, sgla_d,
          yT_d, poolp_d, pools_d, s5p_out, s5s_out, glap_d, glas_d):
    ctx = ExitStack()
    with ctx:
        def sb(name, shape, dt=F32):
            return ctx.enter_context(nc.sbuf_tensor(name, shape, dt))

        def sem(name):
            return ctx.enter_context(nc.semaphore(name))

        ring = sb("ring", [P, SLOTS, UNIT])
        xT = sb("xT", [P, DC, T])
        xn = sb("xn", [P, DC, T])
        sq = sb("sq", [P, DC, T])
        rstd = sb("rstd", [P, T])
        vecs = sb("vecs", [P, NVEC])
        cst = sb("cst", [P, NCST])
        ident = cst[:, C_ID:C_ID + P]
        ones = cst[:, C_ONE:C_ONE + P]
        W = 22400
        work = sb("work", [P, W])
        at = [0]

        def region(*shape, rows=P):
            n = int(math.prod(shape))
            v = work[0:rows, at[0]:at[0] + n]
            at[0] += n
            assert at[0] <= W, at[0]
            if len(shape) == 2:
                v = v.rearrange("p (a b) -> p a b", a=shape[0])
            if len(shape) == 3:
                v = v.rearrange("p (a b c) -> p a b c", a=shape[0], b=shape[1])
            return v

        cosT = region(ST, NPROMPT)
        sinT = region(ST, NPROMPT)
        dyn = at[0]
        tabA = region(ST, P)
        tabB = region(ST, P)
        at[0] = dyn
        rotA = region(2, NPROMPT)
        rotB = region(2, NPROMPT)
        scanned = region(2, 2, NPROMPT)
        backC = region(2, 2, NPROMPT)
        backS = region(2, 2, NPROMPT)
        sig = backC.rearrange("p a b c -> p (a b c)")[:, 0:2 * T].rearrange("p (a b) -> p a b", a=2)
        cblk = region(2, ST, 32)
        cf = region(3, ST, 32)
        bblk = region(4, 2, P)
        ycat = region(DC, T)
        upad = region(NG, 16 + NPROMPT)
        z = upad.rearrange("p a b -> p (a b)")[:, 0:4 * T].rearrange("p (a b) -> p a b", a=4)
        pbuf = region(NG, NSAMP * 16).rearrange("p g (b t) -> p g b t", b=NSAMP)
        h0 = region(2, ST, NSAMP)
        buS = region(2, ST, NSAMP)
        hS = region(2, ST, NSAMP)
        par = region(20, ST)
        s5p = region(3, ST)
        wpool = region(NG, P)
        glast = region(2, ST)
        nhi = region(ST, NSAMP)
        at[0] = 0
        hF = region(FC, T)
        silF = region(3, T)
        at[0] = 0
        qT = region(H, T)
        kT = region(H, T)
        vT = region(DC, T)
        gS = region(DC, T)
        gx = region(H, T)
        bT = region(H, NPROMPT)
        mark = at[0]
        qd = region(H, NPROMPT)
        kd = [region(H, NCH * SUB * (i + 1)) for i in range(NSUB)]
        samp1 = work[:, mark:mark + 2 * H * DV].rearrange("p (a b c) -> p a b c", a=2, b=H)
        gl = work[:, mark:mark + H * T].rearrange("p (a b) -> p a b", a=H)
        qe = region(H, NPROMPT)
        ke = region(H, NPROMPT)
        elast = region(H, NCH)
        attS = region(2, H, CH, rows=CH)
        ketok = region(H * P, rows=CH)
        S = region(H, DV)
        samp0 = region(2, H, DV)
        samp = [samp0, samp1]
        vblk_at = at[0]
        vblk = region(2, 2 * DV, rows=NSAMP)
        ktokS = region(H * P, rows=NSAMP)
        vtokS = region(H * DV, rows=NSAMP)
        egS = region(H, NSAMP)
        gk1 = region(DC, 16)
        gk2 = work[0:16, vblk_at:vblk_at + H * P]
        low = work[0:16, mark:mark + T]
        rms = gx
        assert at[0] <= W - 560 - DC * NE, at[0]
        at[0] = W - 560 - DC * NE
        assert at[0] >= 0
        router = region(DC, NE)
        oT = xn
        vtok = [sq[0:CH, 0:4, :].rearrange("p a b -> p (a b)")[:, 0:H * DV],
                sq[0:CH, 4:8, :].rearrange("p a b -> p (a b)")[:, 0:H * DV]]
        oG = vT
        at[0] = 0
        gbc = region(NE, T)
        hM = region(EC, T)
        silM = region(3, T)
        gpre = region(3, T)
        sel = region(NE, P, rows=NE)
        gT = region(T, rows=NE)
        at[0] = W - 560
        rt = region(16, NRT * NE, rows=RT)
        rsc = region(8, NRT, rows=RT)
        idx = sb("idx", [RT, NRT * 8], U32)

        banks = [ctx.enter_context(nc.psum_tensor(f"bank{i}", [P, 512], F32)) for i in range(2)]
        pairs = [ctx.enter_context(nc.psum_tensor(f"pair{i}", [P, 2, 512], F32)) for i in range(3)]

        slot_full = [sem(f"slot_full{s}") for s in range(SLOTS)]
        units_used = sem("units_used")
        x_loaded, s5_loaded, late_loaded = sem("x_loaded"), sem("s5_loaded"), sem("late_loaded")
        cst_loaded = sem("cst_loaded")
        l1_loaded = sem("l1_loaded")
        sel_loaded = sem("sel_loaded")
        x_ready = sem("x_ready")
        sq_ready, ss_ready, std_ready, xn_ready = (sem(n) for n in ("sq_ready", "ss_ready", "std_ready", "xn_ready"))
        dve_link, act_link, pool_link = sem("dve_link"), sem("act_link"), sem("pool_link")
        dense_done = sem("dense_done")
        u_copied = sem("u_copied")
        s5_dt, s5_arg, s5_trig, s5_tab = sem("s5_dt"), sem("s5_arg"), sem("s5_trig"), sem("s5_tab")
        bu_done, bu_rot = sem("bu_done"), sem("bu_rot")
        scan_done, back_done, y_done, y_out = sem("scan_done"), sem("back_done"), sem("y_done"), sem("y_out")
        hs_ready, ys_done = sem("hs_ready"), sem("ys_done")
        d_ready, pool_out = sem("d_ready"), sem("pool_out")
        z_ready, sig_ready, gated = sem("z_ready"), sem("sig_ready"), sem("gated")
        up_done, sil_done = sem("up_done"), sem("sil_done")
        states_out, pool_states = sem("states_out"), sem("pool_states")
        s5_folded, gpre_done, yp_out = sem("s5_folded"), sem("gpre_done"), sem("yp_out")
        s5_states = sem("s5_states")
        low_done, low_copied, gk_done, gx_ready, gl_ready, b_ready = (
            sem(n) for n in ("low_done", "low_copied", "gk_done", "gx_ready", "gl_ready", "b_ready"))
        q_copied = sem("q_copied")
        dec_arg, dec_exp, dec_ready = sem("dec_arg"), sem("dec_exp"), sem("dec_ready")
        zero_att = sem("zero_att")
        vtr_done, vtr_copied, ktr_done, ktr_copied = (sem(n) for n in ("vtr_done", "vtr_copied", "ktr_done", "ktr_copied"))
        att_done, att_copied, o_done, o_copied, kv_done, S_ready = (
            sem(n) for n in ("att_done", "att_copied", "o_done", "o_copied", "kv_done", "S_ready"))
        str_done, str_copied, samp_loaded0, samp_loaded1 = (
            sem(n) for n in ("str_done", "str_copied", "samp_loaded0", "samp_loaded1"))
        samp_loaded = [samp_loaded0, samp_loaded1]
        samp_saved = [sem("samp_saved0"), sem("samp_saved1")]
        vblk_ready, outer_done, samp_ready, so_done, so_copied = (
            sem(n) for n in ("vblk_ready", "outer_done", "samp_ready", "so_done", "so_copied"))
        osq_ready, oss_done, ostd_ready, og_ready = (sem(n) for n in ("osq_ready", "oss_done", "ostd_ready", "og_ready"))
        logit_done, shifted, exped, gate_ready, gtr_done, gT_ready, gbc_done, gbc_copied = (
            sem(n) for n in ("logit_done", "shifted", "exped", "gate_ready", "gtr_done", "gT_ready", "gbc_done", "gbc_copied"))
        down_done = sem("down_done")
        y_saved = sem("y_saved")

        def unit_end(n):
            if n < W_GLU:
                return dense_done, 2 * (n + 1)
            if n == W_GLU:
                return dense_done, DENSE_GLU + 4
            if n < FFN_UP:
                return dense_done, DENSE_OUT + 2 * (n - W_OUT_E + 1)
            if n < FFN_DOWN:
                return up_done, n - FFN_UP + 1
            if n < W_IN_O:
                return dense_done, DENSE_DOWN + -(-UT * (n - FFN_DOWN + 1) // FC)
            if n < W_OUT_O:
                return dense_done, DENSE_IN_O + 2 * (n - W_IN_O + 1)
            return dense_done, DENSE_OUT_O + 2 * (n - W_OUT_O + 1)

        def back(i, length):
            return 3 if i >= 3 else i + length - max(x for x in range(length) if x % 3 == i)

        def bc(ap, shape):
            return ap.broadcast_to(shape)

        def tokens(ap, h=None):
            return ap[:, :, 0:NPROMPT]

        block = ctx.enter_context(nc.Block())

        @block.sync
        def _(sp):
            for n in range(MOE):
                if n >= SLOTS:
                    sp.wait_ge(*unit_end(n - SLOTS))
                sp.dma_start(ring[:, n % SLOTS, :], main_d[n, :, :]).then_inc(slot_full[n % SLOTS], 16)

            def load_expert_unit(e, i):
                s = (MOE + i) % SLOTS
                if i < EC:
                    src = up_d[bass.ds(e * EC + i, 1), :, :]
                    sp.dma_start(ring[:, s, :], src.rearrange("o p n -> p (o n)")).then_inc(slot_full[s], 16)
                else:
                    src = down_d[bass.ds(e * (DC // 2) + (i - EC), 1), :, :]
                    sp.dma_start(ring[:, s, 0:DOWN_UNIT], src.rearrange("o p n -> p (o n)")
                                 ).then_inc(slot_full[s], 16)

            for i in range(PER_EXPERT):
                sp.wait_ge(*unit_end(MOE + i - SLOTS))
                load_expert_unit(0, i)
            with sp.Fori(1, NE) as e:
                for i in range(PER_EXPERT):
                    if i < EC:
                        sp.wait_ge(up_done, EC * e + (FC - EC + i + 1))
                    else:
                        sp.wait_ge(dense_done, DC * e + (DENSE_MOE - DC + 2 * (i - EC + 1)))
                    load_expert_unit(e, i)

        @block.gpsimd
        def _(pool):
            for j in range(ST):
                pool.wait_ge(scan_done, j + 1)
                if j >= 2:
                    pool.wait_ge(y_done, j - 1)
                g = scanned[:, j % 2]
                nc.gpsimd.tensor_tensor(backC[:, j % 2], g, bc(cosT[:, j:j + 1, :], [P, 2, NPROMPT]), ALU.mult)
                nc.gpsimd.tensor_tensor(backS[:, j % 2], g, bc(sinT[:, j:j + 1, :], [P, 2, NPROMPT]),
                                        ALU.mult).then_inc(back_done, 1)
            pool.wait_ge(s5_states, 1)
            pool.dma_start(s5p_out, glast).then_inc(states_out, 16)
            pool.wait_ge(hs_ready, 1)
            pool.dma_start(s5s_out, hS).then_inc(states_out, 16)
            pool.wait_ge(str_copied, 3)
            for n in range(NSAMP // 2 * H):
                b, h = 2 * (n // H), n % H
                if n >= 2:
                    pool.wait_ge(outer_done, n - 1)
                nc.gpsimd.tensor_tensor(vblk[:, n % 2].rearrange("p (b v) -> p b v", b=2),
                                        bc(vtokS[:, h * DV:(h + 1) * DV].unsqueeze(1), [NSAMP, 2, DV]),
                                        bc(cst[0:NSAMP, C_ID + b:C_ID + b + 2].unsqueeze(2), [NSAMP, 2, DV]),
                                        ALU.mult).then_inc(vblk_ready, 1)
            pool.wait_ge(S_ready, H * NCH)
            pool.dma_start(glap_d, S).then_inc(states_out, 16)
            pool.wait_ge(states_out, 3 * 16)

        @block.scalar
        def _(act):
            links = [0]

            def link(ins):
                links[0] += 1
                ins.then_inc(act_link, 1)
                act.wait_ge(act_link, links[0])

            act.dma_start(xT[:, :, :], xT_d).then_inc(x_loaded, 16)
            act.dma_start(cst[:, :], cst_d).then_inc(cst_loaded, 16)
            act.dma_start(vecs[:, :], vecs_d).then_inc(cst_loaded, 16)
            act.dma_start(s5p, s5p_d).then_inc(s5_loaded, 16)
            act.dma_start(cblk, cblk_d).then_inc(late_loaded, 16)
            act.dma_start(bblk, bblk_d).then_inc(late_loaded, 16)
            act.dma_start(h0, h0_d).then_inc(late_loaded, 16)
            act.dma_start(pbuf[:, :, :, 0:PAST], past_d).then_inc(late_loaded, 16)
            act.dma_start(wpool, wpool_d).then_inc(late_loaded, 16)

            def squares(i, k):
                if i:
                    act.wait_ge(x_ready, 8 * (i - 1) + k + 1)
                nc.scalar.activation(sq[:, k, :], xT[:, k, :], ACT.Square).then_inc(sq_ready, 1)

            def std(i):
                act.wait_ge(ss_ready, i + 1)
                nc.scalar.activation(rstd[:, :], pairs[2][:, 1, 0:T], ACT.Sqrt, scale=1.0 / D,
                                     bias=cst[:, C_EPS:C_EPS + 1]).then_inc(std_ready, 1)

            act.wait_ge(s5_loaded, 16)
            nc.scalar.activation(par[:, 0], s5p[:, 2], ACT.Exp).then_inc(s5_dt, 1)
            act.wait_ge(x_loaded, 16)
            for k in range(DC):
                squares(0, k)
            act.wait_ge(s5_arg, 1)
            nc.scalar.activation(par[:, 3], par[:, 1], ACT.Exp)
            nc.scalar.activation(par[:, 4], par[:, 2], ACT.Sin)
            nc.scalar.activation(par[:, 5], par[:, 6], ACT.Sin).then_inc(s5_trig, 1)
            act.wait_ge(cst_loaded, 2 * 16)
            std(0)

            def copy_u(o):
                act.wait_ge(dense_done, o + 1)
                if o < 4:
                    nc.scalar.copy(ycat[:, 4 + o, :], banks[o % 2][:, 0:T]).then_inc(u_copied, 1)
                else:
                    g = o - 4
                    act.wait_ge(late_loaded, 5 * 16)
                    nc.scalar.copy(upad[:, g, 16:], banks[o % 2][:, 0:NPROMPT])
                    nc.scalar.copy(pbuf[:, g, :, PAST], banks[o % 2][:, NPROMPT:T]).then_inc(u_copied, 1)

            copy_u(0)
            copy_u(1)
            for j in range(ST):
                if j < 6:
                    copy_u(2 + j)
                if j == 6:
                    act.wait_ge(u_copied, 8)
                    act.dma_start(poolp_d, upad[:, :, 16 + NPROMPT - PAST:]).then_inc(pool_states, 16)
                    act.dma_start(pools_d, pbuf[:, :, :, 1:]).then_inc(pool_states, 16)
                if 8 <= j < 12:
                    g = j - 8
                    act.wait_ge(dense_done, 9 + g)
                    nc.scalar.activation(ycat[:, g, :], banks[g % 2][:, 0:T], ACT.Copy,
                                         scale=vecs[:, V_PSCALE + g:V_PSCALE + g + 1]).then_inc(pool_out, 1)
            for c in range(4):
                act.wait_ge(y_out, c + 1)
                nc.scalar.activation(z[:, c, :], z[:, c, :], ACT.Gelu_apprx_tanh).then_inc(z_ready, 1)
            for m in range(4):
                act.wait_ge(dense_done, 13 + m)
                if m >= 2:
                    act.wait_ge(gated, m - 1)
                nc.scalar.activation(sig[:, m % 2, :], banks[m % 2][:, 0:T], ACT.Sigmoid,
                                     bias=vecs[:, V_BGLU + m:V_BGLU + m + 1]).then_inc(sig_ready, 1)
            for k in range(DC):
                squares(1, k)
            std(1)
            act.wait_ge(states_out, 2 * 16)
            act.dma_start(gk1, gk1_d).then_inc(l1_loaded, 16)
            act.dma_start(gk2, gk2_d).then_inc(l1_loaded, 16)
            act.dma_start(router, router_d).then_inc(l1_loaded, 16)
            with act.Fori(0, 2) as r:
                for i in range(SLOTS):
                    act.wait_ge(up_done, SLOTS * r + (i + 1))
                    act.wait_ge(gated, SLOTS * r + (GATED0 + i - back(i, SLOTS) + 1))
                    nc.scalar.activation(silF[:, i % 3, :], pairs[i % 3][:, 0, 0:T], ACT.Silu).then_inc(sil_done, 1)
            for k in range(DC):
                squares(2, k)
            std(2)

            act.wait_ge(low_done, 1)
            nc.scalar.copy(low, pairs[2][0:16, 0, 0:T]).then_inc(low_copied, 1)
            for h in range(H):
                act.wait_ge(gk_done, h + 1)
                nc.scalar.activation(gx[:, h, :], pairs[h % 2][:, 0, 0:T], ACT.Identity,
                                     bias=vecs[:, V_BGK + h:V_BGK + h + 1]).then_inc(gx_ready, 1)
            act.wait_ge(gx_ready, H)
            link(nc.scalar.activation(gl, gx, ACT.Abs))
            link(nc.scalar.activation(gl, gl, ACT.Exp, scale=-1.0))
            nc.scalar.activation(gl, gl, ACT.Ln, bias=1.0).then_inc(gl_ready, 1)
            DB = DENSE_IN_O
            for o in range(16):
                act.wait_ge(dense_done, DB + o + 1)
                b = banks[(DB + o) % 2][:, 0:T]
                if o < 4:
                    nc.scalar.mul(qT[:, o, :], b, float(P) ** -0.5).then_inc(q_copied, 1)
                elif o < 8:
                    nc.scalar.copy(kT[:, o - 4, :], b).then_inc(q_copied, 1)
                else:
                    nc.scalar.copy(vT[:, o - 8, :], b).then_inc(q_copied, 1)
            for n, t in enumerate([qd] + kd):
                act.wait_ge(dec_arg, n + 1)
                nc.scalar.activation(t, t, ACT.Exp).then_inc(dec_exp, 1)
            nc.scalar.activation(qe, bT, ACT.Exp).then_inc(dec_exp, 1)
            act.wait_ge(dec_arg, 6)
            nc.scalar.activation(ke, ke, ACT.Exp).then_inc(dec_exp, 1)
            act.wait_ge(dec_arg, 7)
            nc.scalar.activation(elast, elast, ACT.Exp).then_inc(dec_exp, 1)
            nc.scalar.activation(egS, gx[:, :, NPROMPT:T], ACT.Exp).then_inc(dec_exp, 1)
            for o in range(16, 24):
                act.wait_ge(dense_done, DB + o + 1)
                nc.scalar.activation(gS[:, o - 16, :], banks[(DB + o) % 2][:, 0:T], ACT.Silu).then_inc(q_copied, 1)
            act.dma_start(samp[0], sgla_d[:, 0:2]).then_inc(samp_loaded[0], 16)
            for c in range(NCH):
                act.wait_ge(vtr_done, c + 1)
                if c >= 2:
                    act.wait_ge(kv_done, 2 * (c - 1))
                for u in range(2):
                    last = nc.scalar.copy(vtok[c % 2][:, u * 512:(u + 1) * 512], pairs[0][0:CH, u, :])
                last.then_inc(vtr_copied, 1)
                act.wait_ge(o_done, c + 1)
                for u in range(2):
                    last = nc.scalar.copy(oT[:, 4 * u:4 * u + 4, c * CH:(c + 1) * CH],
                                          pairs[1][:, u, 0:4 * CH].rearrange("p (a b) -> p a b", a=4))
                last.then_inc(o_copied, 1)
            act.wait_ge(str_done, 3)
            nc.scalar.copy(ktokS, pairs[0][0:NSAMP, 0, :]).then_inc(str_copied, 1)
            nc.scalar.copy(vtokS[:, 0:512], pairs[0][0:NSAMP, 1, :]).then_inc(str_copied, 1)
            nc.scalar.copy(vtokS[:, 512:1024], pairs[1][0:NSAMP, 0, :]).then_inc(str_copied, 1)
            def load_pair(p):
                act.dma_start(samp[p % 2], sgla_d[:, 2 * p:2 * p + 2]).then_inc(samp_loaded[p % 2], 16)

            act.wait_ge(att_done, NSUB * NCH)
            load_pair(1)
            for p in range(NSAMP // 2):
                act.wait_ge(samp_ready, H * (p + 1))
                act.dma_start(glas_d[:, 2 * p:2 * p + 2], samp[p % 2]).then_inc(samp_saved[p % 2], 16)
                if p + 2 < NSAMP // 2:
                    act.wait_ge(so_done, p + 1)
                    act.wait_ge(samp_saved[p % 2], 16)
                    load_pair(p + 2)
            act.wait_ge(so_done, NSAMP // 2)
            nc.scalar.copy(oT[:, :, NPROMPT:T],
                           pairs[1][:, 1, 0:DC * NSAMP].rearrange("p (b a) -> p a b", a=DC)).then_inc(so_copied, 1)
            act.wait_ge(so_copied, 1)
            act.wait_ge(o_copied, NCH)
            for k in range(DC):
                nc.scalar.activation(sq[:, k, :], oT[:, k, :], ACT.Square).then_inc(osq_ready, 1)
            for h in range(H):
                act.wait_ge(oss_done, h + 1)
                nc.scalar.activation(rms[:, h, :], pairs[h % 2][:, 0, 0:T], ACT.Sqrt, scale=1.0 / DV,
                                     bias=cst[:, C_EPS:C_EPS + 1]).then_inc(ostd_ready, 1)
            for k in range(DC):
                squares(3, k)
            std(3)
            act.dma_start(sel, sel_d).then_inc(sel_loaded, 16)
            act.wait_ge(shifted, 1)
            nc.scalar.activation(rt[:, 0], rt[:, 0], ACT.Exp).then_inc(exped, 1)
            act.wait_ge(gtr_done, 1)
            nc.scalar.copy(gT, pairs[0][0:NE, 1, 0:T]).then_inc(gT_ready, 1)
            for e in range(NE):
                act.wait_ge(gbc_done, e + 1)
                nc.scalar.copy(gbc[:, e, :], pairs[1 + e % 2][:, 0, 0:T]).then_inc(gbc_copied, 1)
            with act.Fori(0, NE) as e:
                for i in range(EC):
                    act.wait_ge(up_done, EC * e + (FC + i + 1))
                    act.wait_ge(gated, EC * e + (GATED0 + FC + i - back(i, EC) + 1))
                    nc.scalar.activation(silM[:, i % 3, :], pairs[i % 3][:, 0, 0:T], ACT.Silu).then_inc(sil_done, 1)
            for k in range(DC):
                act.wait_ge(x_ready, 8 * (3 + NE) + k + 1 - 8 + 0)
                nc.scalar.activation(sq[:, k, :], xT[:, k, :], ACT.Square).then_inc(sq_ready, 1)
            std(4)
            for k in range(DC):
                act.wait_ge(xn_ready, 8 * 4 + k + 1)
                act.dma_start(yT_d[:, k, :], xn[:, k, :]).then_inc(y_saved, 16)
            for s in (0, 1):
                act.wait_ge(samp_saved[s], 16 * NSAMP // 4)
            act.wait_ge(pool_states, 2 * 16)
            act.wait_ge(y_saved, 16 * DC)

        @block.vector
        def _(dve):
            links = [0]

            def link(ins):
                links[0] += 1
                ins.then_inc(dve_link, 1)
                dve.wait_ge(dve_link, links[0])

            v = nc.vector
            scr = sq[:, :, :].rearrange("p a b -> p (a b)")

            def normalize(i):
                dve.wait_ge(std_ready, i + 1)
                link(v.reciprocal(rstd[:, :], rstd[:, :]))
                for k in range(DC):
                    w = V_NORM[i] + k
                    v.scalar_tensor_tensor(xn[:, k, :], xT[:, k, :], vecs[:, w:w + 1], rstd[:, :],
                                           ALU.mult, ALU.mult).then_inc(xn_ready, 1)

            def residual(first):
                for m in range(DC):
                    dve.wait_ge(dense_done, first + m + 1)
                    v.tensor_tensor(xT[:, m, :], xT[:, m, :], banks[m % 2][:, 0:T], ALU.add).then_inc(x_ready, 1)

            (dt, ardt, ang, mag, sn, cs, carg, lbr, lbi, fr, fi, pc, ps, t0, t1, t2, t3, t4) = (
                par[:, n] for n in range(18))
            are, aim = s5p[:, 0], s5p[:, 1]
            dve.wait_ge(s5_loaded, 16)
            dve.wait_ge(s5_dt, 1)
            v.tensor_tensor(ardt, are, dt, ALU.mult)
            link(v.tensor_tensor(ang, aim, dt, ALU.mult))
            link(v.tensor_scalar(t0, ang, 1.0 / TWO_PI, ROUND, ALU.mult, ALU.add))
            link(v.tensor_scalar(t0, t0, -ROUND, None, ALU.add))
            for part in (PI_1, PI_2, PI_3):
                link(v.scalar_tensor_tensor(ang, t0, -part, ang, ALU.mult, ALU.add))
            link(v.tensor_scalar(ang, ang, math.pi - 1e-6, -math.pi + 1e-6, ALU.min, ALU.max))
            link(v.scalar_tensor_tensor(t1, ang, -1.0, ang, ALU.mult, ALU.max))
            v.tensor_scalar(carg, t1, -1.0, math.pi / 2, ALU.mult, ALU.add).then_inc(s5_arg, 1)
            v.memset(upad[:, :, 0:16], 0.0)
            dve.wait_ge(cst_loaded, 2 * 16)
            normalize(0)
            dve.wait_ge(s5_trig, 1)
            v.tensor_tensor(lbr, mag, cs, ALU.mult)
            v.tensor_tensor(lbi, mag, sn, ALU.mult)
            v.tensor_tensor(t1, are, are, ALU.mult)
            link(v.tensor_tensor(t2, aim, aim, ALU.mult))
            link(v.tensor_tensor(t1, t1, t2, ALU.add))
            link(v.reciprocal(t1, t1))
            link(v.tensor_scalar(t0, lbr, -1.0, None, ALU.add))
            v.tensor_tensor(fr, t0, are, ALU.mult)
            v.tensor_tensor(t3, lbi, aim, ALU.mult)
            v.tensor_tensor(fi, lbi, are, ALU.mult)
            link(v.tensor_tensor(t4, t0, aim, ALU.mult))
            v.tensor_tensor(fr, fr, t3, ALU.add)
            link(v.tensor_tensor(fi, fi, t4, ALU.subtract))
            v.tensor_tensor(fr, fr, t1, ALU.mult)
            v.tensor_tensor(fi, fi, t1, ALU.mult)
            v.memset(cosT[:, :, 0:1], 1.0)
            v.memset(sinT[:, :, 0:1], 0.0)
            v.tensor_copy(pc, cs)
            link(v.tensor_copy(ps, sn))
            n = 1
            while n < NPROMPT:
                m = min(n, NPROMPT - n)
                c0, s0 = cosT[:, :, 0:m], sinT[:, :, 0:m]
                c1, s1 = cosT[:, :, n:n + m], sinT[:, :, n:n + m]
                A, B = tabA[:, :, 0:m], tabB[:, :, 0:m]
                pcb, psb = bc(pc.unsqueeze(2), [P, ST, m]), bc(ps.unsqueeze(2), [P, ST, m])
                v.tensor_tensor(A, c0, pcb, ALU.mult)
                link(v.tensor_tensor(B, s0, psb, ALU.mult))
                link(v.tensor_tensor(c1, A, B, ALU.subtract))
                v.tensor_tensor(A, c0, psb, ALU.mult)
                link(v.tensor_tensor(B, s0, pcb, ALU.mult))
                v.tensor_tensor(s1, A, B, ALU.add)
                v.tensor_tensor(t0, pc, pc, ALU.mult)
                v.tensor_tensor(t2, ps, ps, ALU.mult)
                link(v.tensor_tensor(t3, pc, ps, ALU.mult))
                v.tensor_tensor(pc, t0, t2, ALU.subtract)
                link(v.tensor_tensor(ps, t3, t3, ALU.add))
                n *= 2
            dve.wait_ge(late_loaded, 5 * 16)
            cr, ci = cblk[:, 0], cblk[:, 1]
            frb, fib = bc(fr.unsqueeze(2), [P, ST, 32]), bc(fi.unsqueeze(2), [P, ST, 32])
            w0 = scr[:, 0:512].rearrange("p (a b) -> p a b", a=ST)
            w1 = scr[:, 512:1024].rearrange("p (a b) -> p a b", a=ST)
            v.tensor_tensor(w0, cr, frb, ALU.mult)
            link(v.tensor_tensor(w1, ci, fib, ALU.mult))
            v.tensor_tensor(cf[:, 0], w0, w1, ALU.subtract)
            link(v.tensor_tensor(cf[:, 1], w1, w0, ALU.subtract))
            v.tensor_tensor(w0, cr, fib, ALU.mult)
            link(v.tensor_tensor(w1, ci, frb, ALU.mult))
            link(v.tensor_tensor(w0, w0, w1, ALU.add))
            v.tensor_scalar(cf[:, 2], w0, -1.0, None, ALU.mult).then_inc(s5_folded, 1)

            def windows():
                dve.wait_ge(u_copied, 8)
                cnt = cst[:, C_CNT:C_CNT + 64].rearrange("p (g t) -> p g t", g=NG)
                L = 16 + NPROMPT
                cur = upad
                bufs = [scr[:, 0:4 * L].rearrange("p (g t) -> p g t", g=4),
                        scr[:, 4 * L:7 * L].rearrange("p (g t) -> p g t", g=3)]
                for g in range(NG):
                    w = 1 << g
                    new = bufs[0][:, g:4, :] if g % 2 == 0 else bufs[1][:, g - 1:3, :]
                    old = cur[:, 1:, :] if g else upad
                    s0 = 2 * w - 1
                    link(v.tensor_tensor(new[:, :, s0:], old[:, :, s0:], old[:, :, s0 - w:L - w], ALU.add))
                    link(v.tensor_scalar(ycat[:, g, 0:NPROMPT], new[:, 0, 16:], 1.0 / (2 * w), None, ALU.mult))
                    link(v.tensor_tensor(ycat[:, g, 0:16], new[:, 0, 16:32], cnt[:, g, :], ALU.mult))
                    link(v.tensor_tensor(ycat[:, g, 0:NPROMPT], ycat[:, g, 0:NPROMPT], upad[:, g, 16:],
                                         ALU.subtract))
                    link(v.tensor_reduce(t4[:, 0:NSAMP], pbuf[:, g, :, 16 - 2 * w:], AX.X, ALU.add))
                    v.scalar_tensor_tensor(ycat[:, g, NPROMPT:T], t4[:, 0:NSAMP], 1.0 / (2 * w), pbuf[:, g, :, PAST],
                                           ALU.mult, ALU.subtract).then_inc(d_ready, 1)
                    cur = new

            def skip(c):
                dve.wait_ge(y_done, 4 * c + 4)
                if c == 0:
                    dve.wait_ge(pool_states, 2 * 16)
                v.scalar_tensor_tensor(z[:, c, 0:NPROMPT], ycat[:, 4 + c, 0:NPROMPT], vecs[:, V_D + c:V_D + c + 1],
                                       pairs[2][:, c % 2, 0:NPROMPT], ALU.mult, ALU.add).then_inc(yp_out, 1)

            for j in range(ST):
                dve.wait_ge(bu_done, j + 1)
                src = pairs[j % 2][:, :, 0:NPROMPT]
                v.tensor_copy(buS[:, :, j, :], pairs[j % 2][:, :, NPROMPT:T])
                v.tensor_tensor(rotA, src, bc(cosT[:, j:j + 1, :], [P, 2, NPROMPT]), ALU.mult)
                ins = v.tensor_tensor(rotB, src, bc(sinT[:, j:j + 1, :], [P, 2, NPROMPT]), ALU.mult)
                ins.then_inc(bu_rot, 1)
                dve.wait_ge(bu_rot, j + 1)
                v.tensor_tensor(rotA[:, 0], rotA[:, 0], rotB[:, 1], ALU.add)
                link(v.tensor_tensor(rotA[:, 1], rotA[:, 1], rotB[:, 0], ALU.subtract))
                if j >= 2:
                    dve.wait_ge(back_done, j - 1)
                g = scanned[:, j % 2]
                m = bc(mag[:, j:j + 1], [P, NPROMPT])
                v.tensor_tensor_scan(g[:, 0], m, rotA[:, 0], 0.0, ALU.mult, ALU.add)
                v.tensor_tensor_scan(g[:, 1], m, rotA[:, 1], 0.0, ALU.mult, ALU.add).then_inc(scan_done, 1)
                dve.wait_ge(scan_done, j + 1)
                v.tensor_copy(glast[:, :, j:j + 1], g[:, :, NPROMPT - 1:])
                if j == 6:
                    windows()
                if j % 4 == 3 and j >= 7:
                    skip(j // 4 - 1)
            skip(3)
            shp = [P, ST, NSAMP]
            q = [scr[:, 128 * n:128 * n + 128].rearrange("p (a b) -> p a b", a=ST) for n in range(8)]

            def wide(a):
                return bc(a.unsqueeze(2), shp)

            v.tensor_tensor(q[0], h0[:, 0], wide(lbr), ALU.mult)
            v.tensor_tensor(q[1], h0[:, 1], wide(lbi), ALU.mult)
            v.tensor_tensor(q[2], buS[:, 0], wide(fr), ALU.mult)
            v.tensor_tensor(q[3], buS[:, 1], wide(fi), ALU.mult)
            v.tensor_tensor(q[4], h0[:, 1], wide(lbr), ALU.mult)
            v.tensor_tensor(q[5], h0[:, 0], wide(lbi), ALU.mult)
            v.tensor_tensor(q[6], buS[:, 1], wide(fr), ALU.mult)
            link(v.tensor_tensor(q[7], buS[:, 0], wide(fi), ALU.mult))
            v.tensor_tensor(q[0], q[0], q[1], ALU.subtract)
            v.tensor_tensor(q[2], q[2], q[3], ALU.subtract)
            v.tensor_tensor(q[4], q[4], q[5], ALU.add)
            link(v.tensor_tensor(q[6], q[6], q[7], ALU.add))
            v.tensor_tensor(hS[:, 0], q[0], q[2], ALU.add)
            link(v.tensor_tensor(hS[:, 1], q[4], q[6], ALU.add))
            v.tensor_scalar(nhi, hS[:, 1], -1.0, None, ALU.mult).then_inc(hs_ready, 1)
            cL, sL = cosT[:, :, NPROMPT - 1], sinT[:, :, NPROMPT - 1]

            def times(a, b):
                v.tensor_tensor(t0, glast[:, 0], a, ALU.mult)
                v.tensor_tensor(t1, glast[:, 1], b, ALU.mult)
                v.tensor_tensor(t2, glast[:, 0], b, ALU.mult)
                link(v.tensor_tensor(t3, glast[:, 1], a, ALU.mult))
                v.tensor_tensor(glast[:, 0], t0, t1, ALU.subtract)
                return v.tensor_tensor(glast[:, 1], t2, t3, ALU.add)

            link(times(cL, sL))
            times(fr, fi).then_inc(s5_states, 1)
            dve.wait_ge(ys_done, 1)
            for c in range(4):
                v.scalar_tensor_tensor(z[:, c, NPROMPT:T], ycat[:, 4 + c, NPROMPT:T], vecs[:, V_D + c:V_D + c + 1],
                                       pairs[0][:, 0, c * NSAMP:(c + 1) * NSAMP], ALU.mult, ALU.add
                                       ).then_inc(y_out, 1)
            for m in range(4):
                dve.wait_ge(sig_ready, m + 1)
                v.tensor_tensor(ycat[:, 4 + m, :], z[:, m, :], sig[:, m % 2, :], ALU.mult).then_inc(gated, 1)
            residual(DENSE_OUT)
            normalize(1)
            with dve.Fori(0, 2) as r:
                for i in range(SLOTS):
                    dve.wait_ge(sil_done, SLOTS * r + (i + 1))
                    v.tensor_tensor(hF[:, bass.ds(SLOTS * r + i, 1), :].rearrange("p a b -> p (a b)"),
                                    silF[:, i % 3, :], pairs[i % 3][:, 1, 0:T], ALU.mult).then_inc(gated, 1)
            residual(DENSE_DOWN)
            normalize(2)

            v.memset(attS, 0.0)
            dve.wait_ge(gl_ready, 1)
            link(v.scalar_tensor_tensor(gx, gx, 0.0, gl, ALU.min, ALU.subtract))
            link(v.tensor_scalar(gx, gx, 1.0 / 16.0, None, ALU.mult))
            for h in range(H):
                last = v.tensor_tensor_scan(bT[:, h, :], cst[:, C_RESET:C_RESET + NPROMPT], gx[:, h, 0:NPROMPT], 0.0,
                                            ALU.mult, ALU.add)
            link(last)
            b_sub = bT.rearrange("p h (n s) -> p (h n) s", s=SUB)
            b_ch = bT.rearrange("p h (n s) -> p (h n) s", s=CH)
            HN = H * NCH
            v.tensor_tensor(qd.rearrange("p h (n s) -> p (h n) s", s=SUB), b_sub,
                            bc(b_sub[:, :, MID:MID + 1], [P, HN * NSUB, SUB]), ALU.subtract).then_inc(dec_arg, 1)
            for i in range(NSUB):
                w = SUB * (i + 1)
                r = SUB * i + MID
                v.tensor_tensor(kd[i].rearrange("p h (n s) -> p (h n) s", s=w), bc(b_ch[:, :, r:r + 1], [P, HN, w]),
                                b_ch[:, :, 0:w], ALU.subtract).then_inc(dec_arg, 1)
            v.tensor_tensor(ke.rearrange("p h (n s) -> p (h n) s", s=CH), bc(b_ch[:, :, CH - 1:CH], [P, HN, CH]),
                            b_ch, ALU.subtract).then_inc(dec_arg, 1)
            v.tensor_copy(elast.rearrange("p h n -> p (h n)").unsqueeze(2), b_ch[:, :, CH - 1:CH]).then_inc(dec_arg, 1)
            k4 = kT[:, :, 0:NPROMPT].rearrange("p h (n s) -> p h n s", s=CH)
            dve.wait_ge(q_copied, 8)
            dve.wait_ge(dec_exp, 1)
            v.tensor_tensor(qd, qd, qT[:, :, 0:NPROMPT], ALU.mult).then_inc(dec_ready, 1)
            for i in range(NSUB):
                w = SUB * (i + 1)
                dve.wait_ge(dec_exp, i + 2)
                k3 = kd[i].rearrange("p h (n s) -> p h n s", s=w)
                v.tensor_tensor(k3, k3, k4[:, :, :, 0:w], ALU.mult).then_inc(dec_ready, 1)
            dve.wait_ge(dec_exp, 6)
            v.tensor_tensor(qe, qe, qT[:, :, 0:NPROMPT], ALU.mult).then_inc(dec_ready, 1)
            dve.wait_ge(dec_exp, 7)
            v.tensor_tensor(ke, ke, kT[:, :, 0:NPROMPT], ALU.mult).then_inc(dec_ready, 1)
            dve.wait_ge(dec_exp, 8)
            for c in range(NCH):
                if c >= 2:
                    dve.wait_ge(o_done, c - 1)
                dve.wait_ge(att_done, NSUB * (c + 1))
                for i in range(NSUB):
                    w = SUB * (i + 1)
                    a = pairs[2][0:w, 1, 0:H * CH].rearrange("p (h t) -> p h t", h=H)[:, :, SUB * i:w]
                    m = bc(cst[0:w, C_MASK + SUB * i:C_MASK + w].unsqueeze(1), [w, H, SUB])
                    v.tensor_tensor(attS[0:w, c % 2, :, SUB * i:w], a, m, ALU.mult).then_inc(att_copied, 1)
                dve.wait_ge(ktr_done, c + 1)
                if c:
                    dve.wait_ge(kv_done, 2 * c)
                v.tensor_copy(ketok, pairs[2][0:CH, 0, :]).then_inc(ktr_copied, 1)
                for h in range(H):
                    dve.wait_ge(kv_done, 2 * c + h // 2 + 1)
                    kv = banks[h // 2][:, (h % 2) * DV:(h % 2 + 1) * DV]
                    if c == 0:
                        v.tensor_copy(S[:, h, :], kv).then_inc(S_ready, 1)
                    else:
                        if h == 0:
                            dve.wait_ge(S_ready, H * c)
                        v.scalar_tensor_tensor(S[:, h, :], S[:, h, :], elast[:, h, c:c + 1], kv,
                                               ALU.mult, ALU.add).then_inc(S_ready, 1)
            dve.wait_ge(dec_exp, 9)
            for n in range(NSAMP // 2 * H):
                p, h = n // H, n % H
                if h == 0:
                    dve.wait_ge(samp_loaded[p % 2], 16 * (p // 2 + 1))
                dve.wait_ge(outer_done, n + 1)
                for s in range(2):
                    b = 2 * p + s
                    last = v.scalar_tensor_tensor(samp[p % 2][:, s, h, :], samp[p % 2][:, s, h, :], egS[:, h, b:b + 1],
                                                  banks[n % 2][:, s * DV:(s + 1) * DV], ALU.mult, ALU.add)
                last.then_inc(samp_ready, 1)
            for h in range(H):
                dve.wait_ge(ostd_ready, h + 1)
                link(v.reciprocal(rms[:, h, :], rms[:, h, :]))
                for c in range(VC):
                    last = v.scalar_tensor_tensor(oG[:, VC * h + c, :], oT[:, VC * h + c, :],
                                                  vecs[:, V_GNORM + c:V_GNORM + c + 1], rms[:, h, :],
                                                  ALU.mult, ALU.mult)
                link(last)
                dve.wait_ge(q_copied, 24)
                v.tensor_tensor(oG[:, VC * h:VC * h + VC, :], oG[:, VC * h:VC * h + VC, :],
                                gS[:, VC * h:VC * h + VC, :], ALU.mult).then_inc(og_ready, 1)
            residual(DENSE_OUT_O)
            normalize(3)
            lg, pr, mx8, ix, oh1, oh2 = (rt[:, n].rearrange("p (t e) -> p t e", t=NRT) for n in range(6))
            shp = [RT, NRT, NE]
            mx, sm, den = (rsc[:, n] for n in range(3))
            iota = bc(cst[0:RT, C_IOTA:C_IOTA + NE].unsqueeze(1), shp)
            dve.wait_ge(logit_done, 1)
            lp = pairs[0][0:RT, 0, 0:NRT * NE].rearrange("p (t e) -> p t e", t=NRT)
            link(v.tensor_reduce(mx, lp, AX.X, ALU.max))
            v.tensor_tensor(lg, lp, bc(mx.unsqueeze(2), shp), ALU.subtract).then_inc(shifted, 1)
            dve.wait_ge(exped, 1)
            link(v.tensor_reduce(sm, lg, AX.X, ALU.add))
            link(v.reciprocal(sm, sm))
            link(v.tensor_tensor(pr, lg, bc(sm.unsqueeze(2), shp), ALU.mult))
            for t in range(NRT):
                link(v.max(mx8[:, t, :], pr[:, t, :]))
                link(v.max_index(idx[:, t * 8:(t + 1) * 8], mx8[:, t, :], pr[:, t, :]))
            link(v.tensor_copy(ix.rearrange("p t e -> p (t e)"), idx[:, :]))
            v.tensor_tensor(oh1, iota, bc(ix[:, :, 0:1], shp), ALU.is_equal)
            v.tensor_tensor(oh2, iota, bc(ix[:, :, 1:2], shp), ALU.is_equal)
            link(v.tensor_tensor(den, mx8[:, :, 0], mx8[:, :, 1], ALU.add))
            link(v.reciprocal(den, den))
            v.tensor_tensor(oh1, oh1, bc(mx8[:, :, 0:1], shp), ALU.mult)
            link(v.tensor_tensor(oh2, oh2, bc(mx8[:, :, 1:2], shp), ALU.mult))
            link(v.tensor_tensor(oh1, oh1, oh2, ALU.add))
            v.tensor_tensor(oh1, oh1, bc(den.unsqueeze(2), shp), ALU.mult).then_inc(gate_ready, 1)
            dve.wait_ge(gbc_copied, NE)
            with dve.Fori(0, NE) as e:
                for i in range(EC):
                    dve.wait_ge(sil_done, EC * e + (FC + i + 1))
                    v.tensor_tensor(gpre[:, i % 3, :], silM[:, i % 3, :], pairs[i % 3][:, 1, 0:T],
                                    ALU.mult).then_inc(gpre_done, 1)
                    dve.wait_ge(gpre_done, EC * e + (i + 1))
                    v.tensor_tensor(hM[:, i, :], gpre[:, i % 3, :],
                                    gbc[:, bass.ds(e, 1), :].rearrange("p a b -> p (a b)"),
                                    ALU.mult).then_inc(gated, 1)
                for m in range(DC):
                    dve.wait_ge(dense_done, DC * e + (DENSE_MOE + m + 1))
                    v.tensor_tensor(xT[:, m, :], xT[:, m, :], banks[m % 2][:, 0:T], ALU.add).then_inc(x_ready, 1)
            normalize(4)

        @block.tensor
        def _(pe):
            mm = nc.tensor.matmul

            def slot(n):
                return ring[:, n % SLOTS, :].rearrange("p (t m) -> p t m", m=P)

            def unit_loaded(n):
                pe.wait_ge(slot_full[n % SLOTS], 16 * (n // SLOTS + 1))

            def bank_free(d):
                if d < 2:
                    return
                if d < DENSE_POOL + 2:
                    pe.wait_ge(u_copied, d - 1)
                elif d < DENSE_GLU + 2:
                    pe.wait_ge(pool_out, d - DENSE_POOL - 1)
                elif d < DENSE_OUT + 2:
                    pe.wait_ge(sig_ready, d - DENSE_GLU - 1)
                elif d < DENSE_IN_O + 2:
                    pe.wait_ge(x_ready, d - DENSE_OUT - 1)
                elif d < DENSE_OUT_O + 2:
                    pe.wait_ge(q_copied, d - DENSE_IN_O - 1)
                else:
                    pe.wait_ge(x_ready, d - DENSE_OUT_O - 1 + 16)

            def dense(d, unit, tile, kc, rhs, ready=None):
                bank_free(d)
                for k in range(kc):
                    n = unit + (tile + k) // UT
                    if k == 0 or (tile + k) % UT == 0:
                        unit_loaded(n)
                    if ready is not None:
                        pe.wait_ge(ready[0], ready[1] + k + 1)
                    last = mm(banks[d % 2][:, 0:T], slot(n)[:, (tile + k) % UT, :], rhs[:, k, :],
                              start=(k == 0), stop=(k == kc - 1))
                last.then_inc(dense_done, 1)

            def sum_squares(i):
                for k in range(DC):
                    pe.wait_ge(sq_ready, DC * i + k + 1)
                    last = mm(pairs[2][:, 1, 0:T], ones, sq[:, k, :], start=(k == 0), stop=(k == DC - 1))
                last.then_inc(ss_ready, 1)

            pe.wait_ge(cst_loaded, 2 * 16)
            sum_squares(0)

            def project_in(o):
                dense(o, W_IN_E, DC * o, DC, xn, (xn_ready, 0) if o == 0 else None)

            project_in(0)
            project_in(1)
            pe.wait_ge(late_loaded, 5 * 16)

            def y_tile(j):
                c, r = j // 4, 32 * (j % 4)
                if j == 0:
                    pe.wait_ge(s5_folded, 1)
                if j % 4 == 0 and c >= 2:
                    pe.wait_ge(yp_out, c - 1)
                pe.wait_ge(back_done, j + 1)
                out = pairs[2][r:r + 32, c % 2, 0:NPROMPT]
                mm(out, cf[:, 0, j, :], backC[:, j % 2, 0], start=True, stop=False)
                mm(out, cf[:, 1, j, :], backS[:, j % 2, 1], start=False, stop=False)
                mm(out, cf[:, 2, j, :], backS[:, j % 2, 0], start=False, stop=False)
                mm(out, cf[:, 2, j, :], backC[:, j % 2, 1], start=False, stop=True).then_inc(y_done, 1)

            for j in range(ST):
                c, r = j // 4, 32 * (j % 4)
                if j % 4 == 0:
                    pe.wait_ge(u_copied, c + 1)
                if j >= 2:
                    pe.wait_ge(bu_rot, j - 1)
                for x in range(2):
                    last = mm(pairs[j % 2][:, x, 0:T], bblk[r:r + 32, c, x, :], ycat[r:r + 32, 4 + c, :],
                              start=True, stop=True)
                last.then_inc(bu_done, 1)
                if j < 6:
                    project_in(2 + j)
                if 8 <= j < 12:
                    g = j - 8
                    pe.wait_ge(d_ready, g + 1)
                    bank_free(DENSE_POOL + g)
                    mm(banks[g % 2][:, 0:T], wpool[:, g, :], ycat[:, g, :], start=True, stop=True
                       ).then_inc(dense_done, 1)
                if j:
                    y_tile(j - 1)
            y_tile(ST - 1)
            pe.wait_ge(hs_ready, 1)
            for j in range(ST):
                c, r = j // 4, 32 * (j % 4)
                out = pairs[0][r:r + 32, 0, c * NSAMP:(c + 1) * NSAMP]
                mm(out, cblk[:, 0, j, :], hS[:, 0, j, :], start=True, stop=False)
                last = mm(out, cblk[:, 1, j, :], nhi[:, j, :], start=False, stop=True)
            last.then_inc(ys_done, 1)
            for m in range(4):
                dense(DENSE_GLU + m, W_GLU, 4 * m, 4, z, (z_ready, 0) if m == 0 else None)
            for m in range(DC):
                if m == 0:
                    pe.wait_ge(pool_out, 4)
                    pe.wait_ge(gated, 4)
                dense(DENSE_OUT + m, W_OUT_E, DC * m, DC, ycat)
            sum_squares(1)
            pe.wait_ge(xn_ready, 2 * DC)
            with pe.Fori(0, 2) as r:
                for i in range(SLOTS):
                    s = (FFN_UP + i) % SLOTS
                    pe.wait_ge(slot_full[s], 16 * r + 16 * ((FFN_UP + i) // SLOTS + 1))
                    pe.wait_ge(gated, SLOTS * r + (GATED0 + i - back(i, SLOTS) + 1))
                    for x in range(2):
                        for k in range(DC):
                            last = mm(pairs[i % 3][:, x, 0:T], slot(s)[:, DC * x + k, :], xn[:, k, :],
                                      start=(k == 0), stop=(k == DC - 1))
                    last.then_inc(up_done, 1)
            for m in range(DC):
                dense(DENSE_DOWN + m, FFN_DOWN, FC * m, FC, hF, (gated, GATED0) if m == 0 else None)
            sum_squares(2)
            pe.wait_ge(l1_loaded, 3 * 16)
            for k in range(DC):
                pe.wait_ge(xn_ready, 2 * DC + k + 1)
                last = mm(pairs[2][0:16, 0, 0:T], gk1[:, k, :], xn[:, k, :], start=(k == 0), stop=(k == DC - 1))
            last.then_inc(low_done, 1)
            pe.wait_ge(low_copied, 1)
            for h in range(H):
                if h >= 2:
                    pe.wait_ge(gx_ready, h - 1)
                mm(pairs[h % 2][:, 0, 0:T], gk2[:, h * P:(h + 1) * P], low, start=True, stop=True
                   ).then_inc(gk_done, 1)
            for o in range(24):
                dense(DENSE_IN_O + o, W_IN_O, DC * o, DC, xn)
            for c in range(NCH):
                for i in range(NSUB):
                    w = SUB * (i + 1)
                    if c == 0:
                        pe.wait_ge(dec_ready, i + 2)
                    if c and i == 0:
                        pe.wait_ge(att_copied, NSUB * c)
                    for h in range(H):
                        last = mm(pairs[2][0:w, 1, h * CH + SUB * i:h * CH + w], kd[i][:, h, c * w:(c + 1) * w],
                                  qd[:, h, c * CH + SUB * i:c * CH + w], start=True, stop=True)
                    last.then_inc(att_done, 1)
                if c:
                    pe.wait_ge(vtr_copied, c)
                else:
                    pe.wait_ge(q_copied, 16)
                for k in range(DC):
                    last = nc.tensor.transpose(pairs[0][0:CH, k // 4, (k % 4) * P:(k % 4 + 1) * P],
                                               vT[:, k, c * CH:(c + 1) * CH], ident)
                last.then_inc(vtr_done, 1)
                if c:
                    pe.wait_ge(ktr_copied, c)
                else:
                    pe.wait_ge(dec_ready, 7)
                for h in range(H):
                    last = nc.tensor.transpose(pairs[2][0:CH, 0, h * P:(h + 1) * P],
                                               ke[:, h, c * CH:(c + 1) * CH], ident)
                last.then_inc(ktr_done, 1)
                pe.wait_ge(att_copied, NSUB * (c + 1))
                pe.wait_ge(vtr_copied, c + 1)
                if c:
                    pe.wait_ge(o_copied, c)
                    pe.wait_ge(S_ready, H * c)
                for k in range(DC):
                    h = k // VC
                    out = pairs[1][:, k // 4, (k % 4) * CH:(k % 4 + 1) * CH]
                    last = mm(out, vtok[c % 2][:, k * P:(k + 1) * P], attS[:, c % 2, h, :], start=True, stop=(c == 0))
                    if c:
                        last = mm(out, S[:, h, (k % VC) * P:(k % VC + 1) * P], qe[:, h, c * CH:(c + 1) * CH],
                                  start=False, stop=True)
                last.then_inc(o_done, 1)
                pe.wait_ge(ktr_copied, c + 1)
                if c == 0:
                    pe.wait_ge(q_copied, 24)
                for h in range(H):
                    last = mm(banks[h // 2][:, (h % 2) * DV:(h % 2 + 1) * DV], ketok[:, h * P:(h + 1) * P],
                              vtok[c % 2][:, h * DV:(h + 1) * DV], start=True, stop=True)
                    if h % 2:
                        last.then_inc(kv_done, 1)
            pe.wait_ge(vtr_copied, NCH)
            pe.wait_ge(o_copied, NCH)
            for part in range(3):
                for k in range(4):
                    src = kT[:, k, NPROMPT:T] if part == 0 else vT[:, 4 * (part - 1) + k, NPROMPT:T]
                    dst = (pairs[0][0:NSAMP, 0], pairs[0][0:NSAMP, 1], pairs[1][0:NSAMP, 0])[part]
                    last = nc.tensor.transpose(dst[:, k * P:(k + 1) * P], src, ident)
                last.then_inc(str_done, 1)
            pe.wait_ge(S_ready, H * NCH)
            for n in range(NSAMP // 2 * H):
                p, h = n // H, n % H
                pe.wait_ge(vblk_ready, n + 1)
                if n >= 2:
                    pe.wait_ge(samp_ready, n - 1)
                mm(banks[n % 2][:, :], ktokS[:, h * P:(h + 1) * P], vblk[:, n % 2, :], start=True, stop=True
                   ).then_inc(outer_done, 1)
                if h == H - 1:
                    pe.wait_ge(samp_ready, n + 1)
                    for s in range(2):
                        b = 2 * p + s
                        for k in range(DC):
                            last = mm(pairs[1][:, 1, b * DC + k:b * DC + k + 1],
                                      samp[p % 2][:, s, k // VC, (k % VC) * P:(k % VC + 1) * P],
                                      qT[:, k // VC, NPROMPT + b:NPROMPT + b + 1], start=True, stop=True)
                    last.then_inc(so_done, 1)
            for h in range(H):
                pe.wait_ge(osq_ready, VC * (h + 1))
                if h >= 2:
                    pe.wait_ge(ostd_ready, h - 1)
                for c in range(VC):
                    last = mm(pairs[h % 2][:, 0, 0:T], ones, sq[:, VC * h + c, :], start=(c == 0), stop=(c == VC - 1))
                last.then_inc(oss_done, 1)
            pe.wait_ge(og_ready, H)
            for m in range(DC):
                dense(DENSE_OUT_O + m, W_OUT_O, DC * m, DC, oG)
            sum_squares(3)
            pe.wait_ge(xn_ready, 4 * DC)
            for t in range(NRT):
                for k in range(DC):
                    last = mm(pairs[0][0:RT, 0, t * NE:(t + 1) * NE], xn[:, k, t * RT:(t + 1) * RT], router[:, k, :],
                              start=(k == 0), stop=(k == DC - 1))
            last.then_inc(logit_done, 1)
            pe.wait_ge(gate_ready, 1)
            for t in range(NRT):
                last = nc.tensor.transpose(pairs[0][0:NE, 1, t * RT:(t + 1) * RT], rt[:, 4, t * NE:(t + 1) * NE],
                                           cst[0:RT, C_ID:C_ID + RT])
            last.then_inc(gtr_done, 1)
            pe.wait_ge(gT_ready, 1)
            pe.wait_ge(sel_loaded, 16)
            for e in range(NE):
                if e >= 2:
                    pe.wait_ge(gbc_copied, e - 1)
                mm(pairs[1 + e % 2][:, 0, 0:T], sel[:, e, :], gT, start=True, stop=True).then_inc(gbc_done, 1)
            pe.wait_ge(gbc_copied, NE)
            with pe.Fori(0, NE) as e:
                for i in range(EC):
                    s = (MOE + i) % SLOTS
                    pe.wait_ge(slot_full[s], 16 * e + 16 * ((MOE + i) // SLOTS + 1))
                    pe.wait_ge(gated, EC * e + (GATED0 + FC + i - back(i, EC) + 1))
                    for x in range(2):
                        for k in range(DC):
                            last = mm(pairs[i % 3][:, x, 0:T], slot(s)[:, DC * x + k, :], xn[:, k, :],
                                      start=(k == 0), stop=(k == DC - 1))
                    last.then_inc(up_done, 1)
                for m in range(DC):
                    n = MOE + EC + m // 2
                    s = n % SLOTS
                    if m % 2 == 0:
                        pe.wait_ge(slot_full[s], 16 * e + 16 * (n // SLOTS + 1))
                    pe.wait_ge(x_ready, DC * e + (3 * DC + m - 1))
                    for k in range(EC):
                        if m == 0:
                            pe.wait_ge(gated, EC * e + (GATED0 + FC + k + 1))
                        last = mm(banks[m % 2][:, 0:T], slot(s)[:, EC * (m % 2) + k, :], hM[:, k, :],
                                  start=(k == 0), stop=(k == EC - 1))
                    last.then_inc(dense_done, 1)
            sum_squares(4)


def kernel(**inputs):
    import numpy as np
    import concourse.bacc as bacc
    from concourse import mybir as mb
    from concourse.bass_utils import run_bass_kernel_spmd as run

    a = {k: np.asarray(v) for k, v in inputs.items()}
    f = np.float32

    def features(x):
        return x.reshape(x.shape[0], -1, P).transpose(2, 1, 0)

    def tiles(w):
        K, M = w.shape
        return w.reshape(K // P, P, M // P, P).transpose(2, 0, 1, 3)

    def units(t, n):
        t = t.reshape(-1, n, P, P)
        return t.transpose(0, 2, 1, 3).reshape(t.shape[0], P, n * P)

    x = np.concatenate([a["meta_tokens"], a["x_prompt"][0], a["x_sample"][:, 0]], axis=0)
    ins = {"xT": features(x)}
    vec = np.concatenate([a["norm_mix_e"][0], a["norm_ffn_e"][0], a["norm_mix_o"][0], a["norm_ffn_o"][0],
                          a["norm_final"], a["pool_scale"][0], a["s5_d"][0], a["b_glu"][0], a["b_gk"][0],
                          a["gla_norm"][0]])
    ins["vecs"] = vec.reshape(-1, P).T
    cst = np.zeros((P, NCST), f)
    cst[:, C_ID:C_ID + P] = np.eye(P)
    cst[:, C_ONE:C_ONE + P] = 1
    cst[:CH, C_MASK:C_MASK + CH] = np.triu(np.ones((CH, CH)))
    cst[:, C_IOTA:C_IOTA + NE] = np.arange(NE)
    for g in range(NG):
        cst[:, C_CNT + 16 * g:C_CNT + 16 * g + 16] = 1.0 / np.minimum(np.arange(16) + 1, 2 << g)
    cst[:, C_RESET:C_RESET + NPROMPT] = np.arange(NPROMPT) % CH != 0
    cst[:, C_EPS] = EPS
    ins["cst"] = cst
    sel = np.zeros((NE, NE, P), f)
    sel[np.arange(NE), np.arange(NE)] = 1
    ins["sel"] = sel

    def states(s):
        s = s.reshape(s.shape[:-2] + (ST, P))
        return np.moveaxis(np.moveaxis(s, -1, 0), -1, 1)

    G = 2 * ST
    logdt = np.broadcast_to(a["s5_log_dt"][0][:, None], (G, 64))
    ins["s5p"] = np.stack([states(a["s5_a_re"][0]), states(a["s5_a_im"][0]), states(logdt)], 1)
    ins["h0"] = np.stack([states(a["state_s5_re"][0]), states(a["state_s5_im"][0])], 1)
    bb = np.zeros((4, 2, 16, 4, 2, 2, 64), f)
    cc = np.zeros((2, 64, 2, ST, 2, 16), f)
    for x_, (bn, cn) in enumerate((("s5_b_re", "s5_c_re"), ("s5_b_im", "s5_c_im"))):
        bt = a[bn][0].reshape(4, 4, 2, 64, 16)
        ct = a[cn][0].reshape(ST, 2, 16, 64)
        for g in range(2):
            bb[:, g, :, :, x_, g, :] = bt[:, :, g].transpose(1, 3, 0, 2)
            cc[g, :, x_, :, g, :] = ct[:, g].transpose(2, 0, 1)
    ins["bblk"] = bb.reshape(P, 4, 2, P)
    ins["cblk"] = cc.reshape(P, 2, ST, 32)
    ins["past"] = a["state_pool"][0].reshape(NSAMP, PAST, NG, P).transpose(3, 2, 0, 1)
    ins["wpool"] = a["w_pool"][0].transpose(1, 0, 2)
    win = tiles(a["w_in_e"][0])
    up = np.stack([tiles(a["ffn_w1"][0]), tiles(a["ffn_w3"][0])], 1)
    ins["main"] = np.concatenate([units(t, UT) for t in (
        np.concatenate([win[4:], win[:4]]), tiles(a["w_glu"][0]), tiles(a["w_out_e"][0]), up,
        tiles(a["ffn_w2"][0]), tiles(a["w_in_o"][0]), tiles(a["w_out_o"][0]))])
    ins["up"] = units(np.stack([np.stack([tiles(a["moe_w1"][0, e]), tiles(a["moe_w3"][0, e])], 1)
                                for e in range(NE)]), UT)
    ins["down"] = units(np.stack([tiles(a["moe_w2"][0, e]) for e in range(NE)]), 2 * EC)
    ins["gk1"] = a["w_gk1"][0].reshape(DC, P, 16).transpose(1, 0, 2)
    ins["gk2"] = a["w_gk2"][0]
    ins["router"] = a["w_router"][0].reshape(DC, P, NE).transpose(1, 0, 2)
    ins["sgla"] = a["state_gla"][0].transpose(2, 0, 1, 3)
    outs = [("yT", (P, DC, T)), ("poolp", (P, NG, PAST)), ("pools", (P, NG, NSAMP, PAST)),
            ("s5prompt", (P, 2, ST)), ("s5samp", (P, 2, ST, NSAMP)), ("glap", (P, H, DV)),
            ("glas", (P, NSAMP, H, DV))]
    nc = bacc.Bacc("TRN2", target_bir_lowering=False, num_devices=1)
    arrays, args = {}, []
    for name, v in ins.items():
        v = np.ascontiguousarray(v)
        arrays["in_" + name] = v
        args.append(nc.dram_tensor("in_" + name, v.shape, mb.dt.from_np(v.dtype), kind="ExternalInput").ap())
    for name, shape in outs:
        args.append(nc.dram_tensor("out_" + name, shape, mb.dt.float32, kind="ExternalOutput").ap())
    build(nc, *args)
    r = run(nc, [arrays], core_ids=[0]).results[0]
    o = {name: np.asarray(r["out_" + name]) for name, _ in outs}

    y = o["yT"].transpose(2, 1, 0).reshape(T, D)
    poolp = o["poolp"].transpose(2, 1, 0).reshape(1, 1, PAST, NG * P)
    pools = o["pools"].transpose(2, 3, 1, 0).reshape(1, NSAMP, PAST, NG * P)
    s5p = o["s5prompt"].transpose(1, 2, 0).reshape(2, 1, 1, G, 64)
    s5s = o["s5samp"].transpose(1, 3, 2, 0).reshape(2, 1, NSAMP, G, 64)
    glap = o["glap"].transpose(1, 0, 2)[None, None]
    glas = o["glas"].transpose(1, 2, 0, 3)[None]
    res = (y[None, 16:NPROMPT], y[NPROMPT:, None], poolp, pools, s5p[0], s5s[0], s5p[1], s5s[1], glap, glas)
    return tuple(np.ascontiguousarray(v) for v in res)
```

```python
import math

import concourse.bass as bass
from concourse import mybir
from contextlib import ExitStack

F32 = mybir.dt.float32
U32 = mybir.dt.uint32
ALU = mybir.AluOpType
ACT = mybir.ActivationFunctionType
AX = mybir.AxisListType

P = 128
D = 1024
DC = D // P
NPROMPT = 272
NSAMP = 8
T = NPROMPT + NSAMP
EPS = 1e-6
NG = 4
PAST = 15
ST = 16
FF = 2816
FC = FF // P
H = 4
DV = 256
VC = DV // P
CH = 68
NCH = NPROMPT // CH
SUB = 17
NSUB = CH // SUB
MID = SUB // 2
NE = 8
EC = 896 // P
CAP = 128
EW = EC * P
HW = EW // 2
NRT = 3
RT = -(-T // NRT)
RT0 = [0, RT, T - RT]

TDVE = 10
NDBL = math.ceil(math.log2(NPROMPT))
DBL0 = 4
UT = 16
UNIT = UT * P
SLOTS = 11
W_IN_E, W_GLU, W_OUT_E = 0, 4, 5
FFN_UP = W_OUT_E + 4
FFN_DOWN = FFN_UP + FC
W_IN_O = FFN_DOWN + FC * DC // UT
W_OUT_O = W_IN_O + 12
MOE = W_OUT_O + 4

DENSE_POOL, DENSE_GLU, DENSE_OUT, DENSE_DOWN, DENSE_IN_O, DENSE_OUT_O, DENSE_MOE = 8, 12, 16, 24, 32, 56, 64
GATED0 = 4

V_NORM = [0, 8, 16, 24, 32]
V_PSCALE, V_D, V_BGLU, V_BGK, V_GNORM = 40, 44, 48, 52, 56
NVEC = 58
C_ID, C_ONE, C_MASK, C_IOTA = 0, 128, 256, 324
C_CNT, C_RESET, C_EPS = C_IOTA + P, C_IOTA + P + 64, C_IOTA + P + 64 + NPROMPT
C_OWN = C_EPS + 1
C_SLOT = C_OWN + NRT
NCST = C_SLOT + 1


TWO_PI = 2 * math.pi
PI_1 = 6.28125
PI_2 = 0.0019350051879882812
PI_3 = TWO_PI - PI_1 - PI_2
ROUND = 12582912.0


def build(nc, xT_d, vecs_d, cst_d, sel_d, s5p_d, h0_d, bblk_d, cblk_d, past_d, wpool_d, main_d,
          up_d, down_d, gk1_d, gk2_d, router_d, sgla_d,
          yT_d, poolp_d, pools_d, s5p_out, s5s_out, glap_d, glas_d):
    ctx = ExitStack()
    with ctx:
        def sb(name, shape, dt=F32):
            return ctx.enter_context(nc.sbuf_tensor(name, shape, dt))

        def sem(name):
            return ctx.enter_context(nc.semaphore(name))

        ring = sb("ring", [P, SLOTS, UNIT])
        xT = sb("xT", [P, DC, T])
        xn = sb("xn", [P, DC, T])
        sq = sb("sq", [P, DC, T])
        rstd = sb("rstd", [P, T])
        vecs = sb("vecs", [P, NVEC])
        cst = sb("cst", [P, NCST])
        ident = cst[:, C_ID:C_ID + P]
        ones = cst[:, C_ONE:C_ONE + P]
        W = 22400
        work = sb("work", [P, W])
        at = [0]

        def region(*shape, rows=P):
            n = int(math.prod(shape))
            v = work[0:rows, at[0]:at[0] + n]
            at[0] += n
            assert at[0] <= W, at[0]
            if len(shape) == 2:
                v = v.rearrange("p (a b) -> p a b", a=shape[0])
            if len(shape) == 3:
                v = v.rearrange("p (a b c) -> p a b c", a=shape[0], b=shape[1])
            return v

        cosT = region(ST, NPROMPT)
        sinT = region(ST, NPROMPT)
        dyn = at[0]
        rotA = region(2, 2, NPROMPT)
        rotB = sq[:, :, :].rearrange("p a b -> p (a b)")[:, 0:4 * NPROMPT].rearrange("p (j x t) -> p j x t", j=2, x=2)
        scanned = region(2, 2, NPROMPT)
        backC = region(2, 2, NPROMPT)
        backS = region(2, 2, NPROMPT)
        tab_scratch = [work[:, a:a + 2 * P * n].rearrange("p (x j t) -> p x j t", x=2, t=P)
                       for a, n in ((dyn, TDVE), (dyn + 2 * P * TDVE, ST - TDVE), (dyn, ST))]
        sig = backC.rearrange("p a b c -> p (a b c)")[:, 0:2 * T].rearrange("p (a b) -> p a b", a=2)
        cblk = region(2, ST, 32)
        cf = region(3, ST, 32)
        bblk = region(4, 2, P)
        ycat = region(DC, T)
        upad = region(NG, 16 + NPROMPT)
        z = upad.rearrange("p a b -> p (a b)")[:, 0:4 * T].rearrange("p (a b) -> p a b", a=4)
        pbuf = region(NG, NSAMP * 16).rearrange("p g (b t) -> p g b t", b=NSAMP)
        h0 = region(2, ST, NSAMP)
        buS = region(2, ST, NSAMP)
        hS = region(2, ST, NSAMP)
        par = region(20, ST)
        s5p = region(3, ST)
        wpool = region(NG, P)
        glast = region(2, ST)
        nhi = region(ST, NSAMP)
        at[0] = 0
        hF = region(FC, T)
        silF = region(3, T)
        at[0] = 0
        qT = region(H, T)
        kT = region(H, T)
        vT = region(DC, T)
        gS = region(DC, T)
        gx = region(H, T)
        bT = region(H, NPROMPT)
        mark = at[0]
        qd = region(H, NPROMPT)
        kd = [region(H, NCH * SUB * (i + 1)) for i in range(NSUB)]
        samp1 = work[:, mark:mark + 2 * H * DV].rearrange("p (a b c) -> p a b c", a=2, b=H)
        gl = work[:, mark:mark + H * T].rearrange("p (a b) -> p a b", a=H)
        qe = region(H, NPROMPT)
        ke = region(H, NPROMPT)
        elast = region(H, NCH)
        attS = region(2, H, CH, rows=CH)
        ketok = region(H * P, rows=CH)
        S = region(H, DV)
        samp0 = region(2, H, DV)
        samp = [samp0, samp1]
        vblk_at = at[0]
        vblk = region(2, 2 * DV, rows=NSAMP)
        ktokS = region(H * P, rows=NSAMP)
        vtokS = region(H * DV, rows=NSAMP)
        egS = region(H, NSAMP)
        gk1 = region(DC, 16)
        gk2 = work[0:16, vblk_at:vblk_at + H * P]
        low = work[0:16, mark:mark + T]
        rms = gx
        assert at[0] <= W - 560 - DC * NE, at[0]
        at[0] = W - 560 - DC * NE
        assert at[0] >= 0
        router = region(DC, NE)
        oT = xn
        vtok = [sq[0:CH, 0:4, :].rearrange("p a b -> p (a b)")[:, 0:H * DV],
                sq[0:CH, 4:8, :].rearrange("p a b -> p (a b)")[:, 0:H * DV]]
        oG = vT
        at[0] = 0
        xtok = region(NRT, D, rows=RT)
        selT = region(NE, T)
        pick = region(NRT, CAP, rows=RT)
        xg = region(DC, CAP)
        silG = region(2, HW)
        hs = region(2, HW)
        hG = region(EC, CAP)
        yS = region(D)
        gslot = region(1)
        sel = region(NE, P, rows=NE)
        mT = region(T, rows=NE)
        posT = region(T, rows=NE)
        onesT = region(T, rows=NE)
        top = region(1, rows=1)
        gbc = region(NE, T)
        hM = region(EC, T)
        silM = region(T)
        gpre = region(T)
        gT = region(T, rows=NE)
        base = region(2, rows=1)
        assert at[0] <= W - 560 - DC * NE, at[0]
        at[0] = W - 560
        rt = region(16, NRT * NE, rows=RT)
        rsc = region(8, NRT, rows=RT)
        rtile = [rt[:, n].rearrange("p (t e) -> p t e", t=NRT) for n in range(16)]
        lg, pr, mx8, ix, gates, oh2, taken, postok, gover = rtile[:9]
        idx = sb("idx", [RT, NRT * 8], U32)
        more = sb("more", [1, 1], mybir.dt.int32)
        ringf = ring[:, :, :].rearrange("p s n -> p (s n)")
        up_slot = [ringf[:, k * 2 * EW:(k + 1) * 2 * EW] for k in range(DC)]
        down_slot = [ringf[:, DC * 2 * EW + f * D:DC * 2 * EW + (f + 1) * D] for f in range(EC)]

        banks = [ctx.enter_context(nc.psum_tensor(f"bank{i}", [P, 512], F32)) for i in range(2)]
        pairs = [ctx.enter_context(nc.psum_tensor(f"pair{i}", [P, 2, 512], F32)) for i in range(3)]

        slot_full = [sem(f"slot_full{s}") for s in range(SLOTS)]
        units_used = sem("units_used")
        x_loaded, s5_loaded, late_loaded = sem("x_loaded"), sem("s5_loaded"), sem("late_loaded")
        cst_loaded = sem("cst_loaded")
        l1_loaded = sem("l1_loaded")
        sel_loaded = sem("sel_loaded")
        x_ready = sem("x_ready")
        sq_ready, ss_ready, std_ready, xn_ready = (sem(n) for n in ("sq_ready", "ss_ready", "std_ready", "xn_ready"))
        dve_link, act_link, pool_link = sem("dve_link"), sem("act_link"), sem("pool_link")
        dense_done = sem("dense_done")
        u_copied = sem("u_copied")
        s5_dt, s5_arg, s5_trig, s5_pow = sem("s5_dt"), sem("s5_arg"), sem("s5_trig"), sem("s5_pow")
        bu_done, bu_rot, rot_ready = sem("bu_done"), sem("bu_rot"), sem("rot_ready")
        scan_done, back_done, y_done, y_out = sem("scan_done"), sem("back_done"), sem("y_done"), sem("y_out")
        hs_ready, ys_done = sem("hs_ready"), sem("ys_done")
        d_ready, pool_out = sem("d_ready"), sem("pool_out")
        z_ready, sig_ready, gated = sem("z_ready"), sem("sig_ready"), sem("gated")
        up_done, sil_done = sem("up_done"), sem("sil_done")
        states_out, pool_states = sem("states_out"), sem("pool_states")
        s5_folded, yp_out = sem("s5_folded"), sem("yp_out")
        s5_states = sem("s5_states")
        low_done, low_copied, gk_done, gx_ready, gl_ready, b_ready = (
            sem(n) for n in ("low_done", "low_copied", "gk_done", "gx_ready", "gl_ready", "b_ready"))
        q_copied = sem("q_copied")
        dec_arg, dec_exp, dec_ready = sem("dec_arg"), sem("dec_exp"), sem("dec_ready")
        zero_att = sem("zero_att")
        vtr_done, vtr_copied, ktr_done, ktr_copied = (sem(n) for n in ("vtr_done", "vtr_copied", "ktr_done", "ktr_copied"))
        att_done, att_copied, o_done, o_copied, kv_done, S_ready = (
            sem(n) for n in ("att_done", "att_copied", "o_done", "o_copied", "kv_done", "S_ready"))
        str_done, str_copied, samp_loaded0, samp_loaded1 = (
            sem(n) for n in ("str_done", "str_copied", "samp_loaded0", "samp_loaded1"))
        samp_loaded = [samp_loaded0, samp_loaded1]
        samp_saved = [sem("samp_saved0"), sem("samp_saved1")]
        vblk_ready, outer_done, samp_ready, so_done, so_copied = (
            sem(n) for n in ("vblk_ready", "outer_done", "samp_ready", "so_done", "so_copied"))
        osq_ready, oss_done, ostd_ready, og_ready = (sem(n) for n in ("osq_ready", "oss_done", "ostd_ready", "og_ready"))
        logit_done, shifted, exped, taken_ready, mtr_done, pos_ready, ptr_done = (
            sem(n) for n in ("logit_done", "shifted", "exped", "taken_ready", "mtr_done", "pos_ready", "ptr_done"))
        xtr_done, xtr_copied, pbc_done, selT_ready, more_ready = (
            sem(n) for n in ("xtr_done", "xtr_copied", "pbc_done", "selT_ready", "more_ready"))
        up_full = [sem(f"up_full{k}") for k in range(DC)]
        down_full = [sem(f"down_full{f}") for f in range(EC)]
        pick_ready, gate_done, gate_copied, gath_done, xg_copied = (
            sem(n) for n in ("pick_ready", "gate_done", "gate_copied", "gath_done", "xg_copied"))
        up_used, silg_done, hs_ready2, tr_done, hT_copied, down_used, y_copied, sc_done = (
            sem(n) for n in ("up_used", "silg_done", "hs_ready2", "tr_done", "hT_copied", "down_used", "y_copied",
                             "sc_done"))
        fb_tr, fb_gT, fb_gbc, fb_copied, fb_full, fb_up, fb_sil, fb_gpre, fb_gated, fb_down, fb_x = (
            sem(n) for n in ("fb_tr", "fb_gT", "fb_gbc", "fb_copied", "fb_full", "fb_up", "fb_sil", "fb_gpre",
                             "fb_gated", "fb_down", "fb_x"))
        y_saved = sem("y_saved")

        def unit_end(n):
            if n < W_GLU:
                return dense_done, 2 * (n + 1)
            if n == W_GLU:
                return dense_done, DENSE_GLU + 4
            if n < FFN_UP:
                return dense_done, DENSE_OUT + 2 * (n - W_OUT_E + 1)
            if n < FFN_DOWN:
                return up_done, n - FFN_UP + 1
            if n < W_IN_O:
                return dense_done, DENSE_DOWN + -(-UT * (n - FFN_DOWN + 1) // FC)
            if n < W_OUT_O:
                return dense_done, DENSE_IN_O + 2 * (n - W_IN_O + 1)
            return dense_done, DENSE_OUT_O + 2 * (n - W_OUT_O + 1)

        def back(i, length):
            return 3 if i >= 3 else i + length - max(x for x in range(length) if x % 3 == i)

        def bc(ap, shape):
            return ap.broadcast_to(shape)

        def tokens(ap, h=None):
            return ap[:, :, 0:NPROMPT]

        powers = sq[:, :, :].rearrange("p a b -> p (a b)")[:, DC * T - 2 * ST * NDBL:
                                                           ].rearrange("p (n x j) -> p n x j", n=NDBL, x=2)

        def rotation_tables(eng, link, steps, lo, hi, scratch):
            cT, sT = cosT[:, lo:hi], sinT[:, lo:hi]
            for i in steps:
                n = 1 << i
                m = min(n, NPROMPT - n)
                c0, s0 = cT[:, :, 0:m], sT[:, :, 0:m]
                A, B = scratch[:, 0, 0:hi - lo, 0:m], scratch[:, 1, 0:hi - lo, 0:m]
                pc, ps = (powers[:, i, x, lo:hi].unsqueeze(2).broadcast_to([P, hi - lo, m]) for x in range(2))
                eng.tensor_tensor(A, c0, pc, ALU.mult)
                link(eng.tensor_tensor(B, s0, ps, ALU.mult))
                link(eng.tensor_tensor(cT[:, :, n:n + m], A, B, ALU.subtract))
                eng.tensor_tensor(A, c0, ps, ALU.mult)
                link(eng.tensor_tensor(B, s0, pc, ALU.mult))
                link(eng.tensor_tensor(sT[:, :, n:n + m], A, B, ALU.add))

        block = ctx.enter_context(nc.Block())

        @block.sync
        def _(sp):
            sp.wait_ge(s5_loaded, 16)
            sp.wait_ge(cst_loaded, 2 * 16)
            sp.wait_ge(x_loaded, 16)
            for n in range(MOE):
                if n >= SLOTS:
                    sp.wait_ge(*unit_end(n - SLOTS))
                sp.dma_start(ring[:, n % SLOTS, :], main_d[n, :, :]).then_inc(slot_full[n % SLOTS], 16)

            def load_up(e, k, done):
                sp.dma_start(up_slot[k], up_d[bass.ds(e * DC + k, 1), :, :].rearrange("o p n -> p (o n)")
                             ).then_inc(done, 16)

            def load_down(e, f, done):
                sp.dma_start(down_slot[f], down_d[bass.ds(e * EC + f, 1), :, :].rearrange("o p n -> p (o n)")
                             ).then_inc(done, 16)

            def wait_main(slot):
                first, last = slot
                sp.wait_ge(*unit_end(max(n for n in range(MOE) if first // UNIT <= n % SLOTS <= (last - 1) // UNIT)))

            for k in range(DC):
                wait_main((k * 2 * EW, (k + 1) * 2 * EW))
                load_up(0, k, up_full[k])
            for f in range(EC):
                wait_main((DC * 2 * EW + f * D, DC * 2 * EW + (f + 1) * D))
                load_down(0, f, down_full[f])
            with sp.Fori(1, NE) as e:
                for k in range(DC):
                    sp.wait_ge(up_used, DC * e + (k + 1 - DC))
                    load_up(e, k, up_full[k])
                for f in range(EC):
                    sp.wait_ge(down_used, EC * e + (f + 1 - EC))
                    load_down(e, f, down_full[f])
            sp.wait_ge(more_ready, 1)
            flag = sp.value_load(more[0:1, 0:1], min_val=0, max_val=1)
            with sp.If(flag):
                def load_all(e):
                    for k in range(DC):
                        load_up(e, k, fb_full)
                    for f in range(EC):
                        load_down(e, f, fb_full)

                sp.wait_ge(fb_gbc, NE)
                load_all(0)
                with sp.Fori(1, NE) as e:
                    sp.wait_ge(fb_down, DC * e)
                    load_all(e)

        @block.gpsimd
        def _(pool):
            links = [0]

            def link(ins):
                links[0] += 1
                ins.then_inc(pool_link, 1)
                pool.wait_ge(pool_link, links[0])

            pool.wait_ge(s5_pow, 1)
            rotation_tables(nc.gpsimd, link, range(DBL0, NDBL), TDVE, ST, tab_scratch[1])
            for j in range(ST):
                pool.wait_ge(scan_done, j + 1)
                if j >= 2:
                    pool.wait_ge(y_done, j - 1)
                g = scanned[:, j % 2]
                nc.gpsimd.tensor_tensor(backC[:, j % 2], g, bc(cosT[:, j:j + 1, :], [P, 2, NPROMPT]), ALU.mult)
                nc.gpsimd.tensor_tensor(backS[:, j % 2], g, bc(sinT[:, j:j + 1, :], [P, 2, NPROMPT]),
                                        ALU.mult).then_inc(back_done, 1)
            pool.wait_ge(s5_states, 1)
            pool.dma_start(s5p_out, glast).then_inc(states_out, 16)
            pool.wait_ge(hs_ready, 1)
            pool.dma_start(s5s_out, hS).then_inc(states_out, 16)
            pool.wait_ge(str_copied, 3)
            for n in range(NSAMP // 2 * H):
                b, h = 2 * (n // H), n % H
                if n >= 2:
                    pool.wait_ge(outer_done, n - 1)
                nc.gpsimd.tensor_tensor(vblk[:, n % 2].rearrange("p (b v) -> p b v", b=2),
                                        bc(vtokS[:, h * DV:(h + 1) * DV].unsqueeze(1), [NSAMP, 2, DV]),
                                        bc(cst[0:NSAMP, C_ID + b:C_ID + b + 2].unsqueeze(2), [NSAMP, 2, DV]),
                                        ALU.mult).then_inc(vblk_ready, 1)
            pool.wait_ge(S_ready, H * NCH)
            pool.dma_start(glap_d, S).then_inc(states_out, 16)
            pool.wait_ge(states_out, 3 * 16)

        @block.scalar
        def _(act):
            links = [0]

            def link(ins):
                links[0] += 1
                ins.then_inc(act_link, 1)
                act.wait_ge(act_link, links[0])

            act.dma_start(s5p, s5p_d).then_inc(s5_loaded, 16)
            act.dma_start(xT[:, :, :], xT_d).then_inc(x_loaded, 16)
            act.dma_start(cst[:, :], cst_d).then_inc(cst_loaded, 16)
            act.dma_start(vecs[:, :], vecs_d).then_inc(cst_loaded, 16)
            act.dma_start(cblk, cblk_d).then_inc(late_loaded, 16)
            act.dma_start(bblk, bblk_d).then_inc(late_loaded, 16)
            act.dma_start(h0, h0_d).then_inc(late_loaded, 16)
            act.dma_start(pbuf[:, :, :, 0:PAST], past_d).then_inc(late_loaded, 16)
            act.dma_start(wpool, wpool_d).then_inc(late_loaded, 16)

            def squares(i, k):
                if i:
                    act.wait_ge(x_ready, 8 * (i - 1) + k + 1)
                nc.scalar.activation(sq[:, k, :], xT[:, k, :], ACT.Square).then_inc(sq_ready, 1)

            def std(i):
                act.wait_ge(ss_ready, i + 1)
                nc.scalar.activation(rstd[:, :], pairs[2][:, 1, 0:T], ACT.Sqrt, scale=1.0 / D,
                                     bias=cst[:, C_EPS:C_EPS + 1]).then_inc(std_ready, 1)

            act.wait_ge(s5_loaded, 16)
            nc.scalar.activation(par[:, 0], s5p[:, 2], ACT.Exp).then_inc(s5_dt, 1)
            act.wait_ge(x_loaded, 16)
            for k in range(DC):
                squares(0, k)
            act.wait_ge(s5_arg, 1)
            nc.scalar.activation(par[:, 3], par[:, 1], ACT.Exp)
            nc.scalar.activation(par[:, 4], par[:, 2], ACT.Sin)
            nc.scalar.activation(par[:, 5], par[:, 6], ACT.Sin).then_inc(s5_trig, 1)
            act.wait_ge(cst_loaded, 2 * 16)
            std(0)

            def copy_u(o):
                act.wait_ge(dense_done, o + 1)
                if o < 4:
                    nc.scalar.copy(ycat[:, 4 + o, :], banks[o % 2][:, 0:T]).then_inc(u_copied, 1)
                else:
                    g = o - 4
                    act.wait_ge(late_loaded, 5 * 16)
                    nc.scalar.copy(upad[:, g, 16:], banks[o % 2][:, 0:NPROMPT])
                    nc.scalar.copy(pbuf[:, g, :, PAST], banks[o % 2][:, NPROMPT:T]).then_inc(u_copied, 1)

            copy_u(0)
            copy_u(1)
            for j in range(ST):
                if j < 6:
                    copy_u(2 + j)
                if j == 6:
                    act.wait_ge(u_copied, 8)
                    act.dma_start(poolp_d, upad[:, :, 16 + NPROMPT - PAST:]).then_inc(pool_states, 16)
                    act.dma_start(pools_d, pbuf[:, :, :, 1:]).then_inc(pool_states, 16)
                if 8 <= j < 12:
                    g = j - 8
                    act.wait_ge(dense_done, 9 + g)
                    nc.scalar.activation(ycat[:, g, :], banks[g % 2][:, 0:T], ACT.Copy,
                                         scale=vecs[:, V_PSCALE + g:V_PSCALE + g + 1]).then_inc(pool_out, 1)
            for c in range(4):
                act.wait_ge(y_out, c + 1)
                nc.scalar.activation(z[:, c, :], z[:, c, :], ACT.Gelu_apprx_tanh).then_inc(z_ready, 1)
            for m in range(4):
                act.wait_ge(dense_done, 13 + m)
                if m >= 2:
                    act.wait_ge(gated, m - 1)
                nc.scalar.activation(sig[:, m % 2, :], banks[m % 2][:, 0:T], ACT.Sigmoid,
                                     bias=vecs[:, V_BGLU + m:V_BGLU + m + 1]).then_inc(sig_ready, 1)
            for k in range(DC):
                squares(1, k)
            std(1)
            act.wait_ge(states_out, 2 * 16)
            act.dma_start(gk1, gk1_d).then_inc(l1_loaded, 16)
            act.dma_start(gk2, gk2_d).then_inc(l1_loaded, 16)
            act.dma_start(router, router_d).then_inc(l1_loaded, 16)
            with act.Fori(0, 2) as r:
                for i in range(SLOTS):
                    act.wait_ge(up_done, SLOTS * r + (i + 1))
                    act.wait_ge(gated, SLOTS * r + (GATED0 + i - back(i, SLOTS) + 1))
                    nc.scalar.activation(silF[:, i % 3, :], pairs[i % 3][:, 0, 0:T], ACT.Silu).then_inc(sil_done, 1)
            for k in range(DC):
                squares(2, k)
            std(2)

            act.wait_ge(low_done, 1)
            nc.scalar.copy(low, pairs[2][0:16, 0, 0:T]).then_inc(low_copied, 1)
            for h in range(H):
                act.wait_ge(gk_done, h + 1)
                nc.scalar.activation(gx[:, h, :], pairs[h % 2][:, 0, 0:T], ACT.Identity,
                                     bias=vecs[:, V_BGK + h:V_BGK + h + 1]).then_inc(gx_ready, 1)
            act.wait_ge(gx_ready, H)
            link(nc.scalar.activation(gl, gx, ACT.Abs))
            link(nc.scalar.activation(gl, gl, ACT.Exp, scale=-1.0))
            nc.scalar.activation(gl, gl, ACT.Ln, bias=1.0).then_inc(gl_ready, 1)
            DB = DENSE_IN_O
            for o in range(16):
                act.wait_ge(dense_done, DB + o + 1)
                b = banks[(DB + o) % 2][:, 0:T]
                if o < 4:
                    nc.scalar.mul(qT[:, o, :], b, float(P) ** -0.5).then_inc(q_copied, 1)
                elif o < 8:
                    nc.scalar.copy(kT[:, o - 4, :], b).then_inc(q_copied, 1)
                else:
                    nc.scalar.copy(vT[:, o - 8, :], b).then_inc(q_copied, 1)
            for n, t in enumerate([qd] + kd):
                act.wait_ge(dec_arg, n + 1)
                nc.scalar.activation(t, t, ACT.Exp).then_inc(dec_exp, 1)
            nc.scalar.activation(qe, bT, ACT.Exp).then_inc(dec_exp, 1)
            act.wait_ge(dec_arg, 6)
            nc.scalar.activation(ke, ke, ACT.Exp).then_inc(dec_exp, 1)
            act.wait_ge(dec_arg, 7)
            nc.scalar.activation(elast, elast, ACT.Exp).then_inc(dec_exp, 1)
            nc.scalar.activation(egS, gx[:, :, NPROMPT:T], ACT.Exp).then_inc(dec_exp, 1)
            for o in range(16, 24):
                act.wait_ge(dense_done, DB + o + 1)
                nc.scalar.activation(gS[:, o - 16, :], banks[(DB + o) % 2][:, 0:T], ACT.Silu).then_inc(q_copied, 1)
            act.dma_start(samp[0], sgla_d[:, 0:2]).then_inc(samp_loaded[0], 16)
            for c in range(NCH):
                act.wait_ge(vtr_done, c + 1)
                if c >= 2:
                    act.wait_ge(kv_done, 2 * (c - 1))
                for u in range(2):
                    last = nc.scalar.copy(vtok[c % 2][:, u * 512:(u + 1) * 512], pairs[0][0:CH, u, :])
                last.then_inc(vtr_copied, 1)
                act.wait_ge(o_done, c + 1)
                for u in range(2):
                    last = nc.scalar.copy(oT[:, 4 * u:4 * u + 4, c * CH:(c + 1) * CH],
                                          pairs[1][:, u, 0:4 * CH].rearrange("p (a b) -> p a b", a=4))
                last.then_inc(o_copied, 1)
            act.wait_ge(str_done, 3)
            nc.scalar.copy(ktokS, pairs[0][0:NSAMP, 0, :]).then_inc(str_copied, 1)
            nc.scalar.copy(vtokS[:, 0:512], pairs[0][0:NSAMP, 1, :]).then_inc(str_copied, 1)
            nc.scalar.copy(vtokS[:, 512:1024], pairs[1][0:NSAMP, 0, :]).then_inc(str_copied, 1)
            def load_pair(p):
                act.dma_start(samp[p % 2], sgla_d[:, 2 * p:2 * p + 2]).then_inc(samp_loaded[p % 2], 16)

            act.wait_ge(att_done, NSUB * NCH)
            load_pair(1)
            for p in range(NSAMP // 2):
                act.wait_ge(samp_ready, H * (p + 1))
                act.dma_start(glas_d[:, 2 * p:2 * p + 2], samp[p % 2]).then_inc(samp_saved[p % 2], 16)
                if p + 2 < NSAMP // 2:
                    act.wait_ge(so_done, p + 1)
                    act.wait_ge(samp_saved[p % 2], 16)
                    load_pair(p + 2)
            act.wait_ge(so_done, NSAMP // 2)
            nc.scalar.copy(oT[:, :, NPROMPT:T],
                           pairs[1][:, 1, 0:DC * NSAMP].rearrange("p (b a) -> p a b", a=DC)).then_inc(so_copied, 1)
            act.wait_ge(so_copied, 1)
            act.wait_ge(o_copied, NCH)
            for k in range(DC):
                nc.scalar.activation(sq[:, k, :], oT[:, k, :], ACT.Square).then_inc(osq_ready, 1)
            for h in range(H):
                act.wait_ge(oss_done, h + 1)
                nc.scalar.activation(rms[:, h, :], pairs[h % 2][:, 0, 0:T], ACT.Sqrt, scale=1.0 / DV,
                                     bias=cst[:, C_EPS:C_EPS + 1]).then_inc(ostd_ready, 1)
            for k in range(DC):
                squares(3, k)
            std(3)
            for b in (0, 1):
                act.wait_ge(samp_saved[b], 16 * NSAMP // 4)
            act.wait_ge(states_out, 3 * 16)
            act.dma_start(sel, sel_d).then_inc(sel_loaded, 16)
            for t in range(NRT):
                act.wait_ge(xtr_done, t + 1)
                for u in range(2):
                    last = nc.scalar.copy(xtok[:, t, u * 512:(u + 1) * 512], pairs[t % 2][0:RT, u, :])
                last.then_inc(xtr_copied, 1)
                if t == 0:
                    act.wait_ge(shifted, 1)
                    nc.scalar.activation(lg, lg, ACT.Exp).then_inc(exped, 1)
            def copy_tokens(e):
                for u in range(2):
                    act.wait_ge(gath_done, 2 * e + (u + 1))
                    nc.scalar.copy(xg[:, 4 * u:4 * u + 4, :],
                                   banks[u][:, :].rearrange("p (a b) -> p a b", a=4)).then_inc(xg_copied, 1)

            def silu_and_transposes(e):
                act.wait_ge(up_used, DC * e + DC)
                nc.scalar.activation(silG, pairs[0][:, :, 0:HW], ACT.Silu).then_inc(silg_done, 1)
                for u in range(2):
                    n = 4 if u == 0 else EC - 4
                    act.wait_ge(tr_done, 2 * e + (u + 1))
                    nc.scalar.copy(hG[:, 4 * u:4 * u + n, :],
                                   banks[u][:, 0:n * CAP].rearrange("p (a b) -> p a b", a=n)).then_inc(hT_copied, 1)

            def copy_output(e):
                act.wait_ge(down_used, EC * e + EC)
                for u in range(2):
                    nc.scalar.copy(yS[:, u * 512:(u + 1) * 512], pairs[2][:, u, :]).then_inc(y_copied, 1)

            copy_tokens(0)
            silu_and_transposes(0)
            copy_tokens(1)
            copy_output(0)
            with act.Fori(1, NE - 1) as e:
                silu_and_transposes(e)
                copy_tokens(e + 1)
                copy_output(e)
            silu_and_transposes(NE - 1)
            copy_output(NE - 1)
            act.wait_ge(more_ready, 1)
            flag = act.value_load(more[0:1, 0:1], min_val=0, max_val=1)
            with act.If(flag):
                act.wait_ge(fb_tr, 1)
                nc.scalar.copy(gT, banks[1][0:NE, 0:T]).then_inc(fb_gT, 1)
                for e in range(NE):
                    act.wait_ge(fb_gbc, e + 1)
                    nc.scalar.copy(gbc[:, e, :], pairs[1][:, e % 2, 0:T]).then_inc(fb_copied, 1)
                with act.Fori(0, NE) as e:
                    for i in range(EC):
                        act.wait_ge(fb_up, EC * e + (i + 1))
                        nc.scalar.activation(silM, pairs[0][:, 0, 0:T], ACT.Silu).then_inc(fb_sil, 1)
                act.wait_ge(fb_x, 1 + NE * DC)
            for k in range(DC):
                act.wait_ge(x_ready, 8 * (3 + NE) + k + 1 - 8 + 0)
                nc.scalar.activation(sq[:, k, :], xT[:, k, :], ACT.Square).then_inc(sq_ready, 1)
            std(4)
            for k in range(DC):
                act.wait_ge(xn_ready, 8 * 4 + k + 1)
                act.dma_start(yT_d[:, k, :], xn[:, k, :]).then_inc(y_saved, 16)
            for s in (0, 1):
                act.wait_ge(samp_saved[s], 16 * NSAMP // 4)
            act.wait_ge(pool_states, 2 * 16)
            act.wait_ge(y_saved, 16 * DC)

        @block.vector
        def _(dve):
            links = [0]

            def link(ins):
                links[0] += 1
                ins.then_inc(dve_link, 1)
                dve.wait_ge(dve_link, links[0])

            v = nc.vector
            scr = sq[:, :, :].rearrange("p a b -> p (a b)")

            def normalize(i):
                dve.wait_ge(std_ready, i + 1)
                link(v.reciprocal(rstd[:, :], rstd[:, :]))
                for k in range(DC):
                    w = V_NORM[i] + k
                    v.scalar_tensor_tensor(xn[:, k, :], xT[:, k, :], vecs[:, w:w + 1], rstd[:, :],
                                           ALU.mult, ALU.mult).then_inc(xn_ready, 1)

            def residual(first):
                for m in range(DC):
                    dve.wait_ge(dense_done, first + m + 1)
                    v.tensor_tensor(xT[:, m, :], xT[:, m, :], banks[m % 2][:, 0:T], ALU.add).then_inc(x_ready, 1)

            (dt, ardt, ang, mag, sn, cs, carg, lbr, lbi, fr, fi, pc, ps, t0, t1, t2, t3, t4) = (
                par[:, n] for n in range(18))
            are, aim = s5p[:, 0], s5p[:, 1]
            dve.wait_ge(s5_loaded, 16)
            dve.wait_ge(s5_dt, 1)
            v.tensor_tensor(ardt, are, dt, ALU.mult)
            link(v.tensor_tensor(ang, aim, dt, ALU.mult))
            link(v.tensor_scalar(t0, ang, 1.0 / TWO_PI, ROUND, ALU.mult, ALU.add))
            link(v.tensor_scalar(t0, t0, -ROUND, None, ALU.add))
            for part in (PI_1, PI_2, PI_3):
                link(v.scalar_tensor_tensor(ang, t0, -part, ang, ALU.mult, ALU.add))
            link(v.tensor_scalar(ang, ang, math.pi - 1e-6, -math.pi + 1e-6, ALU.min, ALU.max))
            link(v.scalar_tensor_tensor(t1, ang, -1.0, ang, ALU.mult, ALU.max))
            v.tensor_scalar(carg, t1, -1.0, math.pi / 2, ALU.mult, ALU.add).then_inc(s5_arg, 1)
            v.memset(upad[:, :, 0:16], 0.0)
            dve.wait_ge(cst_loaded, 2 * 16)
            normalize(0)
            dve.wait_ge(s5_trig, 1)
            v.tensor_tensor(lbr, mag, cs, ALU.mult)
            v.tensor_tensor(lbi, mag, sn, ALU.mult)
            v.tensor_tensor(t1, are, are, ALU.mult)
            link(v.tensor_tensor(t2, aim, aim, ALU.mult))
            link(v.tensor_tensor(t1, t1, t2, ALU.add))
            link(v.reciprocal(t1, t1))
            link(v.tensor_scalar(t0, lbr, -1.0, None, ALU.add))
            v.tensor_tensor(fr, t0, are, ALU.mult)
            v.tensor_tensor(t3, lbi, aim, ALU.mult)
            v.tensor_tensor(fi, lbi, are, ALU.mult)
            link(v.tensor_tensor(t4, t0, aim, ALU.mult))
            v.tensor_tensor(fr, fr, t3, ALU.add)
            link(v.tensor_tensor(fi, fi, t4, ALU.subtract))
            v.tensor_tensor(fr, fr, t1, ALU.mult)
            v.tensor_tensor(fi, fi, t1, ALU.mult)
            v.memset(cosT[:, :, 0:1], 1.0)
            v.memset(sinT[:, :, 0:1], 0.0)
            v.tensor_copy(powers[:, 0, 0], cs)
            link(v.tensor_copy(powers[:, 0, 1], sn))
            for i in range(1, NDBL):
                pc, ps = powers[:, i - 1, 0], powers[:, i - 1, 1]
                v.tensor_tensor(t0, pc, pc, ALU.mult)
                v.tensor_tensor(t2, ps, ps, ALU.mult)
                link(v.scalar_tensor_tensor(powers[:, i, 1], pc, 2.0, ps, ALU.mult, ALU.mult))
                link(v.tensor_tensor(powers[:, i, 0], t0, t2, ALU.subtract))
            rotation_tables(nc.vector, link, range(DBL0), 0, ST, tab_scratch[2])
            v.memset(t4, 0.0).then_inc(s5_pow, 1)
            rotation_tables(nc.vector, link, range(DBL0, NDBL), 0, TDVE, tab_scratch[0])
            dve.wait_ge(late_loaded, 5 * 16)
            cr, ci = cblk[:, 0], cblk[:, 1]
            frb, fib = bc(fr.unsqueeze(2), [P, ST, 32]), bc(fi.unsqueeze(2), [P, ST, 32])
            w0 = scr[:, 0:512].rearrange("p (a b) -> p a b", a=ST)
            w1 = scr[:, 512:1024].rearrange("p (a b) -> p a b", a=ST)
            v.tensor_tensor(w0, cr, frb, ALU.mult)
            link(v.tensor_tensor(w1, ci, fib, ALU.mult))
            v.tensor_tensor(cf[:, 0], w0, w1, ALU.subtract)
            link(v.tensor_tensor(cf[:, 1], w1, w0, ALU.subtract))
            v.tensor_tensor(w0, cr, fib, ALU.mult)
            link(v.tensor_tensor(w1, ci, frb, ALU.mult))
            link(v.tensor_tensor(w0, w0, w1, ALU.add))
            v.tensor_scalar(cf[:, 2], w0, -1.0, None, ALU.mult).then_inc(s5_folded, 1)
            dve.wait_ge(s5_folded, 1)

            def windows():
                dve.wait_ge(u_copied, 8)
                cnt = cst[:, C_CNT:C_CNT + 64].rearrange("p (g t) -> p g t", g=NG)
                L = 16 + NPROMPT
                cur = upad
                bufs = [xn[:, :, :].rearrange("p a b -> p (a b)")[:, 0:4 * L].rearrange("p (g t) -> p g t", g=4),
                        scr[:, 4 * NPROMPT:4 * NPROMPT + 3 * L].rearrange("p (g t) -> p g t", g=3)]
                for g in range(NG):
                    w = 1 << g
                    new = bufs[0][:, g:4, :] if g % 2 == 0 else bufs[1][:, g - 1:3, :]
                    old = cur[:, 1:, :] if g else upad
                    s0 = 2 * w - 1
                    link(v.tensor_tensor(new[:, :, s0:], old[:, :, s0:], old[:, :, s0 - w:L - w], ALU.add))
                    link(v.tensor_scalar(ycat[:, g, 0:NPROMPT], new[:, 0, 16:], 1.0 / (2 * w), None, ALU.mult))
                    link(v.tensor_tensor(ycat[:, g, 0:16], new[:, 0, 16:32], cnt[:, g, :], ALU.mult))
                    link(v.tensor_tensor(ycat[:, g, 0:NPROMPT], ycat[:, g, 0:NPROMPT], upad[:, g, 16:],
                                         ALU.subtract))
                    link(v.tensor_reduce(t4[:, 0:NSAMP], pbuf[:, g, :, 16 - 2 * w:], AX.X, ALU.add))
                    v.scalar_tensor_tensor(ycat[:, g, NPROMPT:T], t4[:, 0:NSAMP], 1.0 / (2 * w), pbuf[:, g, :, PAST],
                                           ALU.mult, ALU.subtract).then_inc(d_ready, 1)
                    cur = new

            def skip(c):
                dve.wait_ge(y_done, 4 * c + 4)
                if c == 0:
                    dve.wait_ge(pool_states, 2 * 16)
                v.scalar_tensor_tensor(z[:, c, 0:NPROMPT], ycat[:, 4 + c, 0:NPROMPT], vecs[:, V_D + c:V_D + c + 1],
                                       pairs[2][:, c % 2, 0:NPROMPT], ALU.mult, ALU.add).then_inc(yp_out, 1)

            def scan(j):
                if j >= 2:
                    dve.wait_ge(back_done, j - 1)
                dve.wait_ge(rot_ready, j + 1)
                g = scanned[:, j % 2]
                m = bc(mag[:, j:j + 1], [P, NPROMPT])
                v.tensor_tensor_scan(g[:, 0], m, rotA[:, j % 2, 0], 0.0, ALU.mult, ALU.add)
                v.tensor_tensor_scan(g[:, 1], m, rotA[:, j % 2, 1], 0.0, ALU.mult, ALU.add).then_inc(scan_done, 1)

            def last_state(j):
                dve.wait_ge(scan_done, j + 1)
                v.tensor_copy(glast[:, :, j:j + 1], scanned[:, j % 2, :, NPROMPT - 1:])

            for j in range(ST):
                if j == TDVE:
                    dve.wait_ge(pool_link, 4 * (NDBL - DBL0))
                dve.wait_ge(bu_done, j + 1)
                src = pairs[j % 2][:, :, 0:NPROMPT]
                A, B = rotA[:, j % 2], rotB[:, j % 2]
                v.tensor_copy(buS[:, :, j, :], pairs[j % 2][:, :, NPROMPT:T])
                v.tensor_tensor(A, src, bc(cosT[:, j:j + 1, :], [P, 2, NPROMPT]), ALU.mult)
                v.tensor_tensor(B, src, bc(sinT[:, j:j + 1, :], [P, 2, NPROMPT]), ALU.mult).then_inc(bu_rot, 1)
                if j:
                    scan(j - 1)
                dve.wait_ge(bu_rot, j + 1)
                v.tensor_tensor(A[:, 0], A[:, 0], B[:, 1], ALU.add)
                v.tensor_tensor(A[:, 1], A[:, 1], B[:, 0], ALU.subtract).then_inc(rot_ready, 1)
                if j:
                    last_state(j - 1)
                if j == 6:
                    windows()
                if j % 4 == 1 and j >= 9:
                    skip(j // 4 - 2)
            scan(ST - 1)
            last_state(ST - 1)
            skip(2)
            skip(3)
            shp = [P, ST, NSAMP]
            q = [scr[:, 128 * n:128 * n + 128].rearrange("p (a b) -> p a b", a=ST) for n in range(8)]

            def wide(a):
                return bc(a.unsqueeze(2), shp)

            v.tensor_tensor(q[0], h0[:, 0], wide(lbr), ALU.mult)
            v.tensor_tensor(q[1], h0[:, 1], wide(lbi), ALU.mult)
            v.tensor_tensor(q[2], buS[:, 0], wide(fr), ALU.mult)
            v.tensor_tensor(q[3], buS[:, 1], wide(fi), ALU.mult)
            v.tensor_tensor(q[4], h0[:, 1], wide(lbr), ALU.mult)
            v.tensor_tensor(q[5], h0[:, 0], wide(lbi), ALU.mult)
            v.tensor_tensor(q[6], buS[:, 1], wide(fr), ALU.mult)
            link(v.tensor_tensor(q[7], buS[:, 0], wide(fi), ALU.mult))
            v.tensor_tensor(q[0], q[0], q[1], ALU.subtract)
            v.tensor_tensor(q[2], q[2], q[3], ALU.subtract)
            v.tensor_tensor(q[4], q[4], q[5], ALU.add)
            link(v.tensor_tensor(q[6], q[6], q[7], ALU.add))
            v.tensor_tensor(hS[:, 0], q[0], q[2], ALU.add)
            link(v.tensor_tensor(hS[:, 1], q[4], q[6], ALU.add))
            v.tensor_scalar(nhi, hS[:, 1], -1.0, None, ALU.mult).then_inc(hs_ready, 1)
            cL, sL = cosT[:, :, NPROMPT - 1], sinT[:, :, NPROMPT - 1]

            def times(a, b):
                v.tensor_tensor(t0, glast[:, 0], a, ALU.mult)
                v.tensor_tensor(t1, glast[:, 1], b, ALU.mult)
                v.tensor_tensor(t2, glast[:, 0], b, ALU.mult)
                link(v.tensor_tensor(t3, glast[:, 1], a, ALU.mult))
                v.tensor_tensor(glast[:, 0], t0, t1, ALU.subtract)
                return v.tensor_tensor(glast[:, 1], t2, t3, ALU.add)

            link(times(cL, sL))
            times(fr, fi).then_inc(s5_states, 1)
            dve.wait_ge(ys_done, 1)
            for c in range(4):
                v.scalar_tensor_tensor(z[:, c, NPROMPT:T], ycat[:, 4 + c, NPROMPT:T], vecs[:, V_D + c:V_D + c + 1],
                                       pairs[0][:, 0, c * NSAMP:(c + 1) * NSAMP], ALU.mult, ALU.add
                                       ).then_inc(y_out, 1)
            for m in range(4):
                dve.wait_ge(sig_ready, m + 1)
                v.tensor_tensor(ycat[:, 4 + m, :], z[:, m, :], sig[:, m % 2, :], ALU.mult).then_inc(gated, 1)
            residual(DENSE_OUT)
            normalize(1)
            with dve.Fori(0, 2) as r:
                for i in range(SLOTS):
                    dve.wait_ge(sil_done, SLOTS * r + (i + 1))
                    v.tensor_tensor(hF[:, bass.ds(SLOTS * r + i, 1), :].rearrange("p a b -> p (a b)"),
                                    silF[:, i % 3, :], pairs[i % 3][:, 1, 0:T], ALU.mult).then_inc(gated, 1)
            residual(DENSE_DOWN)
            normalize(2)

            v.memset(attS, 0.0)
            dve.wait_ge(gl_ready, 1)
            link(v.scalar_tensor_tensor(gx, gx, 0.0, gl, ALU.min, ALU.subtract))
            link(v.tensor_scalar(gx, gx, 1.0 / 16.0, None, ALU.mult))
            for h in range(H):
                last = v.tensor_tensor_scan(bT[:, h, :], cst[:, C_RESET:C_RESET + NPROMPT], gx[:, h, 0:NPROMPT], 0.0,
                                            ALU.mult, ALU.add)
            link(last)
            b_sub = bT.rearrange("p h (n s) -> p (h n) s", s=SUB)
            b_ch = bT.rearrange("p h (n s) -> p (h n) s", s=CH)
            HN = H * NCH
            v.tensor_tensor(qd.rearrange("p h (n s) -> p (h n) s", s=SUB), b_sub,
                            bc(b_sub[:, :, MID:MID + 1], [P, HN * NSUB, SUB]), ALU.subtract).then_inc(dec_arg, 1)
            for i in range(NSUB):
                w = SUB * (i + 1)
                r = SUB * i + MID
                v.tensor_tensor(kd[i].rearrange("p h (n s) -> p (h n) s", s=w), bc(b_ch[:, :, r:r + 1], [P, HN, w]),
                                b_ch[:, :, 0:w], ALU.subtract).then_inc(dec_arg, 1)
            v.tensor_tensor(ke.rearrange("p h (n s) -> p (h n) s", s=CH), bc(b_ch[:, :, CH - 1:CH], [P, HN, CH]),
                            b_ch, ALU.subtract).then_inc(dec_arg, 1)
            v.tensor_copy(elast.rearrange("p h n -> p (h n)").unsqueeze(2), b_ch[:, :, CH - 1:CH]).then_inc(dec_arg, 1)
            k4 = kT[:, :, 0:NPROMPT].rearrange("p h (n s) -> p h n s", s=CH)
            dve.wait_ge(q_copied, 8)
            dve.wait_ge(dec_exp, 1)
            v.tensor_tensor(qd, qd, qT[:, :, 0:NPROMPT], ALU.mult).then_inc(dec_ready, 1)
            for i in range(NSUB):
                w = SUB * (i + 1)
                dve.wait_ge(dec_exp, i + 2)
                k3 = kd[i].rearrange("p h (n s) -> p h n s", s=w)
                v.tensor_tensor(k3, k3, k4[:, :, :, 0:w], ALU.mult).then_inc(dec_ready, 1)
            dve.wait_ge(dec_exp, 6)
            v.tensor_tensor(qe, qe, qT[:, :, 0:NPROMPT], ALU.mult).then_inc(dec_ready, 1)
            dve.wait_ge(dec_exp, 7)
            v.tensor_tensor(ke, ke, kT[:, :, 0:NPROMPT], ALU.mult).then_inc(dec_ready, 1)
            dve.wait_ge(dec_exp, 8)
            for c in range(NCH):
                if c >= 2:
                    dve.wait_ge(o_done, c - 1)
                dve.wait_ge(att_done, NSUB * (c + 1))
                for i in range(NSUB):
                    w = SUB * (i + 1)
                    a = pairs[2][0:w, 1, 0:H * CH].rearrange("p (h t) -> p h t", h=H)[:, :, SUB * i:w]
                    m = bc(cst[0:w, C_MASK + SUB * i:C_MASK + w].unsqueeze(1), [w, H, SUB])
                    v.tensor_tensor(attS[0:w, c % 2, :, SUB * i:w], a, m, ALU.mult).then_inc(att_copied, 1)
                dve.wait_ge(ktr_done, c + 1)
                if c:
                    dve.wait_ge(kv_done, 2 * c)
                v.tensor_copy(ketok, pairs[2][0:CH, 0, :]).then_inc(ktr_copied, 1)
                for h in range(H):
                    dve.wait_ge(kv_done, 2 * c + h // 2 + 1)
                    kv = banks[h // 2][:, (h % 2) * DV:(h % 2 + 1) * DV]
                    if c == 0:
                        v.tensor_copy(S[:, h, :], kv).then_inc(S_ready, 1)
                    else:
                        if h == 0:
                            dve.wait_ge(S_ready, H * c)
                        v.scalar_tensor_tensor(S[:, h, :], S[:, h, :], elast[:, h, c:c + 1], kv,
                                               ALU.mult, ALU.add).then_inc(S_ready, 1)
            dve.wait_ge(dec_exp, 9)
            for n in range(NSAMP // 2 * H):
                p, h = n // H, n % H
                if h == 0:
                    dve.wait_ge(samp_loaded[p % 2], 16 * (p // 2 + 1))
                dve.wait_ge(outer_done, n + 1)
                for s in range(2):
                    b = 2 * p + s
                    last = v.scalar_tensor_tensor(samp[p % 2][:, s, h, :], samp[p % 2][:, s, h, :], egS[:, h, b:b + 1],
                                                  banks[n % 2][:, s * DV:(s + 1) * DV], ALU.mult, ALU.add)
                last.then_inc(samp_ready, 1)
            for h in range(H):
                dve.wait_ge(ostd_ready, h + 1)
                link(v.reciprocal(rms[:, h, :], rms[:, h, :]))
                for c in range(VC):
                    last = v.scalar_tensor_tensor(oG[:, VC * h + c, :], oT[:, VC * h + c, :],
                                                  vecs[:, V_GNORM + c:V_GNORM + c + 1], rms[:, h, :],
                                                  ALU.mult, ALU.mult)
                link(last)
                dve.wait_ge(q_copied, 24)
                v.tensor_tensor(oG[:, VC * h:VC * h + VC, :], oG[:, VC * h:VC * h + VC, :],
                                gS[:, VC * h:VC * h + VC, :], ALU.mult).then_inc(og_ready, 1)
            residual(DENSE_OUT_O)
            normalize(3)
            shp = [RT, NRT, NE]
            mx, sm, den = (rsc[:, n] for n in range(3))
            iota = bc(cst[0:RT, C_IOTA:C_IOTA + NE].unsqueeze(1), shp)
            own = bc(cst[0:RT, C_OWN:C_OWN + NRT].unsqueeze(2), shp)
            for b in (0, 1):
                dve.wait_ge(samp_saved[b], 16 * NSAMP // 4)
            dve.wait_ge(states_out, 3 * 16)
            v.memset(onesT, 1.0)
            dve.wait_ge(logit_done, 1)
            lp = banks[0][0:RT, 0:NRT * NE].rearrange("p (t e) -> p t e", t=NRT)
            link(v.tensor_reduce(mx, lp, AX.X, ALU.max))
            v.tensor_tensor(lg, lp, bc(mx.unsqueeze(2), shp), ALU.subtract).then_inc(shifted, 1)
            dve.wait_ge(exped, 1)
            link(v.tensor_reduce(sm, lg, AX.X, ALU.add))
            link(v.reciprocal(sm, sm))
            link(v.tensor_tensor(pr, lg, bc(sm.unsqueeze(2), shp), ALU.mult))
            for t in range(NRT):
                last = v.max(mx8[:, t, :], pr[:, t, :])
            link(last)
            for t in range(NRT):
                last = v.max_index(idx[:, t * 8:(t + 1) * 8], mx8[:, t, :], pr[:, t, :])
            link(last)
            link(v.tensor_copy(ix.rearrange("p t e -> p (t e)"), idx[:, :]))
            v.tensor_tensor(gates, iota, bc(ix[:, :, 0:1], shp), ALU.is_equal)
            link(v.tensor_tensor(oh2, iota, bc(ix[:, :, 1:2], shp), ALU.is_equal))
            v.tensor_tensor(taken, gates, oh2, ALU.add).then_inc(taken_ready, 1)
            link(v.tensor_tensor(den, mx8[:, :, 0], mx8[:, :, 1], ALU.add))
            link(v.reciprocal(den, den))
            v.tensor_tensor(gates, gates, bc(mx8[:, :, 0:1], shp), ALU.mult)
            link(v.tensor_tensor(oh2, oh2, bc(mx8[:, :, 1:2], shp), ALU.mult))
            link(v.tensor_tensor(gates, gates, oh2, ALU.add))
            link(v.tensor_tensor(gates, gates, bc(den.unsqueeze(2), shp), ALU.mult))
            dve.wait_ge(mtr_done, 1)
            link(v.tensor_copy(mT, banks[1][0:NE, 0:T]))
            link(v.tensor_tensor_scan(posT, onesT, mT, 0.0, ALU.mult, ALU.add))
            link(v.tensor_tensor(mT, mT, posT, ALU.mult))
            v.tensor_scalar(mT, mT, -1.0, None, ALU.add).then_inc(pos_ready, 1)
            dve.wait_ge(ptr_done, 1)
            link(v.tensor_scalar(postok, banks[0][0:RT, 0:NRT * NE].rearrange("p (t e) -> p t e", t=NRT),
                                 1.0, None, ALU.add))
            link(v.tensor_tensor(postok, postok, own, ALU.mult))
            link(v.tensor_scalar(postok, postok, -1.0, None, ALU.add))
            link(v.tensor_reduce(top, banks[0][0:1, 64:64 + NE], AX.X, ALU.max))
            link(v.tensor_scalar(top, top, float(CAP), None, ALU.is_gt))
            v.tensor_copy(more[0:1, 0:1], top).then_inc(more_ready, 1)
            link(v.tensor_scalar(gover, postok, float(CAP), None, ALU.is_ge))
            link(v.tensor_tensor(gover, gover, gates, ALU.mult))

            def make_pick(e):
                v.tensor_tensor(pick, bc(cst[0:RT, C_IOTA:C_IOTA + CAP].unsqueeze(1), [RT, NRT, CAP]),
                                bc(postok[:, :, bass.ds(e, 1)], [RT, NRT, CAP]), ALU.is_equal).then_inc(pick_ready, 1)

            def copy_gates(e):
                dve.wait_ge(gate_done, e + 1)
                v.tensor_copy(gslot, pairs[2][:, 0, 0:1]).then_inc(gate_copied, 1)

            def hidden(e):
                dve.wait_ge(gate_copied, e + 1)
                dve.wait_ge(silg_done, e + 1)
                v.scalar_tensor_tensor(hs, pairs[1][:, :, 0:HW], gslot[:, 0:1], silG, ALU.mult, ALU.mult
                                       ).then_inc(hs_ready2, 1)

            def add_output(e):
                for m in range(DC):
                    dve.wait_ge(sc_done, DC * e + (m + 1))
                    v.tensor_tensor(xT[:, m, :], xT[:, m, :], banks[m % 2][:, 0:T], ALU.add).then_inc(x_ready, 1)

            make_pick(0)
            for e in range(NE):
                dve.wait_ge(pbc_done, e + 1)
                v.tensor_scalar(selT[:, e, :], pairs[2][:, e % 2, 0:T], cst[:, C_SLOT:C_SLOT + 1], None,
                                ALU.is_equal).then_inc(selT_ready, 1)
            copy_gates(0)
            hidden(0)
            dve.wait_ge(gath_done, 2)
            make_pick(1)
            copy_gates(1)
            with dve.Fori(1, NE - 1) as e:
                hidden(e)
                dve.wait_ge(gath_done, 2 * e + 2)
                make_pick(e + 1)
                add_output(e - 1)
                copy_gates(e + 1)
            hidden(NE - 1)
            add_output(NE - 2)
            add_output(NE - 1)
            flag = dve.value_load(more[0:1, 0:1], min_val=0, max_val=1)
            with dve.If(flag):
                v.memset(base[:, 0:1], 0.0).then_inc(fb_gated, 1)
                v.memset(base[:, 1:2], 0.0).then_inc(fb_x, 1)
                dve.wait_ge(fb_copied, NE)
                with dve.Fori(0, NE) as e:
                    for i in range(EC):
                        dve.wait_ge(fb_sil, EC * e + (i + 1))
                        v.tensor_tensor(gpre, silM, pairs[0][:, 1, 0:T], ALU.mult).then_inc(fb_gpre, 1)
                        dve.wait_ge(fb_gpre, EC * e + (i + 1))
                        v.tensor_tensor(hM[:, i, :], gpre, gbc[:, bass.ds(e, 1), :].rearrange("p a b -> p (a b)"),
                                        ALU.mult).then_inc(fb_gated, 1)
                    for m in range(DC):
                        dve.wait_ge(fb_down, DC * e + (m + 1))
                        v.tensor_tensor(xT[:, m, :], xT[:, m, :], banks[m % 2][:, 0:T], ALU.add).then_inc(fb_x, 1)
            normalize(4)

        @block.tensor
        def _(pe):
            mm = nc.tensor.matmul

            def slot(n):
                return ring[:, n % SLOTS, :].rearrange("p (t m) -> p t m", m=P)

            def unit_loaded(n):
                pe.wait_ge(slot_full[n % SLOTS], 16 * (n // SLOTS + 1))

            def bank_free(d):
                if d < 2:
                    return
                if d < DENSE_POOL + 2:
                    pe.wait_ge(u_copied, d - 1)
                elif d < DENSE_GLU + 2:
                    pe.wait_ge(pool_out, d - DENSE_POOL - 1)
                elif d < DENSE_OUT + 2:
                    pe.wait_ge(sig_ready, d - DENSE_GLU - 1)
                elif d < DENSE_IN_O + 2:
                    pe.wait_ge(x_ready, d - DENSE_OUT - 1)
                elif d < DENSE_OUT_O + 2:
                    pe.wait_ge(q_copied, d - DENSE_IN_O - 1)
                else:
                    pe.wait_ge(x_ready, d - DENSE_OUT_O - 1 + 16)

            def dense(d, unit, tile, kc, rhs, ready=None):
                bank_free(d)
                for k in range(kc):
                    n = unit + (tile + k) // UT
                    if k == 0 or (tile + k) % UT == 0:
                        unit_loaded(n)
                    if ready is not None:
                        pe.wait_ge(ready[0], ready[1] + k + 1)
                    last = mm(banks[d % 2][:, 0:T], slot(n)[:, (tile + k) % UT, :], rhs[:, k, :],
                              start=(k == 0), stop=(k == kc - 1))
                last.then_inc(dense_done, 1)

            def sum_squares(i):
                for k in range(DC):
                    pe.wait_ge(sq_ready, DC * i + k + 1)
                    last = mm(pairs[2][:, 1, 0:T], ones, sq[:, k, :], start=(k == 0), stop=(k == DC - 1))
                last.then_inc(ss_ready, 1)

            pe.wait_ge(cst_loaded, 2 * 16)
            sum_squares(0)

            def project_in(o):
                dense(o, W_IN_E, DC * o, DC, xn, (xn_ready, 0) if o == 0 else None)

            project_in(0)
            project_in(1)
            pe.wait_ge(late_loaded, 5 * 16)

            def y_tile(j):
                c, r = j // 4, 32 * (j % 4)
                if j == 0:
                    pe.wait_ge(s5_folded, 1)
                if j % 4 == 0 and c >= 2:
                    pe.wait_ge(yp_out, c - 1)
                pe.wait_ge(back_done, j + 1)
                out = pairs[2][r:r + 32, c % 2, 0:NPROMPT]
                mm(out, cf[:, 0, j, :], backC[:, j % 2, 0], start=True, stop=False)
                mm(out, cf[:, 1, j, :], backS[:, j % 2, 1], start=False, stop=False)
                mm(out, cf[:, 2, j, :], backS[:, j % 2, 0], start=False, stop=False)
                mm(out, cf[:, 2, j, :], backC[:, j % 2, 1], start=False, stop=True).then_inc(y_done, 1)

            for j in range(ST):
                c, r = j // 4, 32 * (j % 4)
                if j % 4 == 0:
                    pe.wait_ge(u_copied, c + 1)
                if j >= 2:
                    pe.wait_ge(bu_rot, j - 1)
                for x in range(2):
                    last = mm(pairs[j % 2][:, x, 0:T], bblk[r:r + 32, c, x, :], ycat[r:r + 32, 4 + c, :],
                              start=True, stop=True)
                last.then_inc(bu_done, 1)
                if j < 6:
                    project_in(2 + j)
                if 8 <= j < 12:
                    g = j - 8
                    pe.wait_ge(d_ready, g + 1)
                    bank_free(DENSE_POOL + g)
                    mm(banks[g % 2][:, 0:T], wpool[:, g, :], ycat[:, g, :], start=True, stop=True
                       ).then_inc(dense_done, 1)
                if j >= 2:
                    y_tile(j - 2)
            y_tile(ST - 2)
            y_tile(ST - 1)
            pe.wait_ge(hs_ready, 1)
            for j in range(ST):
                c, r = j // 4, 32 * (j % 4)
                out = pairs[0][r:r + 32, 0, c * NSAMP:(c + 1) * NSAMP]
                mm(out, cblk[:, 0, j, :], hS[:, 0, j, :], start=True, stop=False)
                last = mm(out, cblk[:, 1, j, :], nhi[:, j, :], start=False, stop=True)
            last.then_inc(ys_done, 1)
            for m in range(4):
                dense(DENSE_GLU + m, W_GLU, 4 * m, 4, z, (z_ready, 0) if m == 0 else None)
            for m in range(DC):
                if m == 0:
                    pe.wait_ge(pool_out, 4)
                    pe.wait_ge(gated, 4)
                dense(DENSE_OUT + m, W_OUT_E, DC * m, DC, ycat)
            sum_squares(1)
            pe.wait_ge(xn_ready, 2 * DC)
            with pe.Fori(0, 2) as r:
                for i in range(SLOTS):
                    s = (FFN_UP + i) % SLOTS
                    pe.wait_ge(slot_full[s], 16 * r + 16 * ((FFN_UP + i) // SLOTS + 1))
                    pe.wait_ge(gated, SLOTS * r + (GATED0 + i - back(i, SLOTS) + 1))
                    for x in range(2):
                        for k in range(DC):
                            last = mm(pairs[i % 3][:, x, 0:T], slot(s)[:, DC * x + k, :], xn[:, k, :],
                                      start=(k == 0), stop=(k == DC - 1))
                    last.then_inc(up_done, 1)
            for m in range(DC):
                dense(DENSE_DOWN + m, FFN_DOWN, FC * m, FC, hF, (gated, GATED0) if m == 0 else None)
            sum_squares(2)
            pe.wait_ge(l1_loaded, 3 * 16)
            for k in range(DC):
                pe.wait_ge(xn_ready, 2 * DC + k + 1)
                last = mm(pairs[2][0:16, 0, 0:T], gk1[:, k, :], xn[:, k, :], start=(k == 0), stop=(k == DC - 1))
            last.then_inc(low_done, 1)
            pe.wait_ge(low_copied, 1)
            for h in range(H):
                if h >= 2:
                    pe.wait_ge(gx_ready, h - 1)
                mm(pairs[h % 2][:, 0, 0:T], gk2[:, h * P:(h + 1) * P], low, start=True, stop=True
                   ).then_inc(gk_done, 1)
            for o in range(24):
                dense(DENSE_IN_O + o, W_IN_O, DC * o, DC, xn)
            for c in range(NCH):
                for i in range(NSUB):
                    w = SUB * (i + 1)
                    if c == 0:
                        pe.wait_ge(dec_ready, i + 2)
                    if c and i == 0:
                        pe.wait_ge(att_copied, NSUB * c)
                    for h in range(H):
                        last = mm(pairs[2][0:w, 1, h * CH + SUB * i:h * CH + w], kd[i][:, h, c * w:(c + 1) * w],
                                  qd[:, h, c * CH + SUB * i:c * CH + w], start=True, stop=True)
                    last.then_inc(att_done, 1)
                if c:
                    pe.wait_ge(vtr_copied, c)
                else:
                    pe.wait_ge(q_copied, 16)
                for k in range(DC):
                    last = nc.tensor.transpose(pairs[0][0:CH, k // 4, (k % 4) * P:(k % 4 + 1) * P],
                                               vT[:, k, c * CH:(c + 1) * CH], ident)
                last.then_inc(vtr_done, 1)
                if c:
                    pe.wait_ge(ktr_copied, c)
                else:
                    pe.wait_ge(dec_ready, 7)
                for h in range(H):
                    last = nc.tensor.transpose(pairs[2][0:CH, 0, h * P:(h + 1) * P],
                                               ke[:, h, c * CH:(c + 1) * CH], ident)
                last.then_inc(ktr_done, 1)
                pe.wait_ge(att_copied, NSUB * (c + 1))
                pe.wait_ge(vtr_copied, c + 1)
                if c:
                    pe.wait_ge(o_copied, c)
                    pe.wait_ge(S_ready, H * c)
                for k in range(DC):
                    h = k // VC
                    out = pairs[1][:, k // 4, (k % 4) * CH:(k % 4 + 1) * CH]
                    last = mm(out, vtok[c % 2][:, k * P:(k + 1) * P], attS[:, c % 2, h, :], start=True, stop=(c == 0))
                    if c:
                        last = mm(out, S[:, h, (k % VC) * P:(k % VC + 1) * P], qe[:, h, c * CH:(c + 1) * CH],
                                  start=False, stop=True)
                last.then_inc(o_done, 1)
                pe.wait_ge(ktr_copied, c + 1)
                if c == 0:
                    pe.wait_ge(q_copied, 24)
                for h in range(H):
                    last = mm(banks[h // 2][:, (h % 2) * DV:(h % 2 + 1) * DV], ketok[:, h * P:(h + 1) * P],
                              vtok[c % 2][:, h * DV:(h + 1) * DV], start=True, stop=True)
                    if h % 2:
                        last.then_inc(kv_done, 1)
            pe.wait_ge(vtr_copied, NCH)
            pe.wait_ge(o_copied, NCH)
            for part in range(3):
                for k in range(4):
                    src = kT[:, k, NPROMPT:T] if part == 0 else vT[:, 4 * (part - 1) + k, NPROMPT:T]
                    dst = (pairs[0][0:NSAMP, 0], pairs[0][0:NSAMP, 1], pairs[1][0:NSAMP, 0])[part]
                    last = nc.tensor.transpose(dst[:, k * P:(k + 1) * P], src, ident)
                last.then_inc(str_done, 1)
            pe.wait_ge(S_ready, H * NCH)
            for n in range(NSAMP // 2 * H):
                p, h = n // H, n % H
                pe.wait_ge(vblk_ready, n + 1)
                if n >= 2:
                    pe.wait_ge(samp_ready, n - 1)
                mm(banks[n % 2][:, :], ktokS[:, h * P:(h + 1) * P], vblk[:, n % 2, :], start=True, stop=True
                   ).then_inc(outer_done, 1)
                if h == H - 1:
                    pe.wait_ge(samp_ready, n + 1)
                    for s in range(2):
                        b = 2 * p + s
                        for k in range(DC):
                            last = mm(pairs[1][:, 1, b * DC + k:b * DC + k + 1],
                                      samp[p % 2][:, s, k // VC, (k % VC) * P:(k % VC + 1) * P],
                                      qT[:, k // VC, NPROMPT + b:NPROMPT + b + 1], start=True, stop=True)
                    last.then_inc(so_done, 1)
            for h in range(H):
                pe.wait_ge(osq_ready, VC * (h + 1))
                if h >= 2:
                    pe.wait_ge(ostd_ready, h - 1)
                for c in range(VC):
                    last = mm(pairs[h % 2][:, 0, 0:T], ones, sq[:, VC * h + c, :], start=(c == 0), stop=(c == VC - 1))
                last.then_inc(oss_done, 1)
            pe.wait_ge(og_ready, H)
            for m in range(DC):
                dense(DENSE_OUT_O + m, W_OUT_O, DC * m, DC, oG)
            sum_squares(3)
            pe.wait_ge(xn_ready, 4 * DC)
            for t in range(NRT):
                for k in range(DC):
                    last = mm(banks[0][0:RT, t * NE:(t + 1) * NE], xn[:, k, RT0[t]:RT0[t] + RT], router[:, k, :],
                              start=(k == 0), stop=(k == DC - 1))
            last.then_inc(logit_done, 1)
            for t in range(NRT):
                if t >= 2:
                    pe.wait_ge(xtr_copied, t - 1)
                for k in range(DC):
                    last = nc.tensor.transpose(pairs[t % 2][0:RT, k // 4, (k % 4) * P:(k % 4 + 1) * P],
                                               xn[:, k, RT0[t]:RT0[t] + RT], ident)
                last.then_inc(xtr_done, 1)

            def expert_rows(src):
                for t in (NRT - 1, *range(NRT - 1)):
                    last = nc.tensor.transpose(banks[1][0:NE, RT0[t]:RT0[t] + RT], src[:, t, :],
                                               cst[0:RT, C_ID:C_ID + RT])
                return last

            pe.wait_ge(taken_ready, 1)
            expert_rows(taken).then_inc(mtr_done, 1)
            pe.wait_ge(pos_ready, 1)
            for t in range(NRT):
                nc.tensor.transpose(banks[0][0:RT, t * NE:(t + 1) * NE], mT[:, RT0[t]:RT0[t] + RT],
                                    cst[0:NE, C_ID:C_ID + NE])
            nc.tensor.transpose(banks[0][0:1, 64:64 + NE], posT[:, T - 1:T], cst[0:NE, C_ID:C_ID + NE]
                                ).then_inc(ptr_done, 1)
            pe.wait_ge(sel_loaded, 16)
            for e in range(NE):
                if e >= 2:
                    pe.wait_ge(selT_ready, e - 1)
                mm(pairs[2][:, e % 2, 0:T], sel[:, e, :], mT, start=True, stop=True).then_inc(pbc_done, 1)

            def gather(e):
                pe.wait_ge(pick_ready, e + 1)
                for t in range(NRT):
                    last = mm(pairs[2][:, 0, 0:1], pick[:, t, :], gates[:, t, bass.ds(e, 1)],
                              start=(t == 0), stop=(t == NRT - 1))
                last.then_inc(gate_done, 1)
                for k in range(DC):
                    for t in range(NRT):
                        last = mm(banks[k // 4][:, (k % 4) * CAP:(k % 4 + 1) * CAP], xtok[:, t, k * P:(k + 1) * P],
                                  pick[:, t, :], start=(t == 0), stop=(t == NRT - 1))
                    if k % 4 == 3:
                        last.then_inc(gath_done, 1)

            def up(e):
                for k in range(DC):
                    if k % 4 == 0:
                        pe.wait_ge(xg_copied, 2 * e + (k // 4 + 1))
                    pe.wait_ge(up_full[k], 16 * e + 16)
                    for x in range(2):
                        for u in range(2):
                            last = mm(pairs[x][:, u, 0:HW], xg[:, k, :],
                                      up_slot[k][:, x * EW + u * HW:x * EW + (u + 1) * HW],
                                      start=(k == 0), stop=(k == DC - 1))
                    last.then_inc(up_used, 1)

            def scatter(e):
                pe.wait_ge(y_copied, 2 * e + 2)
                for m in range(DC):
                    if m >= 2:
                        pe.wait_ge(x_ready, DC * e + (3 * DC + m - 1))
                    mm(banks[m % 2][:, 0:T], yS[:, m * P:(m + 1) * P],
                       selT[:, bass.ds(e, 1), :].rearrange("p a b -> p (a b)"), start=True, stop=True
                       ).then_inc(sc_done, 1)

            def transposes(e):
                pe.wait_ge(hs_ready2, e + 1)
                for f in range(EC):
                    h = hs.rearrange("p a b -> p (a b)")[:, f * P:(f + 1) * P]
                    last = nc.tensor.transpose(banks[f // 4][:, (f % 4) * CAP:(f % 4 + 1) * CAP], h, ident)
                    if f in (3, EC - 1):
                        last.then_inc(tr_done, 1)

            def down(e):
                pe.wait_ge(hT_copied, 2 * e + 2)
                for f in range(EC):
                    pe.wait_ge(down_full[f], 16 * e + 16)
                    for u in range(2):
                        last = mm(pairs[2][:, u, :], hG[:, f, :], down_slot[f][:, u * 512:(u + 1) * 512],
                                  start=(f == 0), stop=(f == EC - 1))
                    last.then_inc(down_used, 1)

            pe.wait_ge(selT_ready, NE)
            pe.wait_ge(xtr_copied, NRT)
            gather(0)
            up(0)
            transposes(0)
            pe.wait_ge(hT_copied, 2)
            pe.wait_ge(gate_copied, 1)
            gather(1)
            pe.wait_ge(gate_copied, 2)
            down(0)
            with pe.Fori(1, NE - 1) as e:
                up(e)
                scatter(e - 1)
                pe.wait_ge(x_ready, DC * e + 3 * DC)
                transposes(e)
                pe.wait_ge(hT_copied, 2 * e + 2)
                gather(e + 1)
                pe.wait_ge(gate_copied, e + 2)
                down(e)
            up(NE - 1)
            scatter(NE - 2)
            pe.wait_ge(x_ready, DC * (NE - 1) + 3 * DC)
            transposes(NE - 1)
            down(NE - 1)
            scatter(NE - 1)
            pe.wait_ge(more_ready, 1)
            flag = pe.value_load(more[0:1, 0:1], min_val=0, max_val=1)
            with pe.If(flag):
                pe.wait_ge(x_ready, DC * (NE + 3))
                expert_rows(gover).then_inc(fb_tr, 1)
                pe.wait_ge(fb_gT, 1)
                for e in range(NE):
                    if e >= 2:
                        pe.wait_ge(fb_copied, e - 1)
                    mm(pairs[1][:, e % 2, 0:T], sel[:, e, :], gT, start=True, stop=True).then_inc(fb_gbc, 1)
                with pe.Fori(0, NE) as e:
                    pe.wait_ge(fb_full, 16 * (DC + EC) * e + 16 * (DC + EC))
                    for i in range(EC):
                        pe.wait_ge(fb_gated, EC * e + (i + 1))
                        for x in range(2):
                            for k in range(DC):
                                c = x * EW + i * P
                                last = mm(pairs[0][:, x, 0:T], up_slot[k][:, c:c + P], xn[:, k, :],
                                          start=(k == 0), stop=(k == DC - 1))
                        last.then_inc(fb_up, 1)
                    for m in range(DC):
                        if m == 0:
                            pe.wait_ge(fb_gated, EC * e + (EC + 1))
                        pe.wait_ge(fb_x, DC * e + (m + 1))
                        for f in range(EC):
                            last = mm(banks[m % 2][:, 0:T], down_slot[f][:, m * P:(m + 1) * P], hM[:, f, :],
                                      start=(f == 0), stop=(f == EC - 1))
                        last.then_inc(fb_down, 1)
            sum_squares(4)


def kernel(**inputs):
    import numpy as np
    import concourse.bacc as bacc
    from concourse import mybir as mb
    from concourse.bass_utils import run_bass_kernel_spmd as run

    a = {k: np.asarray(v) for k, v in inputs.items()}
    f = np.float32

    def features(x):
        return x.reshape(x.shape[0], -1, P).transpose(2, 1, 0)

    def tiles(w):
        K, M = w.shape
        return w.reshape(K // P, P, M // P, P).transpose(2, 0, 1, 3)

    def units(t, n):
        t = t.reshape(-1, n, P, P)
        return t.transpose(0, 2, 1, 3).reshape(t.shape[0], P, n * P)

    x = np.concatenate([a["meta_tokens"], a["x_prompt"][0], a["x_sample"][:, 0]], axis=0)
    ins = {"xT": features(x)}
    vec = np.concatenate([a["norm_mix_e"][0], a["norm_ffn_e"][0], a["norm_mix_o"][0], a["norm_ffn_o"][0],
                          a["norm_final"], a["pool_scale"][0], a["s5_d"][0], a["b_glu"][0], a["b_gk"][0],
                          a["gla_norm"][0]])
    ins["vecs"] = vec.reshape(-1, P).T
    cst = np.zeros((P, NCST), f)
    cst[:, C_ID:C_ID + P] = np.eye(P)
    cst[:, C_ONE:C_ONE + P] = 1
    cst[:CH, C_MASK:C_MASK + CH] = np.triu(np.ones((CH, CH)))
    cst[:, C_IOTA:C_IOTA + P] = np.arange(P)
    cst[:, C_SLOT] = np.arange(P)
    cst[:, C_OWN:C_OWN + NRT] = 1
    cst[:NRT * RT - T, C_OWN + NRT - 1] = 0
    for g in range(NG):
        cst[:, C_CNT + 16 * g:C_CNT + 16 * g + 16] = 1.0 / np.minimum(np.arange(16) + 1, 2 << g)
    cst[:, C_RESET:C_RESET + NPROMPT] = np.arange(NPROMPT) % CH != 0
    cst[:, C_EPS] = EPS
    ins["cst"] = cst
    sel = np.zeros((NE, NE, P), f)
    sel[np.arange(NE), np.arange(NE)] = 1
    ins["sel"] = sel

    def states(s):
        s = s.reshape(s.shape[:-2] + (ST, P))
        return np.moveaxis(np.moveaxis(s, -1, 0), -1, 1)

    G = 2 * ST
    logdt = np.broadcast_to(a["s5_log_dt"][0][:, None], (G, 64))
    ins["s5p"] = np.stack([states(a["s5_a_re"][0]), states(a["s5_a_im"][0]), states(logdt)], 1)
    ins["h0"] = np.stack([states(a["state_s5_re"][0]), states(a["state_s5_im"][0])], 1)
    bb = np.zeros((4, 2, 16, 4, 2, 2, 64), f)
    cc = np.zeros((2, 64, 2, ST, 2, 16), f)
    for x_, (bn, cn) in enumerate((("s5_b_re", "s5_c_re"), ("s5_b_im", "s5_c_im"))):
        bt = a[bn][0].reshape(4, 4, 2, 64, 16)
        ct = a[cn][0].reshape(ST, 2, 16, 64)
        for g in range(2):
            bb[:, g, :, :, x_, g, :] = bt[:, :, g].transpose(1, 3, 0, 2)
            cc[g, :, x_, :, g, :] = ct[:, g].transpose(2, 0, 1)
    ins["bblk"] = bb.reshape(P, 4, 2, P)
    ins["cblk"] = cc.reshape(P, 2, ST, 32)
    ins["past"] = a["state_pool"][0].reshape(NSAMP, PAST, NG, P).transpose(3, 2, 0, 1)
    ins["wpool"] = a["w_pool"][0].transpose(1, 0, 2)
    win = tiles(a["w_in_e"][0])
    up = np.stack([tiles(a["ffn_w1"][0]), tiles(a["ffn_w3"][0])], 1)
    ins["main"] = np.concatenate([units(t, UT) for t in (
        np.concatenate([win[4:], win[:4]]), tiles(a["w_glu"][0]), tiles(a["w_out_e"][0]), up,
        tiles(a["ffn_w2"][0]), tiles(a["w_in_o"][0]), tiles(a["w_out_o"][0]))])
    ins["up"] = np.concatenate([a["moe_w1"][0], a["moe_w3"][0]], axis=2).reshape(NE * DC, P, 2 * EW)
    ins["down"] = a["moe_w2"][0].reshape(NE * EC, P, D)
    ins["gk1"] = a["w_gk1"][0].reshape(DC, P, 16).transpose(1, 0, 2)
    ins["gk2"] = a["w_gk2"][0]
    ins["router"] = a["w_router"][0].reshape(DC, P, NE).transpose(1, 0, 2)
    ins["sgla"] = a["state_gla"][0].transpose(2, 0, 1, 3)
    outs = [("yT", (P, DC, T)), ("poolp", (P, NG, PAST)), ("pools", (P, NG, NSAMP, PAST)),
            ("s5prompt", (P, 2, ST)), ("s5samp", (P, 2, ST, NSAMP)), ("glap", (P, H, DV)),
            ("glas", (P, NSAMP, H, DV))]
    nc = bacc.Bacc("TRN2", target_bir_lowering=False, num_devices=1)
    arrays, args = {}, []
    for name, v in ins.items():
        v = np.ascontiguousarray(v)
        arrays["in_" + name] = v
        args.append(nc.dram_tensor("in_" + name, v.shape, mb.dt.from_np(v.dtype), kind="ExternalInput").ap())
    for name, shape in outs:
        args.append(nc.dram_tensor("out_" + name, shape, mb.dt.float32, kind="ExternalOutput").ap())
    build(nc, *args)
    r = run(nc, [arrays], core_ids=[0]).results[0]
    o = {name: np.asarray(r["out_" + name]) for name, _ in outs}

    y = o["yT"].transpose(2, 1, 0).reshape(T, D)
    poolp = o["poolp"].transpose(2, 1, 0).reshape(1, 1, PAST, NG * P)
    pools = o["pools"].transpose(2, 3, 1, 0).reshape(1, NSAMP, PAST, NG * P)
    s5p = o["s5prompt"].transpose(1, 2, 0).reshape(2, 1, 1, G, 64)
    s5s = o["s5samp"].transpose(1, 3, 2, 0).reshape(2, 1, NSAMP, G, 64)
    glap = o["glap"].transpose(1, 0, 2)[None, None]
    glas = o["glas"].transpose(1, 2, 0, 3)[None]
    res = (y[None, 16:NPROMPT], y[NPROMPT:, None], poolp, pools, s5p[0], s5s[0], s5p[1], s5s[1], glap, glas)
    return tuple(np.ascontiguousarray(v) for v in res)
```

```python
import math

import concourse.bass as bass
from concourse import mybir
from contextlib import ExitStack

F32 = mybir.dt.float32
F32R = mybir.dt.float32r
U32 = mybir.dt.uint32
ALU = mybir.AluOpType
ACT = mybir.ActivationFunctionType
AX = mybir.AxisListType

P = 128
D = 1024
DC = D // P
NPROMPT = 272
NSAMP = 8
T = NPROMPT + NSAMP
EPS = 1e-6
NG = 4
PAST = 15
ST = 16
FF = 2816
FC = FF // P
H = 4
DV = 256
VC = DV // P
CH = 68
NCH = NPROMPT // CH
SUB = 17
NSUB = CH // SUB
MID = SUB // 2
NE = 8
EC = 896 // P
CAP = 128
EW = EC * P
HW = EW // 2
NRT = 3
RT = -(-T // NRT)
RT0 = [0, RT, T - RT]

TDVE = 9
NDBL = math.ceil(math.log2(NPROMPT))
DBL0 = 4
NBUF = 3

UT = 16
UNIT = UT * P
SLOTS = 11
W_IN_E, W_GLU, W_OUT_E = 0, 4, 5
FFN_UP = W_OUT_E + 4
FFN_DOWN = FFN_UP + FC
W_IN_O = FFN_DOWN + FC * DC // UT
W_OUT_O = W_IN_O + 12
MOE = W_OUT_O + 4
BODY = 11
RAW = 4
HI_SLOTS, LO_SLOTS = (9, 5, 7), (10, 6, 8)
ROUNDS = (W_IN_O - FFN_UP) // BODY
NIN = W_OUT_O - W_IN_O
OUT_O_SLOTS = (4, 0, 1, 2)

DENSE_POOL, DENSE_GLU, DENSE_OUT, DENSE_DOWN, DENSE_IN_O, DENSE_OUT_O = 8, 12, 16, 24, 32, 56
GATED0 = 4

V_NORM = [0, 8, 16, 24, 32]
V_PSCALE, V_D, V_BGLU, V_BGK, V_GNORM = 40, 44, 48, 52, 56
NVEC = 58
C_ID, C_ONE, C_MASK, C_IOTA = 0, 128, 256, 324
C_CNT, C_RESET, C_EPS = C_IOTA + P, C_IOTA + P + 64, C_IOTA + P + 64 + NPROMPT
C_OWN = C_EPS + 1
C_SLOT = C_OWN + NRT
NCST = C_SLOT + 1


TWO_PI = 2 * math.pi
PI_1 = 6.28125
PI_2 = 0.0019350051879882812
PI_3 = TWO_PI - PI_1 - PI_2
ROUND = 12582912.0


def build(nc, xT_d, vecs_d, cst_d, sel_d, s5p_d, h0_d, bblk_d, cblk_d, past_d, wpool_d, main_d,
          up_d, down_d, gk1_d, gk2_d, router_d, sgla_d,
          yT_d, poolp_d, pools_d, s5p_out, s5s_out, glap_d, glas_d):
    ctx = ExitStack()
    with ctx:
        place = [-(-nc.sbuf_base // 32) * 32]
        where = {}

        def sb(name, shape, dt=F32):
            where[name] = place[0]
            place[0] += -(-4 * math.prod(shape[1:]) // 32) * 32
            return nc.alloc_sbuf_tensor_at(name, shape, dt, offset=where[name])

        def rounded(name, over, first, *shape):
            return nc.alloc_sbuf_tensor_at(name, [P, *shape], F32R, offset=where[over] + 4 * first)

        def sem(name):
            return ctx.enter_context(nc.semaphore(name))

        ring = sb("ring", [P, SLOTS, UNIT])
        xT = sb("xT", [P, DC, T])
        xn = sb("xn", [P, DC, T])
        sq = sb("sq", [P, DC, T])
        rstd = sb("rstd", [P, T])
        vecs = sb("vecs", [P, NVEC])
        cst = sb("cst", [P, NCST])
        ident = cst[:, C_ID:C_ID + P]
        ones = cst[:, C_ONE:C_ONE + P]
        w_hi = [rounded(f"w_hi{n}", "ring", s * UNIT, UT, P) for n, s in enumerate(HI_SLOTS)]
        w_lo = [rounded(f"w_lo{n}", "ring", s * UNIT, UT, P) for n, s in enumerate(LO_SLOTS)]
        x_hi = rounded("x_hi", "sq", 0, DC, T)
        x_lo = rounded("x_lo", "xn", 0, DC, T)
        W = 22400
        work = sb("work", [P, W])
        at = [0]

        def region(*shape, rows=P):
            n = int(math.prod(shape))
            v = work[0:rows, at[0]:at[0] + n]
            at[0] += n
            assert at[0] <= W, at[0]
            if len(shape) == 2:
                v = v.rearrange("p (a b) -> p a b", a=shape[0])
            if len(shape) == 3:
                v = v.rearrange("p (a b c) -> p a b c", a=shape[0], b=shape[1])
            return v

        cosT = region(ST, NPROMPT)
        sinT = region(ST, NPROMPT)
        dyn = at[0]
        rotA = region(2, 2, NPROMPT)
        rotB = sq[:, :, :].rearrange("p a b -> p (a b)")[:, 0:4 * NPROMPT].rearrange("p (j x t) -> p j x t", j=2, x=2)
        scanned = region(2, 2, NPROMPT)
        backC = region(2, 2, NPROMPT)
        backS = region(2, 2, NPROMPT)
        tab_scratch = [work[:, a:a + 2 * P * n].rearrange("p (x j t) -> p x j t", x=2, t=P)
                       for a, n in ((dyn, TDVE), (dyn + 2 * P * TDVE, ST - TDVE), (dyn, ST))]
        sig = backC.rearrange("p a b c -> p (a b c)")[:, 0:2 * T].rearrange("p (a b) -> p a b", a=2)
        cblk = region(2, ST, 32)
        cf = region(3, ST, 32)
        bblk = region(4, 2, P)
        ycat = region(DC, T)
        upad = region(NG, 16 + NPROMPT)
        z = upad.rearrange("p a b -> p (a b)")[:, 0:4 * T].rearrange("p (a b) -> p a b", a=4)
        pbuf = region(NG, NSAMP * 16).rearrange("p g (b t) -> p g b t", b=NSAMP)
        h0 = region(2, ST, NSAMP)
        buS = region(2, ST, NSAMP)
        hS = region(2, ST, NSAMP)
        par = region(20, ST)
        s5p = region(3, ST)
        wpool = region(NG, P)
        glast = region(2, ST)
        nhi = region(ST, NSAMP)
        at[0] = 0
        h_hi = rounded("h_hi", "work", 0, FC, T)
        h_lo = rounded("h_lo", "work", FC * T, FC, T)
        at[0] = 2 * FC * T
        silF = region(3, T)
        hF = region(3, T)
        at[0] = 0
        qT = region(H, T)
        kT = region(H, T)
        vT = region(DC, T)
        gS = region(DC, T)
        gx = region(H, T)
        bT = region(H, NPROMPT)
        mark = at[0]
        qd = region(H, NPROMPT)
        kd = [region(H, NCH * SUB * (i + 1)) for i in range(NSUB)]
        gl = work[:, mark:mark + H * T].rearrange("p (a b) -> p a b", a=H)
        qe = region(H, NPROMPT)
        ke = region(H, NPROMPT)
        elast = region(H, NCH)
        vblk = work[0:NSAMP, at[0]:at[0] + 2 * H * DV].rearrange("p (n v) -> p n v", n=2)
        attS = region(2, H, CH, rows=CH)
        ketok = region(H * P, rows=CH)
        S = region(H, DV)
        samp = region(NBUF, H, DV)
        ktok_at = at[0]
        ktokS = region(H * P, rows=NSAMP)
        vtokS = region(H * DV, rows=NSAMP)
        egS = region(H, NSAMP)
        gk1 = region(DC, 16)
        gk2 = work[0:16, ktok_at:ktok_at + H * P]
        low = work[0:16, mark:mark + T]
        rms = gx
        assert at[0] <= W - 560 - DC * NE, at[0]
        at[0] = W - 560 - DC * NE
        assert at[0] >= 0
        router = region(DC, NE)
        oT = xn
        vtok = [sq[0:CH, 0:4, :].rearrange("p a b -> p (a b)")[:, 0:H * DV],
                sq[0:CH, 4:8, :].rearrange("p a b -> p (a b)")[:, 0:H * DV]]
        oG = vT
        at[0] = 0
        xtok = region(NRT, D, rows=RT)
        selT = region(NE, T)
        pick = region(NRT, CAP, rows=RT)
        xg = region(DC, CAP)
        silG = region(2, HW)
        hs = region(2, HW)
        hG = region(EC, CAP)
        yS = region(D)
        gslot = region(1)
        sel = region(NE, P, rows=NE)
        mT = region(T, rows=NE)
        posT = region(T, rows=NE)
        onesT = region(T, rows=NE)
        top = region(1, rows=1)
        gbc = region(NE, T)
        hM = region(EC, T)
        silM = region(T)
        gpre = region(T)
        gT = region(T, rows=NE)
        base = region(2, rows=1)
        assert at[0] <= W - 560 - DC * NE, at[0]
        at[0] = W - 560
        rt = region(16, NRT * NE, rows=RT)
        rsc = region(8, NRT, rows=RT)
        rtile = [rt[:, n].rearrange("p (t e) -> p t e", t=NRT) for n in range(16)]
        lg, pr, mx8, ix, gates, oh2, taken, postok, gover = rtile[:9]
        idx = sb("idx", [RT, NRT * 8], U32)
        more = sb("more", [1, 1], mybir.dt.int32)
        ringf = ring[:, :, :].rearrange("p s n -> p (s n)")
        up_slot = [ringf[:, k * 2 * EW:(k + 1) * 2 * EW] for k in range(DC)]
        down_slot = [ringf[:, DC * 2 * EW + f * D:DC * 2 * EW + (f + 1) * D] for f in range(EC)]

        banks = [ctx.enter_context(nc.psum_tensor(f"bank{i}", [P, 512], F32)) for i in range(2)]
        pairs = [ctx.enter_context(nc.psum_tensor(f"pair{i}", [P, 2, 512], F32)) for i in range(3)]

        slot_full = [sem(f"slot_full{s}") for s in range(FFN_UP)]
        x_loaded, s5_loaded, late_loaded = sem("x_loaded"), sem("s5_loaded"), sem("late_loaded")
        cst_loaded = sem("cst_loaded")
        l1_loaded = sem("l1_loaded")
        sel_loaded = sem("sel_loaded")
        x_ready = sem("x_ready")
        sq_ready, ss_ready, std_ready, xn_ready = (sem(n) for n in ("sq_ready", "ss_ready", "std_ready", "xn_ready"))
        dve_link, act_link, pool_link = sem("dve_link"), sem("act_link"), sem("pool_link")
        dense_done = sem("dense_done")
        u_copied = sem("u_copied")
        s5_dt, s5_arg, s5_trig, s5_pow = sem("s5_dt"), sem("s5_arg"), sem("s5_trig"), sem("s5_pow")
        bu_done, bu_rot, rot_ready = sem("bu_done"), sem("bu_rot"), sem("rot_ready")
        scan_done, back_done, y_done, y_out = sem("scan_done"), sem("back_done"), sem("y_done"), sem("y_out")
        hs_ready, ys_done = sem("hs_ready"), sem("ys_done")
        d_ready, pool_out = sem("d_ready"), sem("pool_out")
        z_ready, sig_ready, gated = sem("z_ready"), sem("sig_ready"), sem("gated")
        up_done, sil_done = sem("up_done"), sem("sil_done")
        states_out, pool_states = sem("states_out"), sem("pool_states")
        s5_folded, yp_out = sem("s5_folded"), sem("yp_out")
        s5_states = sem("s5_states")
        low_done, low_copied, gk_done, gx_ready, gl_ready = (
            sem(n) for n in ("low_done", "low_copied", "gk_done", "gx_ready", "gl_ready"))
        q_copied = sem("q_copied")
        dec_arg, dec_exp, dec_ready = sem("dec_arg"), sem("dec_exp"), sem("dec_ready")
        vtr_done, vtr_copied, ktr_done, ktr_copied = (sem(n) for n in ("vtr_done", "vtr_copied", "ktr_done", "ktr_copied"))
        att_done, att_copied, o_done, o_copied, kv_done, S_ready = (
            sem(n) for n in ("att_done", "att_copied", "o_done", "o_copied", "kv_done", "S_ready"))
        str_done, str_copied = sem("str_done"), sem("str_copied")
        samp_loaded = [sem(f"samp_loaded{n}") for n in range(NBUF)]
        samp_saved = [sem(f"samp_saved{n}") for n in range(NBUF)]
        vblk_ready, outer_done, samp_ready, so_done, so_copied = (
            sem(n) for n in ("vblk_ready", "outer_done", "samp_ready", "so_done", "so_copied"))
        osq_ready, oss_done, ostd_ready, og_ready = (sem(n) for n in ("osq_ready", "oss_done", "ostd_ready", "og_ready"))
        logit_done, shifted, exped, taken_ready, mtr_done, pos_ready, ptr_done = (
            sem(n) for n in ("logit_done", "shifted", "exped", "taken_ready", "mtr_done", "pos_ready", "ptr_done"))
        xtr_done, xtr_copied, pbc_done, selT_ready, more_ready = (
            sem(n) for n in ("xtr_done", "xtr_copied", "pbc_done", "selT_ready", "more_ready"))
        up_full = [sem(f"up_full{k}") for k in range(DC)]
        down_full = [sem(f"down_full{f}") for f in range(EC)]
        pick_ready, gate_done, gate_copied, gath_done, xg_copied = (
            sem(n) for n in ("pick_ready", "gate_done", "gate_copied", "gath_done", "xg_copied"))
        up_used, silg_done, hidden_ready, tr_done, hT_copied, down_used, y_copied, sc_done = (
            sem(n) for n in ("up_used", "silg_done", "hidden_ready", "tr_done", "hT_copied", "down_used", "y_copied",
                             "sc_done"))
        fb_tr, fb_gT, fb_gbc, fb_copied, fb_full, fb_up, fb_sil, fb_gpre, fb_gated, fb_down, fb_x = (
            sem(n) for n in ("fb_tr", "fb_gT", "fb_gbc", "fb_copied", "fb_full", "fb_up", "fb_sil", "fb_gpre",
                             "fb_gated", "fb_down", "fb_x"))
        y_saved, egs_ready, rms_ready = sem("y_saved"), sem("egs_ready"), sem("rms_ready")
        raw_full = [sem(f"raw_full{n}") for n in range(RAW)]
        w_hi_ready, w_lo_ready, down_unit = sem("w_hi_ready"), sem("w_lo_ready"), sem("down_unit")
        x_hi_ready, x_lo_ready, h_lo_ready, h_hi_ready = (sem(n) for n in ("x_hi_ready", "x_lo_ready", "h_lo_ready",
                                                                      "h_hi_ready"))

        def unit_end(n):
            if n < W_GLU:
                return dense_done, 2 * (n + 1)
            if n == W_GLU:
                return dense_done, DENSE_GLU + 4
            if n < FFN_UP:
                return dense_done, DENSE_OUT + 2 * (n - W_OUT_E + 1)
            return dense_done, DENSE_OUT_O + 2 * (n - W_OUT_O + 1)

        def slot_of(n):
            return n if n < FFN_UP else OUT_O_SLOTS[n - W_OUT_O]

        def split_used(u):
            if u < FC:
                return up_done, u + 1
            if u < ROUNDS * BODY - 1:
                return down_unit, u - FC + 1
            return dense_done, DENSE_IN_O + 2 * (u - ROUNDS * BODY + 1)

        def back(i, length, depth=3):
            return depth if i >= depth else i + length - max(x for x in range(length) if x % depth == i)

        def bc(ap, shape):
            return ap.broadcast_to(shape)

        def power(i, x):
            if i < 8:
                return hS.rearrange("p a b c -> p (a b c)")[:, (2 * i + x) * ST:(2 * i + x + 1) * ST]
            return nhi.rearrange("p a b -> p (a b)")[:, x * ST:(x + 1) * ST]

        def rotation_tables(eng, link, steps, lo, hi, scratch):
            cT, sT = cosT[:, lo:hi], sinT[:, lo:hi]
            for i in steps:
                n = 1 << i
                m = min(n, NPROMPT - n)
                c0, s0 = cT[:, :, 0:m], sT[:, :, 0:m]
                A, B = scratch[:, 0, 0:hi - lo, 0:m], scratch[:, 1, 0:hi - lo, 0:m]
                pc, ps = (power(i, x)[:, lo:hi].unsqueeze(2).broadcast_to([P, hi - lo, m]) for x in range(2))
                eng.tensor_tensor(A, c0, pc, ALU.mult)
                link(eng.tensor_tensor(B, s0, ps, ALU.mult))
                link(eng.tensor_tensor(cT[:, :, n:n + m], A, B, ALU.subtract))
                eng.tensor_tensor(A, c0, ps, ALU.mult)
                link(eng.tensor_tensor(B, s0, pc, ALU.mult))
                link(eng.tensor_tensor(sT[:, :, n:n + m], A, B, ALU.add))

        block = ctx.enter_context(nc.Block())

        @block.sync
        def _(sp):
            sp.wait_ge(s5_loaded, 16)
            sp.wait_ge(cst_loaded, 2 * 16)
            sp.wait_ge(x_loaded, 16)
            def load_main(n, to, done):
                sp.dma_start(ring[:, to, :], main_d[bass.ds(n, 1), :, :].rearrange("o p n -> p (o n)")
                             ).then_inc(done, 16)

            for n in range(FFN_UP):
                load_main(n, n, slot_full[n])
            for i in range(BODY):
                if i < RAW:
                    sp.wait_ge(*unit_end(i))
                else:
                    sp.wait_ge(w_lo_ready, i - RAW + 1)
                load_main(FFN_UP + i, i % RAW, raw_full[i % RAW])
            with sp.Fori(1, ROUNDS) as r:
                for i in range(BODY):
                    sp.wait_ge(w_lo_ready, BODY * r + (i - back(i, BODY, RAW) + 1))
                    load_main(BODY * r + (FFN_UP + i), i % RAW, raw_full[i % RAW])
            for i in range(NIN):
                sp.wait_ge(w_lo_ready, ROUNDS * BODY + i - back(i, BODY, RAW) + 1)
                load_main(W_IN_O + i, i % RAW, raw_full[i % RAW])

            def wait_split(s):
                if s < RAW:
                    sp.wait_ge(w_lo_ready, ROUNDS * BODY + max(range(s, NIN, RAW)) + 1)
                else:
                    k = (HI_SLOTS if s in HI_SLOTS else LO_SLOTS).index(s)
                    sp.wait_ge(*split_used(ROUNDS * BODY + max(range(k, NIN, 3))))

            for n in range(W_OUT_O, MOE):
                s = slot_of(n)
                if s < RAW:
                    wait_split(s)
                else:
                    sp.wait_ge(*unit_end(s))
                load_main(n, s, slot_full[s])

            def load_up(e, k, done):
                sp.dma_start(up_slot[k], up_d[bass.ds(e * DC + k, 1), :, :].rearrange("o p n -> p (o n)")
                             ).then_inc(done, 16)

            def load_down(e, f, done):
                sp.dma_start(down_slot[f], down_d[bass.ds(e * EC + f, 1), :, :].rearrange("o p n -> p (o n)")
                             ).then_inc(done, 16)

            def wait_main(slot):
                first, last = slot
                for s in range(first // UNIT, (last - 1) // UNIT + 1):
                    if s in OUT_O_SLOTS:
                        sp.wait_ge(*unit_end(W_OUT_O + OUT_O_SLOTS.index(s)))
                    else:
                        wait_split(s)

            for k in range(DC):
                wait_main((k * 2 * EW, (k + 1) * 2 * EW))
                load_up(0, k, up_full[k])
            for f in range(EC):
                wait_main((DC * 2 * EW + f * D, DC * 2 * EW + (f + 1) * D))
                load_down(0, f, down_full[f])
            with sp.Fori(1, NE) as e:
                for k in range(DC):
                    sp.wait_ge(up_used, DC * e + (k + 1 - DC))
                    load_up(e, k, up_full[k])
                for f in range(EC):
                    sp.wait_ge(down_used, EC * e + (f + 1 - EC))
                    load_down(e, f, down_full[f])
            sp.wait_ge(more_ready, 1)
            flag = sp.value_load(more[0:1, 0:1], min_val=0, max_val=1)
            with sp.If(flag):
                def load_all(e):
                    for k in range(DC):
                        load_up(e, k, fb_full)
                    for f in range(EC):
                        load_down(e, f, fb_full)

                sp.wait_ge(fb_gbc, NE)
                load_all(0)
                with sp.Fori(1, NE) as e:
                    sp.wait_ge(fb_down, DC * e)
                    load_all(e)

        @block.gpsimd
        def _(pool):
            links = [0]

            def link(ins):
                links[0] += 1
                ins.then_inc(pool_link, 1)
                pool.wait_ge(pool_link, links[0])

            pool.wait_ge(s5_pow, 1)
            rotation_tables(nc.gpsimd, link, range(DBL0, NDBL), TDVE, ST, tab_scratch[1])
            for j in range(ST):
                pool.wait_ge(scan_done, j + 1)
                if j >= 2:
                    pool.wait_ge(y_done, j - 1)
                g = scanned[:, j % 2]
                nc.gpsimd.tensor_tensor(backC[:, j % 2], g, bc(cosT[:, j:j + 1, :], [P, 2, NPROMPT]), ALU.mult)
                nc.gpsimd.tensor_tensor(backS[:, j % 2], g, bc(sinT[:, j:j + 1, :], [P, 2, NPROMPT]),
                                        ALU.mult).then_inc(back_done, 1)
            pool.wait_ge(s5_states, 1)
            pool.dma_start(s5p_out, glast).then_inc(states_out, 16)
            pool.wait_ge(hs_ready, 1)
            pool.dma_start(s5s_out, hS).then_inc(states_out, 16)
            def low_part(r, i):
                pool.wait_ge(w_hi_ready, BODY * r + (i + 1))
                nc.gpsimd.tensor_tensor(w_lo[i % 3][:, :, :], ring[:, i % RAW, :].rearrange("p (t m) -> p t m", m=P),
                                        w_hi[i % 3][:, :, :].bitcast(F32), ALU.subtract).then_inc(w_lo_ready, 1)

            with pool.Fori(0, ROUNDS) as r:
                for i in range(BODY):
                    low_part(r, i)
            for i in range(3):
                low_part(ROUNDS, i)
            def load_sample(b):
                pool.dma_start(samp[:, b % NBUF], sgla_d[:, b]).then_inc(samp_loaded[b % NBUF], 16)

            def save_sample(b):
                pool.wait_ge(samp_ready, b + 1)
                pool.dma_start(glas_d[:, b], samp[:, b % NBUF]).then_inc(samp_saved[b % NBUF], 16)

            pool.wait_ge(xn_ready, 3 * DC)
            for b in range(NBUF):
                load_sample(b)
            for i in range(3, NIN):
                low_part(ROUNDS, i)
            for b in range(NSAMP - 1):
                save_sample(b)
                if b and b - 1 + NBUF < NSAMP:
                    pool.wait_ge(so_done, b)
                    pool.wait_ge(samp_saved[(b - 1) % NBUF], 16 * ((b - 1) // NBUF + 1))
                    load_sample(b - 1 + NBUF)
            save_sample(NSAMP - 1)
            pool.wait_ge(S_ready, H * NCH)
            pool.dma_start(glap_d, S).then_inc(states_out, 16)
            pool.wait_ge(states_out, 3 * 16)

        @block.scalar
        def _(act):
            links = [0]

            def link(ins):
                links[0] += 1
                ins.then_inc(act_link, 1)
                act.wait_ge(act_link, links[0])

            act.dma_start(s5p, s5p_d).then_inc(s5_loaded, 16)
            act.dma_start(xT[:, :, :], xT_d).then_inc(x_loaded, 16)
            act.dma_start(cst[:, :], cst_d).then_inc(cst_loaded, 16)
            act.dma_start(vecs[:, :], vecs_d).then_inc(cst_loaded, 16)
            act.dma_start(cblk, cblk_d).then_inc(late_loaded, 16)
            act.dma_start(bblk, bblk_d).then_inc(late_loaded, 16)
            act.dma_start(h0, h0_d).then_inc(late_loaded, 16)
            act.dma_start(pbuf[:, :, :, 0:PAST], past_d).then_inc(late_loaded, 16)
            act.dma_start(wpool, wpool_d).then_inc(late_loaded, 16)

            def squares(i, k):
                if i:
                    act.wait_ge(x_ready, 8 * (i - 1) + k + 1)
                nc.scalar.activation(sq[:, k, :], xT[:, k, :], ACT.Square).then_inc(sq_ready, 1)

            def std(i):
                act.wait_ge(ss_ready, i + 1)
                nc.scalar.activation(rstd[:, :], pairs[2][:, 1, 0:T], ACT.Sqrt, scale=1.0 / D,
                                     bias=cst[:, C_EPS:C_EPS + 1]).then_inc(std_ready, 1)

            act.wait_ge(s5_loaded, 16)
            nc.scalar.activation(par[:, 0], s5p[:, 2], ACT.Exp).then_inc(s5_dt, 1)
            act.wait_ge(x_loaded, 16)
            for k in range(DC):
                squares(0, k)
            act.wait_ge(s5_arg, 1)
            nc.scalar.activation(par[:, 3], par[:, 1], ACT.Exp)
            nc.scalar.activation(par[:, 4], par[:, 2], ACT.Sin)
            nc.scalar.activation(par[:, 5], par[:, 6], ACT.Sin).then_inc(s5_trig, 1)
            act.wait_ge(cst_loaded, 2 * 16)
            std(0)

            def copy_u(o):
                act.wait_ge(dense_done, o + 1)
                if o < 4:
                    nc.scalar.copy(ycat[:, 4 + o, :], banks[o % 2][:, 0:T]).then_inc(u_copied, 1)
                else:
                    g = o - 4
                    act.wait_ge(late_loaded, 5 * 16)
                    nc.scalar.copy(upad[:, g, 16:], banks[o % 2][:, 0:NPROMPT])
                    nc.scalar.copy(pbuf[:, g, :, PAST], banks[o % 2][:, NPROMPT:T]).then_inc(u_copied, 1)

            copy_u(0)
            copy_u(1)
            for j in range(ST):
                if j < 6:
                    copy_u(2 + j)
                if j == 6:
                    act.wait_ge(u_copied, 8)
                    act.dma_start(poolp_d, upad[:, :, 16 + NPROMPT - PAST:]).then_inc(pool_states, 16)
                    act.dma_start(pools_d, pbuf[:, :, :, 1:]).then_inc(pool_states, 16)
                if 8 <= j < 12:
                    g = j - 8
                    act.wait_ge(dense_done, 9 + g)
                    nc.scalar.activation(ycat[:, g, :], banks[g % 2][:, 0:T], ACT.Copy,
                                         scale=vecs[:, V_PSCALE + g:V_PSCALE + g + 1]).then_inc(pool_out, 1)
            for c in range(4):
                act.wait_ge(y_out, c + 1)
                nc.scalar.activation(z[:, c, :], z[:, c, :], ACT.Gelu_apprx_tanh).then_inc(z_ready, 1)
            for m in range(4):
                act.wait_ge(dense_done, 13 + m)
                if m >= 2:
                    act.wait_ge(gated, m - 1)
                nc.scalar.activation(sig[:, m % 2, :], banks[m % 2][:, 0:T], ACT.Sigmoid,
                                     bias=vecs[:, V_BGLU + m:V_BGLU + m + 1]).then_inc(sig_ready, 1)
            def high_part(r, i, used=None):
                per = len(range(i % RAW, BODY, RAW))
                act.wait_ge(raw_full[i % RAW], 16 * per * r + 16 * (i // RAW + 1))
                if used is not None:
                    act.wait_ge(*used)
                nc.scalar.copy(w_hi[i % 3][:, :, :], ring[:, i % RAW, :].rearrange("p (t m) -> p t m", m=P)
                               ).then_inc(w_hi_ready, 1)

            high_part(0, 0)
            for k in range(DC):
                squares(1, k)
            std(1)
            act.wait_ge(dense_done, DENSE_DOWN)
            high_part(0, 1)
            high_part(0, 2)
            for k in range(DC):
                act.wait_ge(xn_ready, DC + k + 1)
                nc.scalar.copy(x_hi[:, k, :], xn[:, k, :]).then_inc(x_hi_ready, 1)
            act.wait_ge(states_out, 2 * 16)
            act.dma_start(gk1, gk1_d).then_inc(l1_loaded, 16)
            act.dma_start(gk2, gk2_d).then_inc(l1_loaded, 16)
            act.dma_start(router, router_d).then_inc(l1_loaded, 16)
            with act.Fori(0, 2) as r:
                for i in range(SLOTS):
                    act.wait_ge(up_done, SLOTS * r + (i + 1))
                    act.wait_ge(gated, SLOTS * r + (GATED0 + i - back(i, SLOTS) + 1))
                    nc.scalar.activation(silF[:, i % 3, :], pairs[i % 3][:, 0, 0:T], ACT.Silu).then_inc(sil_done, 1)
                    j = (i + 3) % BODY
                    high_part(r + (i + 3) // BODY, j, (up_done, BODY * r + (i + 3 - back(j, BODY) + 1)))
            for u in range(2 * BODY + 3, ROUNDS * BODY):
                i = u % BODY
                high_part(u // BODY, i, split_used(u - back(i, BODY)))
            for k in range(DC - 1):
                squares(2, k)
            N = ROUNDS * BODY
            high_part(ROUNDS, 0, split_used(N - back(0, BODY)))
            squares(2, DC - 1)
            std(2)
            for i in (1, 2):
                high_part(ROUNDS, i, split_used(N + i - back(i, BODY)))
            for k in range(DC):
                act.wait_ge(xn_ready, 2 * DC + k + 1)
                nc.scalar.copy(x_hi[:, k, :], xn[:, k, :]).then_inc(x_hi_ready, 1)

            act.wait_ge(low_done, 1)
            nc.scalar.copy(low, pairs[2][0:16, 0, 0:T]).then_inc(low_copied, 1)
            for h in range(H):
                act.wait_ge(gk_done, h + 1)
                nc.scalar.activation(gx[:, h, :], pairs[h % 2][:, 0, 0:T], ACT.Identity,
                                     bias=vecs[:, V_BGK + h:V_BGK + h + 1]).then_inc(gx_ready, 1)
            act.wait_ge(gx_ready, H)
            link(nc.scalar.activation(gl, gx, ACT.Abs))
            link(nc.scalar.activation(gl, gl, ACT.Exp, scale=-1.0))
            nc.scalar.activation(gl, gl, ACT.Ln, bias=1.0).then_inc(gl_ready, 1)
            DB = DENSE_IN_O
            for o in range(16):
                act.wait_ge(dense_done, DB + o + 1)
                b = banks[(DB + o) % 2][:, 0:T]
                if o < 4:
                    nc.scalar.mul(qT[:, o, :], b, float(P) ** -0.5).then_inc(q_copied, 1)
                elif o < 8:
                    nc.scalar.copy(kT[:, o - 4, :], b).then_inc(q_copied, 1)
                else:
                    nc.scalar.copy(vT[:, o - 8, :], b).then_inc(q_copied, 1)
                if o % 2:
                    high_part(ROUNDS, o // 2 + 3, split_used(N + o // 2))
            act.wait_ge(dec_arg, 1)
            nc.scalar.activation(egS, gx[:, :, NPROMPT:T], ACT.Exp).then_inc(egs_ready, 1)

            def decay(n):
                t = [qd, *kd, qe, ke, elast][n]
                if n != NSUB + 1:
                    act.wait_ge(dec_arg, n + 1 if n <= NSUB else n)
                nc.scalar.activation(t, bT if n == NSUB + 1 else t, ACT.Exp).then_inc(dec_exp, 1)

            def value_row(b):
                if b >= 2:
                    act.wait_ge(outer_done, b - 1)
                nc.scalar.activation(vblk[:, b % 2], vtokS, ACT.Copy,
                                     scale=cst[0:NSAMP, C_ID + b:C_ID + b + 1]).then_inc(vblk_ready, 1)

            for o in range(16, 24):
                act.wait_ge(dense_done, DB + o + 1)
                nc.scalar.activation(gS[:, o - 16, :], banks[(DB + o) % 2][:, 0:T], ACT.Silu).then_inc(q_copied, 1)
                if o == 16:
                    act.wait_ge(str_done, 3)
                    nc.scalar.copy(ktokS, pairs[0][0:NSAMP, 0, :]).then_inc(str_copied, 1)
                    nc.scalar.copy(vtokS[:, 0:512], pairs[0][0:NSAMP, 1, :]).then_inc(str_copied, 1)
                    nc.scalar.copy(vtokS[:, 512:1024], pairs[1][0:NSAMP, 0, :]).then_inc(str_copied, 1)
                    act.wait_ge(str_copied, 3)
                value_row(o - 16)
                if o in (16, 19, 21):
                    for n in ((0, 1, 2), (3, 4), (5, 6, 7))[(16, 19, 21).index(o)]:
                        decay(n)
                if o == 17:
                    high_part(ROUNDS, 11, split_used(N + 8))
            act.wait_ge(so_done, NSAMP)
            nc.scalar.copy(oT[:, :, NPROMPT:T],
                           pairs[2][:, 1, 0:DC * NSAMP].rearrange("p (b a) -> p a b", a=DC)).then_inc(so_copied, 1)
            def values_as_rows(c):
                act.wait_ge(vtr_done, c + 1)
                if c >= 2:
                    act.wait_ge(kv_done, 2 * (c - 1))
                for u in range(2):
                    last = nc.scalar.copy(vtok[c % 2][:, u * 512:(u + 1) * 512], pairs[0][0:CH, u, :])
                last.then_inc(vtr_copied, 1)

            values_as_rows(0)
            for c in range(NCH):
                act.wait_ge(o_done, c + 1)
                for u in range(2):
                    last = nc.scalar.copy(oT[:, 4 * u:4 * u + 4, c * CH:(c + 1) * CH],
                                          pairs[1][:, u, 0:4 * CH].rearrange("p (a b) -> p a b", a=4))
                last.then_inc(o_copied, 1)
                if c + 1 < NCH:
                    values_as_rows(c + 1)
            act.wait_ge(so_copied, 1)
            act.wait_ge(o_copied, NCH)
            act.wait_ge(kv_done, 2 * NCH)
            for k in range(DC):
                nc.scalar.activation(sq[:, k, :], oT[:, k, :], ACT.Square).then_inc(osq_ready, 1)
            for h in range(H):
                act.wait_ge(oss_done, h + 1)
                nc.scalar.activation(rms[:, h, :], pairs[h % 2][:, 0, 0:T], ACT.Sqrt, scale=1.0 / DV,
                                     bias=cst[:, C_EPS:C_EPS + 1]).then_inc(ostd_ready, 1)
            for k in range(DC):
                squares(3, k)
            std(3)
            for b in range(NBUF):
                act.wait_ge(samp_saved[b], 16 * len(range(b, NSAMP, NBUF)))
            act.wait_ge(states_out, 3 * 16)
            act.dma_start(sel, sel_d).then_inc(sel_loaded, 16)
            act.wait_ge(shifted, 1)
            nc.scalar.activation(lg, lg, ACT.Exp).then_inc(exped, 1)
            for t in range(NRT):
                act.wait_ge(xtr_done, t + 1)
                for u in range(2):
                    last = nc.scalar.copy(xtok[:, t, u * 512:(u + 1) * 512], pairs[t % 2][0:RT, u, :])
                last.then_inc(xtr_copied, 1)
            def copy_tokens(e):
                for u in range(2):
                    act.wait_ge(gath_done, 2 * e + (u + 1))
                    nc.scalar.copy(xg[:, 4 * u:4 * u + 4, :],
                                   banks[u][:, :].rearrange("p (a b) -> p a b", a=4)).then_inc(xg_copied, 1)

            def silu(e):
                act.wait_ge(up_used, DC * e + DC)
                nc.scalar.activation(silG, pairs[0][:, :, 0:HW], ACT.Silu).then_inc(silg_done, 1)

            def copy_hidden(e):
                for u in range(2):
                    n = 4 if u == 0 else EC - 4
                    act.wait_ge(tr_done, 2 * e + (u + 1))
                    nc.scalar.copy(hG[:, 4 * u:4 * u + n, :],
                                   banks[u][:, 0:n * CAP].rearrange("p (a b) -> p a b", a=n)).then_inc(hT_copied, 1)

            def copy_output(e):
                act.wait_ge(down_used, EC * e + EC)
                for u in range(2):
                    nc.scalar.copy(yS[:, u * 512:(u + 1) * 512], pairs[2][:, u, :]).then_inc(y_copied, 1)

            copy_tokens(0)
            silu(0)
            copy_tokens(1)
            copy_hidden(0)
            copy_output(0)
            with act.Fori(1, NE - 1) as e:
                silu(e)
                copy_tokens(e + 1)
                copy_hidden(e)
                copy_output(e)
            silu(NE - 1)
            copy_hidden(NE - 1)
            copy_output(NE - 1)
            act.wait_ge(more_ready, 1)
            flag = act.value_load(more[0:1, 0:1], min_val=0, max_val=1)
            with act.If(flag):
                act.wait_ge(fb_tr, 1)
                nc.scalar.copy(gT, banks[1][0:NE, 0:T]).then_inc(fb_gT, 1)
                for e in range(NE):
                    act.wait_ge(fb_gbc, e + 1)
                    nc.scalar.copy(gbc[:, e, :], pairs[1][:, e % 2, 0:T]).then_inc(fb_copied, 1)
                with act.Fori(0, NE) as e:
                    for i in range(EC):
                        act.wait_ge(fb_up, EC * e + (i + 1))
                        nc.scalar.activation(silM, pairs[0][:, 0, 0:T], ACT.Silu).then_inc(fb_sil, 1)
                act.wait_ge(fb_x, 1 + NE * DC)
            for k in range(DC):
                act.wait_ge(x_ready, DC * (2 + NE) + k + 1)
                nc.scalar.activation(sq[:, k, :], xT[:, k, :], ACT.Square).then_inc(sq_ready, 1)
            std(4)
            for k in range(DC):
                act.wait_ge(xn_ready, 8 * 4 + k + 1)
                act.dma_start(yT_d[:, k, :], xn[:, k, :]).then_inc(y_saved, 16)
            act.wait_ge(pool_states, 2 * 16)
            act.wait_ge(y_saved, 16 * DC)

        @block.vector
        def _(dve):
            links = [0]

            def link(ins):
                links[0] += 1
                ins.then_inc(dve_link, 1)
                dve.wait_ge(dve_link, links[0])

            v = nc.vector
            scr = sq[:, :, :].rearrange("p a b -> p (a b)")

            def normalize(i):
                dve.wait_ge(std_ready, i + 1)
                link(v.reciprocal(rstd[:, :], rstd[:, :]))
                for k in range(DC):
                    w = V_NORM[i] + k
                    v.scalar_tensor_tensor(xn[:, k, :], xT[:, k, :], vecs[:, w:w + 1], rstd[:, :],
                                           ALU.mult, ALU.mult).then_inc(xn_ready, 1)

            def residual(first):
                for m in range(DC):
                    dve.wait_ge(dense_done, first + m + 1)
                    v.tensor_tensor(xT[:, m, :], xT[:, m, :], banks[m % 2][:, 0:T], ALU.add).then_inc(x_ready, 1)

            (dt, ardt, ang, mag, sn, cs, carg, lbr, lbi, fr, fi, pc, ps, t0, t1, t2, t3, t4) = (
                par[:, n] for n in range(18))
            are, aim = s5p[:, 0], s5p[:, 1]
            dve.wait_ge(s5_loaded, 16)
            dve.wait_ge(s5_dt, 1)
            v.tensor_tensor(ardt, are, dt, ALU.mult)
            link(v.tensor_tensor(ang, aim, dt, ALU.mult))
            link(v.tensor_scalar(t0, ang, 1.0 / TWO_PI, ROUND, ALU.mult, ALU.add))
            link(v.tensor_scalar(t0, t0, -ROUND, None, ALU.add))
            for part in (PI_1, PI_2, PI_3):
                link(v.scalar_tensor_tensor(ang, t0, -part, ang, ALU.mult, ALU.add))
            link(v.tensor_scalar(ang, ang, math.pi - 1e-6, -math.pi + 1e-6, ALU.min, ALU.max))
            link(v.scalar_tensor_tensor(t1, ang, -1.0, ang, ALU.mult, ALU.max))
            v.tensor_scalar(carg, t1, -1.0, math.pi / 2, ALU.mult, ALU.add).then_inc(s5_arg, 1)
            v.memset(upad[:, :, 0:16], 0.0)
            dve.wait_ge(s5_trig, 1)
            v.tensor_tensor(lbr, mag, cs, ALU.mult)
            v.tensor_tensor(lbi, mag, sn, ALU.mult)
            v.tensor_tensor(t1, are, are, ALU.mult)
            link(v.tensor_tensor(t2, aim, aim, ALU.mult))
            link(v.tensor_tensor(t1, t1, t2, ALU.add))
            link(v.reciprocal(t1, t1))
            link(v.tensor_scalar(t0, lbr, -1.0, None, ALU.add))
            v.tensor_tensor(fr, t0, are, ALU.mult)
            v.tensor_tensor(t3, lbi, aim, ALU.mult)
            v.tensor_tensor(fi, lbi, are, ALU.mult)
            link(v.tensor_tensor(t4, t0, aim, ALU.mult))
            v.tensor_tensor(fr, fr, t3, ALU.add)
            link(v.tensor_tensor(fi, fi, t4, ALU.subtract))
            v.tensor_tensor(fr, fr, t1, ALU.mult)
            v.tensor_tensor(fi, fi, t1, ALU.mult)
            v.memset(cosT[:, :, 0:1], 1.0)
            v.memset(sinT[:, :, 0:1], 0.0)
            v.tensor_copy(power(0, 0), cs)
            link(v.tensor_copy(power(0, 1), sn))
            for i in range(1, NDBL):
                pc, ps = power(i - 1, 0), power(i - 1, 1)
                v.tensor_tensor(t0, pc, pc, ALU.mult)
                v.tensor_tensor(t2, ps, ps, ALU.mult)
                link(v.scalar_tensor_tensor(power(i, 1), pc, 2.0, ps, ALU.mult, ALU.mult))
                link(v.tensor_tensor(power(i, 0), t0, t2, ALU.subtract))
            dve.wait_ge(cst_loaded, 2 * 16)
            normalize(0)
            rotation_tables(nc.vector, link, range(DBL0), 0, ST, tab_scratch[2])
            v.memset(t4, 0.0).then_inc(s5_pow, 1)
            rotation_tables(nc.vector, link, range(DBL0, NDBL), 0, TDVE, tab_scratch[0])
            def fold():
                free = ycat[:, 0:4, :].rearrange("p a b -> p (a b)")
                dve.wait_ge(late_loaded, 5 * 16)
                cr, ci = cblk[:, 0], cblk[:, 1]
                frb, fib = bc(fr.unsqueeze(2), [P, ST, 32]), bc(fi.unsqueeze(2), [P, ST, 32])
                w0 = free[:, 0:512].rearrange("p (a b) -> p a b", a=ST)
                w1 = free[:, 512:1024].rearrange("p (a b) -> p a b", a=ST)
                v.tensor_tensor(w0, cr, frb, ALU.mult)
                link(v.tensor_tensor(w1, ci, fib, ALU.mult))
                v.tensor_tensor(cf[:, 0], w0, w1, ALU.subtract)
                link(v.tensor_tensor(cf[:, 1], w1, w0, ALU.subtract))
                v.tensor_tensor(w0, cr, fib, ALU.mult)
                link(v.tensor_tensor(w1, ci, frb, ALU.mult))
                link(v.tensor_tensor(w0, w0, w1, ALU.add))
                v.tensor_scalar(cf[:, 2], w0, -1.0, None, ALU.mult).then_inc(s5_folded, 1)

            def windows():
                dve.wait_ge(u_copied, 8)
                cnt = cst[:, C_CNT:C_CNT + 64].rearrange("p (g t) -> p g t", g=NG)
                L = 16 + NPROMPT
                cur = upad
                bufs = [xn[:, :, :].rearrange("p a b -> p (a b)")[:, 0:4 * L].rearrange("p (g t) -> p g t", g=4),
                        scr[:, 4 * NPROMPT:4 * NPROMPT + 3 * L].rearrange("p (g t) -> p g t", g=3)]
                for g in range(NG):
                    w = 1 << g
                    new = bufs[0][:, g:4, :] if g % 2 == 0 else bufs[1][:, g - 1:3, :]
                    old = cur[:, 1:, :] if g else upad
                    s0 = 2 * w - 1
                    link(v.tensor_tensor(new[:, :, s0:], old[:, :, s0:], old[:, :, s0 - w:L - w], ALU.add))
                    link(v.tensor_scalar(ycat[:, g, 0:NPROMPT], new[:, 0, 16:], 1.0 / (2 * w), None, ALU.mult))
                    link(v.tensor_tensor(ycat[:, g, 0:16], new[:, 0, 16:32], cnt[:, g, :], ALU.mult))
                    link(v.tensor_tensor(ycat[:, g, 0:NPROMPT], ycat[:, g, 0:NPROMPT], upad[:, g, 16:],
                                         ALU.subtract))
                    link(v.tensor_reduce(t4[:, 0:NSAMP], pbuf[:, g, :, 16 - 2 * w:], AX.X, ALU.add))
                    v.scalar_tensor_tensor(ycat[:, g, NPROMPT:T], t4[:, 0:NSAMP], 1.0 / (2 * w), pbuf[:, g, :, PAST],
                                           ALU.mult, ALU.subtract).then_inc(d_ready, 1)
                    cur = new

            def skip(c):
                dve.wait_ge(y_done, 4 * c + 4)
                if c == 0:
                    dve.wait_ge(pool_states, 2 * 16)
                v.scalar_tensor_tensor(z[:, c, 0:NPROMPT], ycat[:, 4 + c, 0:NPROMPT], vecs[:, V_D + c:V_D + c + 1],
                                       pairs[2][:, c % 2, 0:NPROMPT], ALU.mult, ALU.add).then_inc(yp_out, 1)

            dve.wait_ge(late_loaded, 5 * 16)
            def scan(j):
                if j >= 2:
                    dve.wait_ge(back_done, j - 1)
                dve.wait_ge(rot_ready, j + 1)
                g = scanned[:, j % 2]
                m = bc(mag[:, j:j + 1], [P, NPROMPT])
                v.tensor_tensor_scan(g[:, 0], m, rotA[:, j % 2, 0], 0.0, ALU.mult, ALU.add)
                v.tensor_tensor_scan(g[:, 1], m, rotA[:, j % 2, 1], 0.0, ALU.mult, ALU.add).then_inc(scan_done, 1)

            def last_state(j):
                dve.wait_ge(scan_done, j + 1)
                v.tensor_copy(glast[:, :, j:j + 1], scanned[:, j % 2, :, NPROMPT - 1:])

            for j in range(ST):
                if j == TDVE:
                    dve.wait_ge(pool_link, 4 * (NDBL - DBL0))
                dve.wait_ge(bu_done, j + 1)
                src = pairs[j % 2][:, :, 0:NPROMPT]
                A, B = rotA[:, j % 2], rotB[:, j % 2]
                v.tensor_copy(buS[:, :, j, :], pairs[j % 2][:, :, NPROMPT:T])
                v.tensor_tensor(A, src, bc(cosT[:, j:j + 1, :], [P, 2, NPROMPT]), ALU.mult)
                v.tensor_tensor(B, src, bc(sinT[:, j:j + 1, :], [P, 2, NPROMPT]), ALU.mult).then_inc(bu_rot, 1)
                if j:
                    scan(j - 1)
                dve.wait_ge(bu_rot, j + 1)
                v.tensor_tensor(A[:, 0], A[:, 0], B[:, 1], ALU.add)
                v.tensor_tensor(A[:, 1], A[:, 1], B[:, 0], ALU.subtract).then_inc(rot_ready, 1)
                if j:
                    last_state(j - 1)
                if j == 1:
                    fold()
                if j == 6:
                    windows()
                if j % 4 == 1 and j >= 9:
                    skip(j // 4 - 2)
            scan(ST - 1)
            last_state(ST - 1)
            shp = [P, ST, NSAMP]
            q = [scr[:, 128 * n:128 * n + 128].rearrange("p (a b) -> p a b", a=ST) for n in range(8)]

            def wide(a):
                return bc(a.unsqueeze(2), shp)

            v.tensor_tensor(q[0], h0[:, 0], wide(lbr), ALU.mult)
            v.tensor_tensor(q[1], h0[:, 1], wide(lbi), ALU.mult)
            v.tensor_tensor(q[2], buS[:, 0], wide(fr), ALU.mult)
            v.tensor_tensor(q[3], buS[:, 1], wide(fi), ALU.mult)
            v.tensor_tensor(q[4], h0[:, 1], wide(lbr), ALU.mult)
            v.tensor_tensor(q[5], h0[:, 0], wide(lbi), ALU.mult)
            v.tensor_tensor(q[6], buS[:, 1], wide(fr), ALU.mult)
            link(v.tensor_tensor(q[7], buS[:, 0], wide(fi), ALU.mult))
            v.tensor_tensor(q[0], q[0], q[1], ALU.subtract)
            v.tensor_tensor(q[2], q[2], q[3], ALU.subtract)
            v.tensor_tensor(q[4], q[4], q[5], ALU.add)
            link(v.tensor_tensor(q[6], q[6], q[7], ALU.add))
            v.tensor_tensor(hS[:, 0], q[0], q[2], ALU.add)
            link(v.tensor_tensor(hS[:, 1], q[4], q[6], ALU.add))
            v.tensor_scalar(nhi, hS[:, 1], -1.0, None, ALU.mult).then_inc(hs_ready, 1)
            cL, sL = cosT[:, :, NPROMPT - 1], sinT[:, :, NPROMPT - 1]

            def times(a, b):
                v.tensor_tensor(t0, glast[:, 0], a, ALU.mult)
                v.tensor_tensor(t1, glast[:, 1], b, ALU.mult)
                v.tensor_tensor(t2, glast[:, 0], b, ALU.mult)
                link(v.tensor_tensor(t3, glast[:, 1], a, ALU.mult))
                v.tensor_tensor(glast[:, 0], t0, t1, ALU.subtract)
                return v.tensor_tensor(glast[:, 1], t2, t3, ALU.add)

            link(times(cL, sL))
            times(fr, fi).then_inc(s5_states, 1)
            skip(2)
            skip(3)
            dve.wait_ge(ys_done, 1)
            for c in range(4):
                v.scalar_tensor_tensor(z[:, c, NPROMPT:T], ycat[:, 4 + c, NPROMPT:T], vecs[:, V_D + c:V_D + c + 1],
                                       pairs[0][:, 0, c * NSAMP:(c + 1) * NSAMP], ALU.mult, ALU.add
                                       ).then_inc(y_out, 1)
            for m in range(4):
                dve.wait_ge(sig_ready, m + 1)
                v.tensor_tensor(ycat[:, 4 + m, :], z[:, m, :], sig[:, m % 2, :], ALU.mult).then_inc(gated, 1)
            residual(DENSE_OUT)
            normalize(1)
            for k in range(DC):
                dve.wait_ge(x_hi_ready, k + 1)
                v.tensor_tensor(x_lo[:, k, :], xn[:, k, :], x_hi[:, k, :].bitcast(F32), ALU.subtract
                                ).then_inc(x_lo_ready, 1)
            with dve.Fori(0, 2) as r:
                for i in range(SLOTS):
                    dve.wait_ge(sil_done, SLOTS * r + (i + 1))
                    v.tensor_tensor(hF[:, i % 3, :], silF[:, i % 3, :], pairs[i % 3][:, 1, 0:T], ALU.mult
                                    ).then_inc(gated, 1)
                    dve.wait_ge(gated, SLOTS * r + (GATED0 + i + 1))
                    hi = h_hi[:, bass.ds(SLOTS * r + i, 1), :].rearrange("p a b -> p (a b)")
                    lo = h_lo[:, bass.ds(SLOTS * r + i, 1), :].rearrange("p a b -> p (a b)")
                    v.tensor_copy(hi, hF[:, i % 3, :]).then_inc(h_hi_ready, 1)
                    dve.wait_ge(h_hi_ready, SLOTS * r + (i + 1))
                    v.tensor_tensor(lo, hF[:, i % 3, :], hi.bitcast(F32), ALU.subtract).then_inc(h_lo_ready, 1)
            residual(DENSE_DOWN)
            normalize(2)
            dve.wait_ge(low_done, 1)
            for k in range(DC):
                dve.wait_ge(x_hi_ready, DC + k + 1)
                v.tensor_tensor(x_lo[:, k, :], xn[:, k, :], x_hi[:, k, :].bitcast(F32), ALU.subtract
                                ).then_inc(x_lo_ready, 1)

            dve.wait_ge(gl_ready, 1)
            link(v.scalar_tensor_tensor(gx, gx, 0.0, gl, ALU.min, ALU.subtract))
            link(v.tensor_scalar(gx, gx, 1.0 / 16.0, None, ALU.mult))
            for h in range(H):
                last = v.tensor_tensor_scan(bT[:, h, :], cst[:, C_RESET:C_RESET + NPROMPT], gx[:, h, 0:NPROMPT], 0.0,
                                            ALU.mult, ALU.add)
            link(last)
            b_sub = bT.rearrange("p h (n s) -> p (h n) s", s=SUB)
            b_ch = bT.rearrange("p h (n s) -> p (h n) s", s=CH)
            HN = H * NCH
            v.tensor_tensor(qd.rearrange("p h (n s) -> p (h n) s", s=SUB), b_sub,
                            bc(b_sub[:, :, MID:MID + 1], [P, HN * NSUB, SUB]), ALU.subtract).then_inc(dec_arg, 1)
            for i in range(NSUB):
                w = SUB * (i + 1)
                r = SUB * i + MID
                v.tensor_tensor(kd[i].rearrange("p h (n s) -> p (h n) s", s=w), bc(b_ch[:, :, r:r + 1], [P, HN, w]),
                                b_ch[:, :, 0:w], ALU.subtract).then_inc(dec_arg, 1)
            v.tensor_tensor(ke.rearrange("p h (n s) -> p (h n) s", s=CH), bc(b_ch[:, :, CH - 1:CH], [P, HN, CH]),
                            b_ch, ALU.subtract).then_inc(dec_arg, 1)
            v.tensor_copy(elast.rearrange("p h n -> p (h n)").unsqueeze(2), b_ch[:, :, CH - 1:CH]).then_inc(dec_arg, 1)
            def decayed(n):
                dve.wait_ge(dec_exp, n + 1)
                if n == 0:
                    v.tensor_tensor(qd, qd, qT[:, :, 0:NPROMPT], ALU.mult).then_inc(dec_ready, 1)
                elif n <= NSUB:
                    w = SUB * n
                    k3 = kd[n - 1].rearrange("p h (n s) -> p h n s", s=w)
                    v.tensor_tensor(k3, k3, k4[:, :, :, 0:w], ALU.mult).then_inc(dec_ready, 1)
                elif n == NSUB + 1:
                    v.tensor_tensor(qe, qe, qT[:, :, 0:NPROMPT], ALU.mult).then_inc(dec_ready, 1)
                else:
                    v.tensor_tensor(ke, ke, kT[:, :, 0:NPROMPT], ALU.mult).then_inc(dec_ready, 1)

            k4 = kT[:, :, 0:NPROMPT].rearrange("p h (n s) -> p h n s", s=CH)
            dve.wait_ge(q_copied, 8)
            for b in range(NSAMP):
                if b < NSUB + 3:
                    decayed(b)
                if b == 0:
                    dve.wait_ge(egs_ready, 1)
                dve.wait_ge(samp_loaded[b % NBUF], 16 * (b // NBUF + 1))
                dve.wait_ge(outer_done, b + 1)
                for h in range(H):
                    last = v.scalar_tensor_tensor(samp[:, b % NBUF, h, :], samp[:, b % NBUF, h, :], egS[:, h, b:b + 1],
                                                  pairs[b % 2][:, h // 2, (h % 2) * DV:(h % 2 + 1) * DV],
                                                  ALU.mult, ALU.add)
                last.then_inc(samp_ready, 1)
            dve.wait_ge(dec_exp, NSUB + 4)
            link(v.memset(attS, 0.0))
            def mask_scores(c):
                if c >= 2:
                    dve.wait_ge(o_done, c - 1)
                dve.wait_ge(att_done, NSUB * (c + 1))
                for i in range(NSUB):
                    w = SUB * (i + 1)
                    a = pairs[2][0:w, 1, 0:H * CH].rearrange("p (h t) -> p h t", h=H)[:, :, SUB * i:w]
                    m = bc(cst[0:w, C_MASK + SUB * i:C_MASK + w].unsqueeze(1), [w, H, SUB])
                    v.tensor_tensor(attS[0:w, c % 2, :, SUB * i:w], a, m, ALU.mult).then_inc(att_copied, 1)

            def keys_as_rows(c):
                dve.wait_ge(ktr_done, c + 1)
                if c:
                    dve.wait_ge(kv_done, 2 * c)
                v.tensor_copy(ketok, pairs[2][0:CH, 0, :]).then_inc(ktr_copied, 1)

            mask_scores(0)
            keys_as_rows(0)
            for c in range(NCH):
                if c + 1 < NCH:
                    mask_scores(c + 1)
                for h in range(H):
                    dve.wait_ge(kv_done, 2 * c + h // 2 + 1)
                    kv = banks[h // 2][:, (h % 2) * DV:(h % 2 + 1) * DV]
                    if c == 0:
                        v.tensor_copy(S[:, h, :], kv).then_inc(S_ready, 1)
                    else:
                        if h == 0:
                            dve.wait_ge(S_ready, H * c)
                        v.scalar_tensor_tensor(S[:, h, :], S[:, h, :], elast[:, h, c:c + 1], kv,
                                               ALU.mult, ALU.add).then_inc(S_ready, 1)
                if c + 1 < NCH:
                    keys_as_rows(c + 1)
            dve.wait_ge(q_copied, 24)
            dve.wait_ge(so_copied, 1)
            dve.wait_ge(o_copied, NCH)
            for k in range(DC):
                last = v.scalar_tensor_tensor(oG[:, k, :], oT[:, k, :], vecs[:, V_GNORM + k % VC:V_GNORM + k % VC + 1],
                                              gS[:, k, :], ALU.mult, ALU.mult)
            link(last)
            for h in range(H + 1):
                if h < H:
                    dve.wait_ge(ostd_ready, h + 1)
                    v.reciprocal(rms[:, h, :], rms[:, h, :]).then_inc(rms_ready, 1)
                if h:
                    dve.wait_ge(rms_ready, h)
                    v.tensor_tensor(oG[:, VC * (h - 1):VC * h, :], oG[:, VC * (h - 1):VC * h, :],
                                    bc(rms[:, h - 1:h, :], [P, VC, T]), ALU.mult).then_inc(og_ready, 1)
            residual(DENSE_OUT_O)
            normalize(3)
            shp = [RT, NRT, NE]
            mx, sm, den = (rsc[:, n] for n in range(3))
            iota = bc(cst[0:RT, C_IOTA:C_IOTA + NE].unsqueeze(1), shp)
            own = bc(cst[0:RT, C_OWN:C_OWN + NRT].unsqueeze(2), shp)
            for b in range(NBUF):
                dve.wait_ge(samp_saved[b], 16 * len(range(b, NSAMP, NBUF)))
            dve.wait_ge(states_out, 3 * 16)
            v.memset(onesT, 1.0)
            dve.wait_ge(logit_done, 1)
            lp = banks[0][0:RT, 0:NRT * NE].rearrange("p (t e) -> p t e", t=NRT)
            link(v.tensor_reduce(mx, lp, AX.X, ALU.max))
            v.tensor_tensor(lg, lp, bc(mx.unsqueeze(2), shp), ALU.subtract).then_inc(shifted, 1)
            dve.wait_ge(exped, 1)
            link(v.tensor_reduce(sm, lg, AX.X, ALU.add))
            link(v.reciprocal(sm, sm))
            link(v.tensor_tensor(pr, lg, bc(sm.unsqueeze(2), shp), ALU.mult))
            for t in range(NRT):
                last = v.max(mx8[:, t, :], pr[:, t, :])
            link(last)
            for t in range(NRT):
                last = v.max_index(idx[:, t * 8:(t + 1) * 8], mx8[:, t, :], pr[:, t, :])
            link(last)
            link(v.tensor_copy(ix.rearrange("p t e -> p (t e)"), idx[:, :]))
            v.tensor_tensor(gates, iota, bc(ix[:, :, 0:1], shp), ALU.is_equal)
            link(v.tensor_tensor(oh2, iota, bc(ix[:, :, 1:2], shp), ALU.is_equal))
            v.tensor_tensor(taken, gates, oh2, ALU.add).then_inc(taken_ready, 1)
            link(v.tensor_tensor(den, mx8[:, :, 0], mx8[:, :, 1], ALU.add))
            link(v.reciprocal(den, den))
            v.tensor_tensor(gates, gates, bc(mx8[:, :, 0:1], shp), ALU.mult)
            link(v.tensor_tensor(oh2, oh2, bc(mx8[:, :, 1:2], shp), ALU.mult))
            link(v.tensor_tensor(gates, gates, oh2, ALU.add))
            link(v.tensor_tensor(gates, gates, bc(den.unsqueeze(2), shp), ALU.mult))
            dve.wait_ge(mtr_done, 1)
            link(v.tensor_copy(mT, banks[1][0:NE, 0:T]))
            link(v.tensor_tensor_scan(posT, onesT, mT, 0.0, ALU.mult, ALU.add))
            link(v.tensor_tensor(mT, mT, posT, ALU.mult))
            v.tensor_scalar(mT, mT, -1.0, None, ALU.add).then_inc(pos_ready, 1)
            dve.wait_ge(ptr_done, 1)
            link(v.tensor_scalar(postok, banks[0][0:RT, 0:NRT * NE].rearrange("p (t e) -> p t e", t=NRT),
                                 1.0, None, ALU.add))
            link(v.tensor_tensor(postok, postok, own, ALU.mult))
            link(v.tensor_scalar(postok, postok, -1.0, None, ALU.add))
            link(v.tensor_reduce(top, banks[0][0:1, 64:64 + NE], AX.X, ALU.max))
            link(v.tensor_scalar(top, top, float(CAP), None, ALU.is_gt))
            v.tensor_copy(more[0:1, 0:1], top).then_inc(more_ready, 1)
            link(v.tensor_scalar(gover, postok, float(CAP), None, ALU.is_ge))
            link(v.tensor_tensor(gover, gover, gates, ALU.mult))

            def make_pick(e):
                v.tensor_tensor(pick, bc(cst[0:RT, C_IOTA:C_IOTA + CAP].unsqueeze(1), [RT, NRT, CAP]),
                                bc(postok[:, :, bass.ds(e, 1)], [RT, NRT, CAP]), ALU.is_equal).then_inc(pick_ready, 1)

            def copy_gates(e, first=False):
                if not first:
                    dve.wait_ge(hidden_ready, e)
                dve.wait_ge(gate_done, e + 1)
                v.tensor_copy(gslot, pairs[2][:, 0, 0:1]).then_inc(gate_copied, 1)

            def hidden(e):
                dve.wait_ge(gate_copied, e + 1)
                dve.wait_ge(silg_done, e + 1)
                v.scalar_tensor_tensor(hs, pairs[1][:, :, 0:HW], gslot[:, 0:1], silG, ALU.mult, ALU.mult
                                       ).then_inc(hidden_ready, 1)

            def add_output(e):
                for m in range(DC):
                    dve.wait_ge(sc_done, DC * e + (m + 1))
                    v.tensor_tensor(xT[:, m, :], xT[:, m, :], banks[m % 2][:, 0:T], ALU.add).then_inc(x_ready, 1)

            make_pick(0)
            copy_gates(0, first=True)
            for e in range(NE):
                dve.wait_ge(pbc_done, e + 1)
                v.tensor_scalar(selT[:, e, :], pairs[2][:, e % 2, 0:T], cst[:, C_SLOT:C_SLOT + 1], None,
                                ALU.is_equal).then_inc(selT_ready, 1)
            dve.wait_ge(gath_done, 2)
            make_pick(1)
            hidden(0)
            copy_gates(1)
            with dve.Fori(1, NE - 1) as e:
                dve.wait_ge(gath_done, 2 * e + 2)
                make_pick(e + 1)
                add_output(e - 1)
                hidden(e)
                copy_gates(e + 1)
            add_output(NE - 2)
            hidden(NE - 1)
            add_output(NE - 1)
            flag = dve.value_load(more[0:1, 0:1], min_val=0, max_val=1)
            with dve.If(flag):
                v.memset(base[:, 0:1], 0.0).then_inc(fb_gated, 1)
                v.memset(base[:, 1:2], 0.0).then_inc(fb_x, 1)
                dve.wait_ge(fb_copied, NE)
                with dve.Fori(0, NE) as e:
                    for i in range(EC):
                        dve.wait_ge(fb_sil, EC * e + (i + 1))
                        v.tensor_tensor(gpre, silM, pairs[0][:, 1, 0:T], ALU.mult).then_inc(fb_gpre, 1)
                        dve.wait_ge(fb_gpre, EC * e + (i + 1))
                        v.tensor_tensor(hM[:, i, :], gpre, gbc[:, bass.ds(e, 1), :].rearrange("p a b -> p (a b)"),
                                        ALU.mult).then_inc(fb_gated, 1)
                    for m in range(DC):
                        dve.wait_ge(fb_down, DC * e + (m + 1))
                        v.tensor_tensor(xT[:, m, :], xT[:, m, :], banks[m % 2][:, 0:T], ALU.add).then_inc(fb_x, 1)
            normalize(4)

        @block.tensor
        def _(pe):
            mm = nc.tensor.matmul

            def slot(n):
                return ring[:, slot_of(n), :].rearrange("p (t m) -> p t m", m=P)

            def unit_loaded(n):
                pe.wait_ge(slot_full[slot_of(n)], 16 if n < FFN_UP else 32)

            def split_product(out, i, tile, hi, lo, start, stop):
                wh, wl = w_hi[i % 3][:, tile, :], w_lo[i % 3][:, tile, :]
                mm(out, wh, hi, start=start, stop=False)
                mm(out, wh, lo, start=False, stop=False)
                return mm(out, wl, hi, start=False, stop=stop)

            def bank_free(d):
                if d < 2:
                    return
                if d < DENSE_POOL + 2:
                    pe.wait_ge(u_copied, d - 1)
                elif d < DENSE_GLU + 2:
                    pe.wait_ge(pool_out, d - DENSE_POOL - 1)
                elif d < DENSE_OUT + 2:
                    pe.wait_ge(sig_ready, d - DENSE_GLU - 1)
                elif d < DENSE_IN_O + 2:
                    pe.wait_ge(x_ready, d - DENSE_OUT - 1)
                elif d < DENSE_OUT_O + 2:
                    pe.wait_ge(q_copied, d - DENSE_IN_O - 1)
                else:
                    pe.wait_ge(x_ready, d - DENSE_OUT_O - 1 + 16)

            def dense(d, unit, tile, kc, rhs, ready=None):
                bank_free(d)
                for k in range(kc):
                    n = unit + (tile + k) // UT
                    if k == 0 or (tile + k) % UT == 0:
                        unit_loaded(n)
                    if ready is not None:
                        pe.wait_ge(ready[0], ready[1](k) if callable(ready[1]) else ready[1] + k + 1)
                    last = mm(banks[d % 2][:, 0:T], slot(n)[:, (tile + k) % UT, :], rhs[:, k, :],
                              start=(k == 0), stop=(k == kc - 1))
                last.then_inc(dense_done, 1)

            def sum_squares(i):
                for k in range(DC):
                    pe.wait_ge(sq_ready, DC * i + k + 1)
                    last = mm(pairs[2][:, 1, 0:T], ones, sq[:, k, :], start=(k == 0), stop=(k == DC - 1))
                last.then_inc(ss_ready, 1)

            pe.wait_ge(cst_loaded, 2 * 16)
            sum_squares(0)

            def project_in(o):
                dense(o, W_IN_E, DC * o, DC, xn, (xn_ready, 0) if o == 0 else None)

            project_in(0)
            project_in(1)
            pe.wait_ge(late_loaded, 5 * 16)

            def y_tile(j):
                c, r = j // 4, 32 * (j % 4)
                if j == 0:
                    pe.wait_ge(s5_folded, 1)
                if j % 4 == 0 and c >= 2:
                    pe.wait_ge(yp_out, c - 1)
                pe.wait_ge(back_done, j + 1)
                out = pairs[2][r:r + 32, c % 2, 0:NPROMPT]
                mm(out, cf[:, 0, j, :], backC[:, j % 2, 0], start=True, stop=False)
                mm(out, cf[:, 1, j, :], backS[:, j % 2, 1], start=False, stop=False)
                mm(out, cf[:, 2, j, :], backS[:, j % 2, 0], start=False, stop=False)
                mm(out, cf[:, 2, j, :], backC[:, j % 2, 1], start=False, stop=True).then_inc(y_done, 1)

            for j in range(ST):
                c, r = j // 4, 32 * (j % 4)
                if j % 4 == 0:
                    pe.wait_ge(u_copied, c + 1)
                if j >= 2:
                    pe.wait_ge(bu_rot, j - 1)
                for x in range(2):
                    last = mm(pairs[j % 2][:, x, 0:T], bblk[r:r + 32, c, x, :], ycat[r:r + 32, 4 + c, :],
                              start=True, stop=True)
                last.then_inc(bu_done, 1)
                if j < 6:
                    project_in(2 + j)
                if 8 <= j < 12:
                    g = j - 8
                    pe.wait_ge(d_ready, g + 1)
                    bank_free(DENSE_POOL + g)
                    mm(banks[g % 2][:, 0:T], wpool[:, g, :], ycat[:, g, :], start=True, stop=True
                       ).then_inc(dense_done, 1)
                if j >= 3:
                    y_tile(j - 3)
            for j in range(ST - 3, ST):
                y_tile(j)
            pe.wait_ge(hs_ready, 1)
            for j in range(ST):
                c, r = j // 4, 32 * (j % 4)
                out = pairs[0][r:r + 32, 0, c * NSAMP:(c + 1) * NSAMP]
                mm(out, cblk[:, 0, j, :], hS[:, 0, j, :], start=True, stop=False)
                last = mm(out, cblk[:, 1, j, :], nhi[:, j, :], start=False, stop=True)
            last.then_inc(ys_done, 1)
            for m in range(4):
                dense(DENSE_GLU + m, W_GLU, 4 * m, 4, z, (z_ready, 0) if m == 0 else None)
            for m in range(DC):
                if m == 0:
                    pe.wait_ge(pool_out, 4)
                    pe.wait_ge(gated, 4)
                dense(DENSE_OUT + m, W_OUT_E, DC * m, DC, ycat)
            sum_squares(1)
            pe.wait_ge(x_lo_ready, DC)
            with pe.Fori(0, 2) as r:
                for i in range(SLOTS):
                    pe.wait_ge(w_lo_ready, BODY * r + (i + 1))
                    pe.wait_ge(gated, SLOTS * r + (GATED0 + i - back(i, SLOTS) + 1))
                    for x in range(2):
                        for k in range(DC):
                            last = split_product(pairs[i % 3][:, x, 0:T], i, DC * x + k, x_hi[:, k, :], x_lo[:, k, :],
                                                 k == 0, k == DC - 1)
                    last.then_inc(up_done, 1)
            pe.wait_ge(h_lo_ready, FC)
            for m in range(DC):
                bank_free(DENSE_DOWN + m)
                for k in range(FC):
                    u, tile = divmod(FC * m + k, UT)
                    if tile == 0 or k == 0:
                        pe.wait_ge(w_lo_ready, FC + u + 1)
                    last = split_product(banks[m % 2][:, 0:T], u, tile, h_hi[:, k, :], h_lo[:, k, :],
                                         k == 0, k == FC - 1)
                    if tile == UT - 1 and k < FC - 1:
                        last.then_inc(down_unit, 1)
                last.then_inc(dense_done, 1)
            sum_squares(2)
            pe.wait_ge(l1_loaded, 3 * 16)
            for k in range(DC):
                pe.wait_ge(xn_ready, 2 * DC + k + 1)
                last = mm(pairs[2][0:16, 0, 0:T], gk1[:, k, :], xn[:, k, :], start=(k == 0), stop=(k == DC - 1))
            last.then_inc(low_done, 1)
            pe.wait_ge(low_copied, 1)
            for h in range(H):
                if h >= 2:
                    pe.wait_ge(gx_ready, h - 1)
                mm(pairs[h % 2][:, 0, 0:T], gk2[:, h * P:(h + 1) * P], low, start=True, stop=True
                   ).then_inc(gk_done, 1)
            def project_qkvg(o):
                bank_free(DENSE_IN_O + o)
                pe.wait_ge(w_lo_ready, ROUNDS * BODY + o // 2 + 1)
                for k in range(DC):
                    if o == 0:
                        pe.wait_ge(x_lo_ready, DC + k + 1)
                    last = split_product(banks[(DENSE_IN_O + o) % 2][:, 0:T], o // 2, DC * (o % 2) + k,
                                         x_hi[:, k, :], x_lo[:, k, :], k == 0, k == DC - 1)
                last.then_inc(dense_done, 1)

            for o in range(17):
                project_qkvg(o)
            pe.wait_ge(q_copied, 16)
            for part in range(3):
                for k in range(4):
                    src = kT[:, k, NPROMPT:T] if part == 0 else vT[:, 4 * (part - 1) + k, NPROMPT:T]
                    dst = (pairs[0][0:NSAMP, 0], pairs[0][0:NSAMP, 1], pairs[1][0:NSAMP, 0])[part]
                    last = nc.tensor.transpose(dst[:, k * P:(k + 1) * P], src, ident)
                last.then_inc(str_done, 1)

            def sample_output(b):
                pe.wait_ge(samp_ready, b + 1)
                for k in range(DC):
                    last = mm(pairs[2][:, 1, b * DC + k:b * DC + k + 1],
                              samp[:, b % NBUF, k // VC, (k % VC) * P:(k % VC + 1) * P],
                              qT[:, k // VC, NPROMPT + b:NPROMPT + b + 1], start=True, stop=True)
                last.then_inc(so_done, 1)

            for b in range(NSAMP):
                if 17 + b < 24:
                    project_qkvg(17 + b)
                pe.wait_ge(vblk_ready, b + 1)
                if b >= 2:
                    pe.wait_ge(samp_ready, b - 1)
                for h in range(H):
                    last = mm(pairs[b % 2][:, h // 2, (h % 2) * DV:(h % 2 + 1) * DV], ktokS[:, h * P:(h + 1) * P],
                              vblk[:, b % 2, h * DV:(h + 1) * DV], start=True, stop=True)
                last.then_inc(outer_done, 1)
                if b:
                    sample_output(b - 1)
            sample_output(NSAMP - 1)

            def scores(c):
                for i in range(NSUB):
                    w = SUB * (i + 1)
                    if c == 0:
                        pe.wait_ge(dec_ready, i + 2)
                    if c and i == 0:
                        pe.wait_ge(att_copied, NSUB * c)
                    for h in range(H):
                        last = mm(pairs[2][0:w, 1, h * CH + SUB * i:h * CH + w], kd[i][:, h, c * w:(c + 1) * w],
                                  qd[:, h, c * CH + SUB * i:c * CH + w], start=True, stop=True)
                    last.then_inc(att_done, 1)

            def value_rows(c):
                if c:
                    pe.wait_ge(vtr_copied, c)
                for k in range(DC):
                    last = nc.tensor.transpose(pairs[0][0:CH, k // 4, (k % 4) * P:(k % 4 + 1) * P],
                                               vT[:, k, c * CH:(c + 1) * CH], ident)
                last.then_inc(vtr_done, 1)

            def key_rows(c):
                if c:
                    pe.wait_ge(ktr_copied, c)
                else:
                    pe.wait_ge(dec_ready, 7)
                for h in range(H):
                    last = nc.tensor.transpose(pairs[2][0:CH, 0, h * P:(h + 1) * P],
                                               ke[:, h, c * CH:(c + 1) * CH], ident)
                last.then_inc(ktr_done, 1)

            def chunk_output(c):
                pe.wait_ge(att_copied, NSUB * (c + 1))
                pe.wait_ge(vtr_copied, c + 1)
                if c:
                    pe.wait_ge(o_copied, c)
                    pe.wait_ge(S_ready, H * c)
                for k in range(DC):
                    h = k // VC
                    out = pairs[1][:, k // 4, (k % 4) * CH:(k % 4 + 1) * CH]
                    last = mm(out, vtok[c % 2][:, k * P:(k + 1) * P], attS[:, c % 2, h, :], start=True, stop=(c == 0))
                    if c:
                        last = mm(out, S[:, h, (k % VC) * P:(k % VC + 1) * P], qe[:, h, c * CH:(c + 1) * CH],
                                  start=False, stop=True)
                last.then_inc(o_done, 1)

            def state_update(c):
                pe.wait_ge(ktr_copied, c + 1)
                for h in range(H):
                    last = mm(banks[h // 2][:, (h % 2) * DV:(h % 2 + 1) * DV], ketok[:, h * P:(h + 1) * P],
                              vtok[c % 2][:, h * DV:(h + 1) * DV], start=True, stop=True)
                    if h % 2:
                        last.then_inc(kv_done, 1)

            key_rows(0)
            value_rows(0)
            pe.wait_ge(so_copied, 1)
            scores(0)
            pe.wait_ge(q_copied, 24)
            for c in range(NCH):
                chunk_output(c)
                if c + 1 < NCH:
                    scores(c + 1)
                    value_rows(c + 1)
                state_update(c)
                if c + 1 < NCH:
                    key_rows(c + 1)
            for h in range(H):
                pe.wait_ge(osq_ready, VC * (h + 1))
                if h >= 2:
                    pe.wait_ge(ostd_ready, h - 1)
                for c in range(VC):
                    last = mm(pairs[h % 2][:, 0, 0:T], ones, sq[:, VC * h + c, :], start=(c == 0), stop=(c == VC - 1))
                last.then_inc(oss_done, 1)
            for m in range(DC):
                dense(DENSE_OUT_O + m, W_OUT_O, DC * m, DC, oG, (og_ready, lambda k: k // VC + 1) if m == 0 else None)
            sum_squares(3)
            pe.wait_ge(xn_ready, 4 * DC)
            for t in range(NRT):
                for k in range(DC):
                    last = mm(banks[0][0:RT, t * NE:(t + 1) * NE], xn[:, k, RT0[t]:RT0[t] + RT], router[:, k, :],
                              start=(k == 0), stop=(k == DC - 1))
            last.then_inc(logit_done, 1)
            for t in range(NRT):
                if t >= 2:
                    pe.wait_ge(xtr_copied, t - 1)
                for k in range(DC):
                    last = nc.tensor.transpose(pairs[t % 2][0:RT, k // 4, (k % 4) * P:(k % 4 + 1) * P],
                                               xn[:, k, RT0[t]:RT0[t] + RT], ident)
                last.then_inc(xtr_done, 1)

            def expert_rows(src):
                for t in (NRT - 1, *range(NRT - 1)):
                    last = nc.tensor.transpose(banks[1][0:NE, RT0[t]:RT0[t] + RT], src[:, t, :],
                                               cst[0:RT, C_ID:C_ID + RT])
                return last

            pe.wait_ge(taken_ready, 1)
            expert_rows(taken).then_inc(mtr_done, 1)
            pe.wait_ge(pos_ready, 1)
            for t in range(NRT):
                nc.tensor.transpose(banks[0][0:RT, t * NE:(t + 1) * NE], mT[:, RT0[t]:RT0[t] + RT],
                                    cst[0:NE, C_ID:C_ID + NE])
            nc.tensor.transpose(banks[0][0:1, 64:64 + NE], posT[:, T - 1:T], cst[0:NE, C_ID:C_ID + NE]
                                ).then_inc(ptr_done, 1)
            def gather(e):
                pe.wait_ge(pick_ready, e + 1)
                for t in range(NRT):
                    last = mm(pairs[2][:, 0, 0:1], pick[:, t, :], gates[:, t, bass.ds(e, 1)],
                              start=(t == 0), stop=(t == NRT - 1))
                last.then_inc(gate_done, 1)
                for k in range(DC):
                    for t in range(NRT):
                        last = mm(banks[k // 4][:, (k % 4) * CAP:(k % 4 + 1) * CAP], xtok[:, t, k * P:(k + 1) * P],
                                  pick[:, t, :], start=(t == 0), stop=(t == NRT - 1))
                    if k % 4 == 3:
                        last.then_inc(gath_done, 1)

            def up(e, scatter=False):
                for k in range(DC):
                    if k % 4 == 0:
                        pe.wait_ge(xg_copied, 2 * e + (k // 4 + 1))
                    pe.wait_ge(up_full[k], 16 * e + 16)
                    for x in range(2):
                        for u in range(2):
                            last = mm(pairs[x][:, u, 0:HW], xg[:, k, :],
                                      up_slot[k][:, x * EW + u * HW:x * EW + (u + 1) * HW],
                                      start=(k == 0), stop=(k == DC - 1))
                    last.then_inc(up_used, 1)
                    if scatter:
                        scatter_chunk(e - 1, k)

            def scatter_chunk(e, m, more_tokens=True):
                if m == 0:
                    pe.wait_ge(y_copied, 2 * e + 2)
                    if more_tokens:
                        pe.wait_ge(xg_copied, 2 * e + 4)
                if m >= 2:
                    pe.wait_ge(x_ready, DC * e + (3 * DC + m - 1))
                mm(banks[m % 2][:, 0:T], yS[:, m * P:(m + 1) * P],
                   selT[:, bass.ds(e, 1), :].rearrange("p a b -> p (a b)"), start=True, stop=True
                   ).then_inc(sc_done, 1)

            def transposes(e):
                pe.wait_ge(hidden_ready, e + 1)
                for f in range(EC):
                    h = hs.rearrange("p a b -> p (a b)")[:, f * P:(f + 1) * P]
                    last = nc.tensor.transpose(banks[f // 4][:, (f % 4) * CAP:(f % 4 + 1) * CAP], h, ident)
                    if f in (3, EC - 1):
                        last.then_inc(tr_done, 1)

            def down(e):
                for f in range(EC):
                    if f % 4 == 0:
                        pe.wait_ge(hT_copied, 2 * e + (f // 4 + 1))
                    pe.wait_ge(down_full[f], 16 * e + 16)
                    for u in range(2):
                        last = mm(pairs[2][:, u, :], hG[:, f, :], down_slot[f][:, u * 512:(u + 1) * 512],
                                  start=(f == 0), stop=(f == EC - 1))
                    last.then_inc(down_used, 1)

            pe.wait_ge(xtr_copied, NRT)
            gather(0)
            pe.wait_ge(sel_loaded, 16)
            pe.wait_ge(gate_copied, 1)
            for e in range(NE):
                if e >= 2:
                    pe.wait_ge(selT_ready, e - 1)
                mm(pairs[2][:, e % 2, 0:T], sel[:, e, :], mT, start=True, stop=True).then_inc(pbc_done, 1)
            up(0)
            pe.wait_ge(selT_ready, NE)
            gather(1)
            pe.wait_ge(xg_copied, 4)
            transposes(0)
            pe.wait_ge(gate_copied, 2)
            down(0)
            with pe.Fori(1, NE - 1) as e:
                up(e, scatter=True)
                pe.wait_ge(x_ready, DC * e + 3 * DC)
                gather(e + 1)
                pe.wait_ge(xg_copied, 2 * e + 4)
                transposes(e)
                pe.wait_ge(gate_copied, e + 2)
                down(e)
            up(NE - 1, scatter=True)
            pe.wait_ge(x_ready, DC * (NE - 1) + 3 * DC)
            transposes(NE - 1)
            down(NE - 1)
            for m in range(DC):
                scatter_chunk(NE - 1, m, more_tokens=False)
            pe.wait_ge(more_ready, 1)
            flag = pe.value_load(more[0:1, 0:1], min_val=0, max_val=1)
            with pe.If(flag):
                pe.wait_ge(x_ready, DC * (NE + 3))
                expert_rows(gover).then_inc(fb_tr, 1)
                pe.wait_ge(fb_gT, 1)
                for e in range(NE):
                    if e >= 2:
                        pe.wait_ge(fb_copied, e - 1)
                    mm(pairs[1][:, e % 2, 0:T], sel[:, e, :], gT, start=True, stop=True).then_inc(fb_gbc, 1)
                with pe.Fori(0, NE) as e:
                    pe.wait_ge(fb_full, 16 * (DC + EC) * e + 16 * (DC + EC))
                    for i in range(EC):
                        pe.wait_ge(fb_gated, EC * e + (i + 1))
                        for x in range(2):
                            for k in range(DC):
                                c = x * EW + i * P
                                last = mm(pairs[0][:, x, 0:T], up_slot[k][:, c:c + P], xn[:, k, :],
                                          start=(k == 0), stop=(k == DC - 1))
                        last.then_inc(fb_up, 1)
                    for m in range(DC):
                        if m == 0:
                            pe.wait_ge(fb_gated, EC * e + (EC + 1))
                        pe.wait_ge(fb_x, DC * e + (m + 1))
                        for f in range(EC):
                            last = mm(banks[m % 2][:, 0:T], down_slot[f][:, m * P:(m + 1) * P], hM[:, f, :],
                                      start=(f == 0), stop=(f == EC - 1))
                        last.then_inc(fb_down, 1)
            sum_squares(4)


def kernel(**inputs):
    import numpy as np
    import concourse.bacc as bacc
    from concourse import mybir as mb
    from concourse.bass_utils import run_bass_kernel_spmd as run

    a = {k: np.asarray(v) for k, v in inputs.items()}
    f = np.float32

    def features(x):
        return x.reshape(x.shape[0], -1, P).transpose(2, 1, 0)

    def tiles(w):
        K, M = w.shape
        return w.reshape(K // P, P, M // P, P).transpose(2, 0, 1, 3)

    def units(t, n):
        t = t.reshape(-1, n, P, P)
        return t.transpose(0, 2, 1, 3).reshape(t.shape[0], P, n * P)

    x = np.concatenate([a["meta_tokens"], a["x_prompt"][0], a["x_sample"][:, 0]], axis=0)
    ins = {"xT": features(x)}
    vec = np.concatenate([a["norm_mix_e"][0], a["norm_ffn_e"][0], a["norm_mix_o"][0], a["norm_ffn_o"][0],
                          a["norm_final"], a["pool_scale"][0], a["s5_d"][0], a["b_glu"][0], a["b_gk"][0],
                          a["gla_norm"][0]])
    ins["vecs"] = vec.reshape(-1, P).T
    cst = np.zeros((P, NCST), f)
    cst[:, C_ID:C_ID + P] = np.eye(P)
    cst[:, C_ONE:C_ONE + P] = 1
    cst[:CH, C_MASK:C_MASK + CH] = np.triu(np.ones((CH, CH)))
    cst[:, C_IOTA:C_IOTA + P] = np.arange(P)
    cst[:, C_SLOT] = np.arange(P)
    cst[:, C_OWN:C_OWN + NRT] = 1
    cst[:NRT * RT - T, C_OWN + NRT - 1] = 0
    for g in range(NG):
        cst[:, C_CNT + 16 * g:C_CNT + 16 * g + 16] = 1.0 / np.minimum(np.arange(16) + 1, 2 << g)
    cst[:, C_RESET:C_RESET + NPROMPT] = np.arange(NPROMPT) % CH != 0
    cst[:, C_EPS] = EPS
    ins["cst"] = cst
    sel = np.zeros((NE, NE, P), f)
    sel[np.arange(NE), np.arange(NE)] = 1
    ins["sel"] = sel

    def states(s):
        s = s.reshape(s.shape[:-2] + (ST, P))
        return np.moveaxis(np.moveaxis(s, -1, 0), -1, 1)

    G = 2 * ST
    logdt = np.broadcast_to(a["s5_log_dt"][0][:, None], (G, 64))
    ins["s5p"] = np.stack([states(a["s5_a_re"][0]), states(a["s5_a_im"][0]), states(logdt)], 1)
    ins["h0"] = np.stack([states(a["state_s5_re"][0]), states(a["state_s5_im"][0])], 1)
    bb = np.zeros((4, 2, 16, 4, 2, 2, 64), f)
    cc = np.zeros((2, 64, 2, ST, 2, 16), f)
    for x_, (bn, cn) in enumerate((("s5_b_re", "s5_c_re"), ("s5_b_im", "s5_c_im"))):
        bt = a[bn][0].reshape(4, 4, 2, 64, 16)
        ct = a[cn][0].reshape(ST, 2, 16, 64)
        for g in range(2):
            bb[:, g, :, :, x_, g, :] = bt[:, :, g].transpose(1, 3, 0, 2)
            cc[g, :, x_, :, g, :] = ct[:, g].transpose(2, 0, 1)
    ins["bblk"] = bb.reshape(P, 4, 2, P)
    ins["cblk"] = cc.reshape(P, 2, ST, 32)
    ins["past"] = a["state_pool"][0].reshape(NSAMP, PAST, NG, P).transpose(3, 2, 0, 1)
    ins["wpool"] = a["w_pool"][0].transpose(1, 0, 2)
    win = tiles(a["w_in_e"][0])
    up = np.stack([tiles(a["ffn_w1"][0]), tiles(a["ffn_w3"][0])], 1)
    ins["main"] = np.concatenate([units(t, UT) for t in (
        np.concatenate([win[4:], win[:4]]), tiles(a["w_glu"][0]), tiles(a["w_out_e"][0]), up,
        tiles(a["ffn_w2"][0]), tiles(a["w_in_o"][0]), tiles(a["w_out_o"][0]))])
    ins["up"] = np.concatenate([a["moe_w1"][0], a["moe_w3"][0]], axis=2).reshape(NE * DC, P, 2 * EW)
    ins["down"] = a["moe_w2"][0].reshape(NE * EC, P, D)
    ins["gk1"] = a["w_gk1"][0].reshape(DC, P, 16).transpose(1, 0, 2)
    ins["gk2"] = a["w_gk2"][0]
    ins["router"] = a["w_router"][0].reshape(DC, P, NE).transpose(1, 0, 2)
    ins["sgla"] = a["state_gla"][0].transpose(2, 0, 1, 3)
    outs = [("yT", (P, DC, T)), ("poolp", (P, NG, PAST)), ("pools", (P, NG, NSAMP, PAST)),
            ("s5prompt", (P, 2, ST)), ("s5samp", (P, 2, ST, NSAMP)), ("glap", (P, H, DV)),
            ("glas", (P, NSAMP, H, DV))]
    nc = bacc.Bacc("TRN2", target_bir_lowering=False, num_devices=1)
    arrays, args = {}, []
    for name, v in ins.items():
        v = np.ascontiguousarray(v)
        arrays["in_" + name] = v
        args.append(nc.dram_tensor("in_" + name, v.shape, mb.dt.from_np(v.dtype), kind="ExternalInput").ap())
    for name, shape in outs:
        args.append(nc.dram_tensor("out_" + name, shape, mb.dt.float32, kind="ExternalOutput").ap())
    build(nc, *args)
    r = run(nc, [arrays], core_ids=[0]).results[0]
    o = {name: np.asarray(r["out_" + name]) for name, _ in outs}

    y = o["yT"].transpose(2, 1, 0).reshape(T, D)
    poolp = o["poolp"].transpose(2, 1, 0).reshape(1, 1, PAST, NG * P)
    pools = o["pools"].transpose(2, 3, 1, 0).reshape(1, NSAMP, PAST, NG * P)
    s5p = o["s5prompt"].transpose(1, 2, 0).reshape(2, 1, 1, G, 64)
    s5s = o["s5samp"].transpose(1, 3, 2, 0).reshape(2, 1, NSAMP, G, 64)
    glap = o["glap"].transpose(1, 0, 2)[None, None]
    glas = o["glas"].transpose(1, 2, 0, 3)[None]
    res = (y[None, 16:NPROMPT], y[NPROMPT:, None], poolp, pools, s5p[0], s5s[0], s5p[1], s5s[1], glap, glas)
    return tuple(np.ascontiguousarray(v) for v in res)
```
